# Optimizing a Trainium2 kernel written in Bass

```python
import math
import jax, jax.numpy as jnp
from jax import lax
import numpy as np

D_MODEL = 1024
BATCH = 1
SEQ = 1024
DEPTH = 1
DEC_BATCH = 8
DEC_SEQ = 16
PAST_LEN = 1024

CHUNK = 64
GMLP_CHUNK = 128
GMLP_WIDTH = D_MODEL // 2
GMLP_HEADS = 4
GMLP_HEAD_DIM = GMLP_WIDTH // GMLP_HEADS
SSM_WIDTH = D_MODEL - GMLP_WIDTH
SSM_GROUP = 16
SSM_GROUPS = SSM_WIDTH // SSM_GROUP
SSM_STATE = 64
MIX_WIDTH = GMLP_WIDTH + SSM_WIDTH
IN_WIDTH = 2 * GMLP_WIDTH + SSM_WIDTH
N_EXPERTS = 16
N_EXPERT_GROUPS = 4
EXPERTS_PER_GROUP = N_EXPERTS // N_EXPERT_GROUPS
TOP_K = 2
D_EXPERT = D_MODEL // 2
EPS = 1e-6
DT_MIN = 1e-3
DT_MAX = 1e-1

kernel_name = 'hybrid_gmlp_s5_moe_stream_step'

F32 = jnp.float32

def rmsnorm(x, g):
    xf = x.astype(F32)
    y = xf * lax.rsqrt(jnp.mean(xf * xf, axis=-1, keepdims=True) + EPS)
    return (y * g.astype(F32)).astype(x.dtype)

def gmlp_mix(uv, v_gain, w_s, b_s):
    z = jax.nn.gelu(uv.astype(F32))
    u, v = z[..., :GMLP_WIDTH], z[..., GMLP_WIDTH:]
    vc = v - jnp.mean(v, axis=-1, keepdims=True)
    vn = vc * lax.rsqrt(jnp.mean(vc * vc, axis=-1, keepdims=True) + EPS) * v_gain.astype(F32)
    bt, seq_len, _ = vn.shape
    pad = (-seq_len) % GMLP_CHUNK
    n_chunks = (seq_len + pad) // GMLP_CHUNK
    vp = jnp.pad(vn, ((0, 0), (0, pad), (0, 0)))
    vp = vp.reshape(bt, n_chunks, GMLP_CHUNK, GMLP_HEADS, GMLP_HEAD_DIM)
    pos = jnp.arange(GMLP_CHUNK)
    mask = (pos[None, :] // CHUNK) <= (pos[:, None] // CHUNK)
    w = jnp.where(mask[None], w_s.astype(F32), 0.0)
    mixed = jnp.einsum('hij,bcjhd->bcihd', w, vp) + b_s.astype(F32).T[None, None, :, :, None]
    mixed = mixed.reshape(bt, n_chunks * GMLP_CHUNK, GMLP_WIDTH)[:, :seq_len]
    return u * mixed, vn

def s5_combine(e1, e2):
    ar1, ai1, br1, bi1 = e1
    ar2, ai2, br2, bi2 = e2
    ar = ar1 * ar2 - ai1 * ai2
    ai = ar1 * ai2 + ai1 * ar2
    br = ar2 * br1 - ai2 * bi1 + br2
    bi = ar2 * bi1 + ai2 * br1 + bi2
    return (ar, ai, br, bi)

def s5_mix(u, h0_re, h0_im, a_re, a_im, log_dt, b_re, b_im, c_re, c_im, d_skip):
    a_re = a_re.astype(F32)
    a_im = a_im.astype(F32)
    dt = jnp.exp(log_dt.astype(F32))[:, None]
    mag = jnp.exp(a_re * dt)
    ang = a_im * dt
    lb_re = mag * jnp.cos(ang)
    lb_im = mag * jnp.sin(ang)
    num_re = lb_re - 1.0
    num_im = lb_im
    den = a_re * a_re + a_im * a_im
    coef_re = (num_re * a_re + num_im * a_im) / den
    coef_im = (num_im * a_re - num_re * a_im) / den
    b_re = b_re.astype(F32)
    b_im = b_im.astype(F32)
    bb_re = coef_re[..., None] * b_re - coef_im[..., None] * b_im
    bb_im = coef_re[..., None] * b_im + coef_im[..., None] * b_re
    bu_re = jnp.einsum('blgq,gpq->blgp', u, bb_re)
    bu_im = jnp.einsum('blgq,gpq->blgp', u, bb_im)
    elems = (jnp.broadcast_to(lb_re, bu_re.shape), jnp.broadcast_to(lb_im, bu_re.shape), bu_re, bu_im)
    p_re, p_im, h_re, h_im = lax.associative_scan(s5_combine, elems, axis=1)
    if h0_re is not None:
        s_re = h0_re.astype(F32)[:, None]
        s_im = h0_im.astype(F32)[:, None]
        h_re = h_re + p_re * s_re - p_im * s_im
        h_im = h_im + p_re * s_im + p_im * s_re
    y = (jnp.einsum('blgp,gqp->blgq', h_re, c_re.astype(F32))
         - jnp.einsum('blgp,gqp->blgq', h_im, c_im.astype(F32))
         + d_skip.astype(F32) * u)
    return y, h_re[:, -1], h_im[:, -1]

def moe(h, w_router, b_router, w_gate, w_up, w_down):
    logits = h.astype(F32) @ w_router.astype(F32) + b_router.astype(F32)
    scores = jax.nn.softmax(logits, axis=-1)
    n_tok = scores.shape[0]
    grouped = scores.reshape(n_tok, N_EXPERT_GROUPS, EXPERTS_PER_GROUP)
    group_score = jnp.sum(lax.top_k(grouped, TOP_K)[0], axis=-1)
    g_idx = jnp.argmax(group_score, axis=-1)
    in_group = (jnp.arange(N_EXPERTS) // EXPERTS_PER_GROUP)[None, :] == g_idx[:, None]
    vals, idx = lax.top_k(jnp.where(in_group, scores, -jnp.inf), TOP_K)
    weights = vals / jnp.sum(vals, axis=-1, keepdims=True)
    gate = jnp.sum(weights[..., None] * jax.nn.one_hot(idx, N_EXPERTS, dtype=F32), axis=1)
    y = jnp.zeros(h.shape, F32)
    for e in range(N_EXPERTS):
        he = jax.nn.silu(h @ w_gate[e]) * (h @ w_up[e])
        y = y + gate[:, e:e + 1] * (he @ w_down[e]).astype(F32)
    return y.astype(h.dtype)

def layer(x, c, h0_re, h0_im, w_ada, b_ada, g_mix, g_ffn, w_in, v_gain, w_s, b_s,
          a_re, a_im, log_dt, b_re, b_im, c_re, c_im, d_skip, w_glu, b_glu, w_out,
          w_router, b_router, w_gate, w_up, w_down):
    bt, seq_len, _ = x.shape
    mod = (jax.nn.silu(c) @ w_ada + b_ada)[:, None, :]
    shift_m, scale_m, gate_m, shift_f, scale_f, gate_f = jnp.split(mod, 6, axis=-1)
    h = rmsnorm(x, g_mix) * (1 + scale_m) + shift_m
    proj = h @ w_in
    a_out, v_rows = gmlp_mix(proj[..., :2 * GMLP_WIDTH], v_gain, w_s, b_s)
    ub = proj[..., 2 * GMLP_WIDTH:].reshape(bt, seq_len, SSM_GROUPS, SSM_GROUP).astype(F32)
    y_ssm, h_re, h_im = s5_mix(ub, h0_re, h0_im, a_re, a_im, log_dt, b_re, b_im, c_re, c_im, d_skip)
    y_ssm = jax.nn.gelu(y_ssm.reshape(bt, seq_len, SSM_WIDTH))
    b_out = y_ssm * jax.nn.sigmoid(y_ssm @ w_glu.astype(F32) + b_glu.astype(F32))
    mixed = jnp.concatenate([a_out, b_out], axis=-1).astype(x.dtype)
    x = x + gate_m * (mixed @ w_out)
    h2 = rmsnorm(x, g_ffn) * (1 + scale_f) + shift_f
    ffn = moe(h2.reshape(bt * seq_len, D_MODEL), w_router, b_router, w_gate, w_up, w_down)
    x = x + gate_f * ffn.reshape(bt, seq_len, D_MODEL)
    return x, h_re, h_im, v_rows.astype(x.dtype)

def setup_inputs(seed: int = 0) -> dict:
    key = jax.random.key(seed)
    ks = jax.random.split(key, 32)

    def nrm(k, shape, scale):
        return jax.random.normal(k, shape, F32) * scale

    n_idx = jnp.arange(SSM_STATE, dtype=F32)
    ssm_state_shape = (DEPTH, DEC_BATCH, SSM_GROUPS, SSM_STATE)
    return {
        'x_prompt': nrm(ks[0], (BATCH, SEQ, D_MODEL), 1.0),
        'x_sample': nrm(ks[1], (DEC_BATCH, DEC_SEQ, D_MODEL), 1.0),
        'c_prompt': nrm(ks[2], (BATCH, D_MODEL), 1.0),
        'c_sample': nrm(ks[3], (DEC_BATCH, D_MODEL), 1.0),
        'state_s5_re': nrm(ks[4], ssm_state_shape, 0.5),
        'state_s5_im': nrm(ks[5], ssm_state_shape, 0.5),
        'w_ada': nrm(ks[6], (DEPTH, D_MODEL, 6 * D_MODEL), 0.5 * D_MODEL ** -0.5),
        'b_ada': nrm(ks[7], (DEPTH, 6 * D_MODEL), 0.02),
        'g_norm_mix': 1.0 + nrm(ks[8], (DEPTH, D_MODEL), 0.02),
        'g_norm_ffn': 1.0 + nrm(ks[9], (DEPTH, D_MODEL), 0.02),
        'w_in': nrm(ks[10], (DEPTH, D_MODEL, IN_WIDTH), D_MODEL ** -0.5),
        'gmlp_v_gain': 1.0 + nrm(ks[11], (DEPTH, GMLP_WIDTH), 0.02),
        'gmlp_w_spatial': nrm(ks[12], (DEPTH, GMLP_HEADS, GMLP_CHUNK, GMLP_CHUNK), 0.5 * GMLP_CHUNK ** -0.5),
        'gmlp_b_spatial': 1.0 + nrm(ks[13], (DEPTH, GMLP_HEADS, GMLP_CHUNK), 0.1),
        's5_a_re': -0.5 + nrm(ks[14], (DEPTH, SSM_GROUPS, SSM_STATE), 0.01),
        's5_a_im': math.pi * n_idx + nrm(ks[15], (DEPTH, SSM_GROUPS, SSM_STATE), 0.01),
        's5_log_dt': jax.random.uniform(ks[16], (DEPTH, SSM_GROUPS), F32, math.log(DT_MIN), math.log(DT_MAX)),
        's5_b_re': nrm(ks[17], (DEPTH, SSM_GROUPS, SSM_STATE, SSM_GROUP), (2 * SSM_GROUP) ** -0.5),
        's5_b_im': nrm(ks[18], (DEPTH, SSM_GROUPS, SSM_STATE, SSM_GROUP), (2 * SSM_GROUP) ** -0.5),
        's5_c_re': nrm(ks[19], (DEPTH, SSM_GROUPS, SSM_GROUP, SSM_STATE), SSM_STATE ** -0.5),
        's5_c_im': nrm(ks[20], (DEPTH, SSM_GROUPS, SSM_GROUP, SSM_STATE), SSM_STATE ** -0.5),
        's5_d': nrm(ks[21], (DEPTH, SSM_GROUPS, SSM_GROUP), 1.0),
        's5_w_glu': nrm(ks[22], (DEPTH, SSM_WIDTH, SSM_WIDTH), SSM_WIDTH ** -0.5),
        's5_b_glu': nrm(ks[23], (DEPTH, SSM_WIDTH), 0.02),
        'w_out': nrm(ks[24], (DEPTH, MIX_WIDTH, D_MODEL), MIX_WIDTH ** -0.5),
        'w_router': nrm(ks[25], (D_MODEL, N_EXPERTS), D_MODEL ** -0.5),
        'b_router': nrm(ks[26], (N_EXPERTS,), 0.01),
        'w_gate': nrm(ks[27], (DEPTH, N_EXPERTS, D_MODEL, D_EXPERT), D_MODEL ** -0.5),
        'w_up': nrm(ks[28], (DEPTH, N_EXPERTS, D_MODEL, D_EXPERT), D_MODEL ** -0.5),
        'w_down': nrm(ks[29], (DEPTH, N_EXPERTS, D_EXPERT, D_MODEL), D_EXPERT ** -0.5),
        'g_final': 1.0 + nrm(ks[30], (D_MODEL,), 0.02),
    }

def reference(x_prompt, x_sample, c_prompt, c_sample, state_s5_re, state_s5_im,
              w_ada, b_ada, g_norm_mix, g_norm_ffn, w_in, gmlp_v_gain, gmlp_w_spatial, gmlp_b_spatial,
              s5_a_re, s5_a_im, s5_log_dt, s5_b_re, s5_b_im, s5_c_re, s5_c_im, s5_d, s5_w_glu, s5_b_glu,
              w_out, w_router, b_router, w_gate, w_up, w_down, g_final):
    xp = x_prompt
    xs = x_sample
    sp_re, sp_im, ss_re, ss_im, v_new = [], [], [], [], []
    for l in range(DEPTH):
        p = (w_ada[l], b_ada[l], g_norm_mix[l], g_norm_ffn[l], w_in[l], gmlp_v_gain[l],
             gmlp_w_spatial[l], gmlp_b_spatial[l], s5_a_re[l], s5_a_im[l], s5_log_dt[l],
             s5_b_re[l], s5_b_im[l], s5_c_re[l], s5_c_im[l], s5_d[l], s5_w_glu[l], s5_b_glu[l],
             w_out[l], w_router, b_router, w_gate[l], w_up[l], w_down[l])
        xp, hp_re, hp_im, _ = layer(xp, c_prompt, None, None, *p)
        xs, hs_re, hs_im, vs = layer(xs, c_sample, state_s5_re[l], state_s5_im[l], *p)
        sp_re.append(hp_re)
        sp_im.append(hp_im)
        ss_re.append(hs_re)
        ss_im.append(hs_im)
        v_new.append(vs)
    y_prompt = rmsnorm(xp, g_final)
    y_sample = rmsnorm(xs, g_final)
    return (y_prompt, y_sample, jnp.stack(sp_re), jnp.stack(sp_im), jnp.stack(ss_re), jnp.stack(ss_im), jnp.stack(v_new))


_drawn_inputs = setup_inputs


def setup_inputs(seed=0):
    import zlib

    import numpy as np

    out = dict(_drawn_inputs(seed))
    spreads = {}
    factors = {'g_norm_mix': 2.684,
     'gmlp_v_gain': 21.09,
     's5_a_re': 45.316,
     's5_b_glu': 21.823,
     'b_router': 4.608,
     'g_final': 21.096,
     'g_norm_ffn': 2.985}
    for name, (base, spread) in spreads.items():
        noise = np.random.default_rng([zlib.crc32(name.encode()), seed]).standard_normal(out[name].shape)
        drawn = base * np.exp(spread * noise) if base else spread * noise
        out[name] = __import__('jax').numpy.asarray(drawn.astype(out[name].dtype))
    for name, factor in factors.items():
        out[name] = (out[name] * factor).astype(out[name].dtype)
    return out
```

```python
import math
from contextlib import ExitStack

import concourse.bass as bass
from concourse import mybir

ALU = mybir.AluOpType
ACT = mybir.ActivationFunctionType
AX = mybir.AxisListType
F32 = mybir.dt.float32
I32 = mybir.dt.int32
BF16 = mybir.dt.bfloat16

P = 128
D = 1024
KD = D // P
SEQ, DB, DS = 1024, 8, 16
NT = (SEQ + DB * DS) // P
TP = SEQ // P
TOK = NT * P
NC = 1 + DB
GW = D // 2
GH = 4
KG = GW // P
SG, SQ, SS = 32, 16, 64
PR = SG // 2
L = 8
CH = TOK // L
CP = SEQ // L
SB = 2
NE, NG, EG = 16, 4, 4
DE = D // 2
KE = DE // P
BN = 192
HB = BN // 2
CAP = TOK
ROUNDS = CAP // BN
EXTRA = 2 * TOK // (BN + 1)
MAXB = NE + EXTRA
LROWS = (MAXB + 1) * BN
EPS = 1e-6
PI = math.pi
TWO_PI_HI = 6.28125
TWO_PI_MID = 0.0019340515136718750
TWO_PI_LO = 2 * math.pi - TWO_PI_HI - TWO_PI_MID
assert CAP % BN == 0 and L * SQ == P


def hybrid_step(nc, x_prompt, x_sample, c_prompt, c_sample, state_re, state_im, w_ada, b_ada, g_mix, g_ffn,
                w_in, v_gain, w_sp, b_sp, a_re, a_im, log_dt, b_re, b_im, c_re, c_im, d_skip, w_glu, b_glu,
                w_out, w_router, b_router, w_gate, w_up, w_down, g_final,
                y_prompt, y_sample, sp_re, sp_im, ss_re, ss_im, v_new):
    ctx = ExitStack()
    with ctx:
        def sb(name, shape, dt=F32):
            return ctx.enter_context(nc.sbuf_tensor(name, shape, dt))

        def sem(name):
            return ctx.enter_context(nc.semaphore(name))

        ctx.enter_context(nc.allow_non_contiguous_dma(reason="small parameter tables"))

        ub_d = nc.dram_tensor("ub_scratch", (GW, L, CH), F32).ap()
        y_d = nc.dram_tensor("y_scratch", (GW, L, CH), F32).ap()
        h2_d = nc.dram_tensor("h2_scratch", (TOK, D), F32).ap()
        list_d = nc.dram_tensor("list_scratch", (LROWS, 1), I32).ap()
        ys_d = nc.dram_tensor("expert_rows", (MAXB * BN, D), F32).ap()

        sizes = dict(RA=9216, RB=4608, RC=4608, RD=2304, RE=4608, RF=4608, RG=4096, RT=2560, RW=12288)
        arena = sb("arena", [P, sum(sizes.values())])
        off = {}
        at = 0
        for name, n in sizes.items():
            off[name] = at
            at += n

        def area(region, start, *shape, parts=P):
            n = math.prod(shape)
            a = off[region] + start
            flat = arena[0:parts, a:a + n]
            if len(shape) == 1:
                return flat
            names = ["i", "j", "k", "l"][:len(shape)]
            return flat.rearrange("p (" + " ".join(names) + ") -> p " + " ".join(names),
                                  **dict(zip(names[1:], shape[1:])))

        ring = area("RW", 0, 3, KD, 512)
        hT = area("RA", 0, KD, TOK)
        H = area("RA", 0, 2, PR, CH)
        Y = area("RA", 4608, SG, CH)
        dtmp = area("RC", 0, SG, SQ)
        uT = area("RB", 0, KG, TOK)
        vn = area("RC", 0, NT, GW)
        bT = area("RC", 0, KG, TOK)
        ubT = area("RD", 0, 2, L, CH)
        U = area("RE", 0, SG, CH)
        yT = area("RE", 0, KG, L * CH)
        W = area("RF", 0, 2, PR, L + 1, SQ)
        X1 = area("RE", 0, NT, D)
        MT = area("RG", 0, SG, P)
        xin = area("RT", 0, 2, D)
        rows = area("RB", 0, 2, P)
        arow = area("RB", 256, 2, P)
        srow = area("RB", 512, 2, P)
        crow = area("RB", 768, 4, P)
        wsrow = area("RB", 1280, GH, P)
        junk_x = area("RB", 2304, 512).bitcast(BF16)
        junk_h = area("RA", 5120, 512).bitcast(BF16)
        zi = area("RB", 2816, LROWS // P).bitcast(I32)
        zf = area("RD", 1536, 512)
        vgain = area("RD", 1536, GW)
        bsp = area("RD", 512, GH, P)
        smp = area("RT", 1024, 6, PR, DB)
        cc = area("RT", 2048, 2, PR, SQ)
        arows = area("RD", 1024, 512, parts=NC)
        EH = area("RT", 512, 2, PR, SS)
        wS = area("RT", 0, GH, P)
        bnat = area("RB", 1792, 2, PR, SQ)
        wtmp = area("RC", 0, 2, PR, L + 1, SQ)[:, 0]
        wtmp2 = area("RC", 2304, PR, L + 1, SQ)
        KT = area("RE", 0, SG, P, parts=SQ)
        gnat = area("RT", 0, 2, SB, L, SQ)
        gt = area("RT", 512, 2, SB, P)
        tm = area("RT", 1024, 6, SB, P)
        bc = area("RG", 0, 6, D)
        gfb = area("RD", 0, 2, D)
        h2r = area("RA", 0, 2, D)
        h2T = area("RA", 2048, 2, KD, P)
        wtm = area("RA", 4096, 2, 512)
        ytm = area("RD", 0, 2, 288)
        gtm = area("RD", 0, 2, SB, L * SQ).rearrange("p i s (l q) -> p i s l q", l=L)
        mtm = area("RD", 1024, GH, P)
        fsr = area("RD", 1536, 4, P)
        wg = area("RW", 0, KD, DE)
        wu = area("RW", 4096, KD, DE)
        wd = area("RW", 8192, KE, D)
        XR = area("RB", 0, 2, D, parts=HB)
        OUT = area("RB", 2048, 2, D, parts=HB)
        xT = area("RA", 0, KD, BN)
        heT = area("RA", 1536, KE, BN)
        sil = area("RA", 2304, 2, BN)
        YA = area("RW", 0, 2, 2, D)
        fin = area("RW", 4096, 2, D)
        gfin = area("RG", 0, D)
        rt = area("RC", 0, 16, NT * NE)

        ident = sb("ident", [P, P])
        tri = sb("tri", [P, P], BF16)
        ones = sb("ones", [P, P], BF16)
        modT = sb("modT", [P, 48, NC])
        Am = sb("Am", [P, KD, NC])
        Af = sb("Af", [P, KD, NC])
        vecT = sb("vecT", [P, 68])
        cT = sb("cT", [P, NC, KD])
        wT = sb("wT", [P, GH, P])
        LP = sb("LP", [P, 2, PR, L + 1])
        LR = sb("LR", [P, 2, PR, L])
        aT = sb("aT", [P, 2, PR])
        h0 = sb("h0", [P, 2, DB, PR])
        q = sb("q", [P, 24, PR])
        qi = sb("qi", [P, PR], I32)
        bb = sb("bb", [P, 2, PR, SQ])
        dq = sb("dq", [SQ, SG])
        fs = sb("fs", [P, 2, NC, PR])
        st = sb("st", [P, 6, NT])
        bn6 = sb("bn6", [P, 2, 6])
        wr = sb("wr", [P, KD, NE])
        brt = sb("brt", [P, NE])
        mv = sb("mv", [P, NT, 2])
        small = area("RC", 2304, 20, NT)
        ohb = sb("ohb", [P, NT, NE], BF16)
        ebase = sb("ebase", [P, NE])
        iot = sb("iot", [1, EXTRA])
        etab = sb("etab", [1, NE])
        lst = sb("lst", [P, 2, NT], I32)
        tokid = sb("tokid", [P, NT], I32)
        gates = sb("gates", [P, 2, NT])
        tab = sb("tab", [1, 32], I32)
        nblk = sb("nblk", [1, 1], I32)
        idx = sb("idx", [HB, 2], I32)
        eps = sb("eps", [P, 1])
        b64 = area("RC", 2560, 32, parts=1)

        B = [ctx.enter_context(nc.psum_tensor(f"bank{i}", [P, 512], F32)) for i in range(8)]

        names = ("ys_zero idx_seen wide_in ws_zero ld_gain ld_vec ld_s5 ld_c ld_mlp ld_x0 ld_x1 ld_w0 ld_w1 ld_w2 ld_xres ld_gates "
                 "consts zeroed cols_t cond_t s5_t ws_t cond_done cT_done w_table kt_ps kt_sb kt_done mt_placed "
                 "ada_rows ada_ps ada_sb am_done sq_done x_rs x_norm x_used xt_ps ht_sb_v ht_sb_s ring_used ub_ps ub_sb ub_out0 ub_out1 u_in "
                 "v_ps v_gelu v_done v_out uu_ps u_sb e_done g_nat g_ps g_sb v5_ps v5_used h_done ws_done "
                 "mix_ps mix_sb y_ps y_sb y_out y_in glu_ps sig_sb b_done bc_ps bc_sb wo_ps wo_used x1_done ss_done rs_done "
                 "h2_rows h2_out0 h2_out1 h2t_ps h2t_sb lg_ps exp_done e_in oh_done pre_ps pos_done list_zero scat tab_done "
                 "idx_in rows_in xt2_ps xt2_sb gate_ps up_ps silu_done he_done gu_free wd_free ld_gu ld_wd down_ps out_sb out_d rows_free "
                 "comb_in0 comb_in1 comb_used fin_ss fin_rs fin_done y_done0 y_done1 fs_t fs_sb fs_out chain_v chain_s chain_g chain_p smp wdiag "
                 "x_scale e_out dt_in mg_in ang_in cs_in stats_v std_v ldq mod_all").split()
        S = {n: sem(n) for n in names}

        block = ctx.enter_context(nc.Block())

        def chained(eng, s):
            count = [0]

            def link(ins):
                count[0] += 1
                ins.then_inc(s, 1)
                eng.wait_ge(s, count[0])
            return link

        def cols(w, c):
            return w.rearrange("(k p) n -> p k n", p=P)[:, :, c * 512:(c + 1) * 512]
        ORDER = [("ada", c) for c in range(4)] + [("in", 2), ("in", 1), ("in", 0)] \
            + [("ada", c) for c in range(4, 12)] + [("glu", 0), ("out", 0), ("out", 1)]
        WSRC = {"ada": w_ada[0], "in": w_in[0], "glu": w_glu[0], "out": w_out[0]}
        place = {item: n for n, item in enumerate(ORDER)}
        LDW = [S["ld_w0"], S["ld_w1"], S["ld_w2"]]

        def arrived(eng, item):
            n = place[item]
            eng.wait_ge(LDW[n % 3], 16 * (n // 3 + 1))
            return ring[:, n % 3]

        x_rows = x_prompt[0].rearrange("(t p) d -> t p d", p=P)
        xs_rows = x_sample.rearrange("b s d -> (b s) d")

        def x_tile(t):
            return x_rows[t] if t < TP else xs_rows

        def c_rows(eng, r, c_in):
            for h in range(2):
                for gg in range(8):
                    src = c_in[0, 16 * h + 2 * gg:16 * h + 2 * gg + 2].rearrange("a q p -> q a p")
                    eng.dma_start(crow[16 * gg:16 * gg + 16, 2 * r + h].rearrange("q (a p) -> q a p", a=2), src).then_inc(S["ld_c"], 16)

        @block.sync
        def _(sp):
            sp.dma_start(rows[0:8, 0], c_prompt.rearrange("a (k p) -> (a k) p", p=P)).then_inc(S["ld_vec"], 16)
            sp.dma_start(rows[8:72, 0], c_sample.rearrange("a (k p) -> (a k) p", p=P)).then_inc(S["ld_vec"], 16)
            sp.dma_start(rows[0:48, 1], b_ada.rearrange("a (k p) -> (a k) p", p=P)).then_inc(S["ld_vec"], 16)
            sp.dma_start(rows[48:56, 1], g_mix.rearrange("a (k p) -> (a k) p", p=P)).then_inc(S["ld_vec"], 16)
            sp.dma_start(rows[56:64, 1], g_ffn.rearrange("a (k p) -> (a k) p", p=P)).then_inc(S["ld_vec"], 16)
            sp.dma_start(rows[64:68, 1], b_glu.rearrange("a (k p) -> (a k) p", p=P)).then_inc(S["ld_vec"], 16)
            c_rows(sp, 1, c_im)
            for n in range(3):
                kind, c = ORDER[n]
                sp.dma_start(ring[:, n], cols(WSRC[kind], c)).then_inc(LDW[n], 16)
            for n in range(3, len(ORDER)):
                kind, c = ORDER[n]
                sp.wait_ge(S["ring_used"], n - 2)
                dst = ring[:, n % 3, 0:4] if kind == "glu" else ring[:, n % 3]
                sp.dma_start(dst, cols(WSRC[kind], c)).then_inc(LDW[n % 3], 16)
            for i in range(1):
                sp.wait_ge(S["ring_used"], len(ORDER))
                sp.dma_start(wg, w_gate[0, 0].rearrange("(k p) n -> p k n", p=P)).then_inc(S["ld_gu"], 16)
                sp.dma_start(wu, w_up[0, 0].rearrange("(k p) n -> p k n", p=P)).then_inc(S["ld_gu"], 16)
                sp.dma_start(wd, w_down[0, 0].rearrange("(k p) n -> p k n", p=P)).then_inc(S["ld_wd"], 16)
            sp.wait_ge(S["tab_done"], 1)
            n_blocks = sp.value_load(nblk[0:1, 0:1], min_val=NE, max_val=NE + EXTRA)
            with sp.Fori(1, n_blocks) as i:
                e = sp.value_load(tab[0:1, bass.ds(i, 1)], min_val=0, max_val=NE - 1)
                sp.wait_ge(S["gu_free"], i)
                sp.dma_start(wg, w_gate[0, bass.ds(e, 1)].rearrange("a (k p) n -> p (a k) n", p=P)).then_inc(S["ld_gu"], 16)
                sp.dma_start(wu, w_up[0, bass.ds(e, 1)].rearrange("a (k p) n -> p (a k) n", p=P)).then_inc(S["ld_gu"], 16)
                sp.wait_ge(S["wd_free"], i)
                sp.dma_start(wd, w_down[0, bass.ds(e, 1)].rearrange("a (k p) n -> p (a k) n", p=P)).then_inc(S["ld_wd"], 16)
            for t in range(NT):
                sp.wait_ge(S["fin_done"], t + 1)
                dst = y_prompt[0].rearrange("(t p) d -> t p d", p=P)[t] if t < TP else y_sample.rearrange("b s d -> (b s) d")
                sp.dma_start(dst, fin[:, t % 2]).then_inc(S[f"y_done{t % 2}"], 16)
            sp.wait_ge(S["y_done0"], 16 * 5)
            sp.wait_ge(S["y_done1"], 16 * 4)
            sp.wait_ge(S["fs_out"], 64)
            sp.wait_ge(S["v_out"], 16)

        @block.gpsimd
        def _(gp):
            g = nc.gpsimd
            lk = chained(gp, S["chain_g"])
            lk(g.memset(ident[:, :], 0.0))
            lk(g.affine_select(out=ident[:, :], in_=ident[:, :], compare_op=ALU.not_equal, fill=1.0, base=0,
                               pattern=[[-1, P]], channel_multiplier=1))
            g.memset(eps[:, :], EPS).then_inc(S["consts"], 1)
            g.memset(ones[:, :], 1.0).then_inc(S["consts"], 1)
            lk(g.memset(tri[:, :], 1.0))
            g.affine_select(out=tri[:, :], in_=tri[:, :], compare_op=ALU.is_gt, fill=0.0, base=0,
                            pattern=[[1, P]], channel_multiplier=-1).then_inc(S["consts"], 1)
            gp.dma_start(arow[0:PR, 0], a_re[0].rearrange("(g a) p -> g (a p)", a=2)).then_inc(S["ld_s5"], 16)
            gp.dma_start(arow[0:PR, 1], a_im[0].rearrange("(g a) p -> g (a p)", a=2)).then_inc(S["ld_s5"], 16)
            for r, (s_in, b_in) in enumerate(((state_re, b_re), (state_im, b_im))):
                gp.dma_start(srow[:, r], s_in[0].rearrange("b (g a) p -> (b g) (a p)", a=2)).then_inc(S["ld_s5"], 16)
                gp.dma_start(bnat[:, r], b_in[0].rearrange("(g a) p q -> (a p) g q", a=2)).then_inc(S["ld_s5"], 16)
            for a in range(2):
                gp.dma_start(q[SS * a:SS * a + SS, 0], log_dt[0].rearrange("(g a) -> a g", a=2)[a].partition_broadcast(SS)).then_inc(S["ld_s5"], 16)
            gp.dma_start(dq[:, :], d_skip[0].rearrange("g q -> q g")).then_inc(S["ldq"], 16)
            g.memset(MT, 0.0).then_inc(S["zeroed"], 1)
            lk(g.memset(zi, 0))
            g.iota(tokid[:, :], pattern=[[P, NT]], base=0, channel_multiplier=1).then_inc(S["zeroed"], 1)
            lk(g.memset(zf, 0.0))
            gp.dma_start(ys_d[NE * BN:MAXB * BN].rearrange("(p a) (b n) -> p (a b) n", p=64, n=512),
                         zf[0:64].unsqueeze(1).to_broadcast([64, EXTRA * BN // 64 * 2, 512])).then_inc(S["ys_zero"], 16)
            g.iota(ebase[:, :], pattern=[[BN, NE]], base=0, channel_multiplier=0, allow_small_or_imprecise_dtypes=True).then_inc(S["zeroed"], 1)
            g.iota(iot[:, :], pattern=[[1, EXTRA]], base=0, channel_multiplier=0, allow_small_or_imprecise_dtypes=True).then_inc(S["zeroed"], 1)
            g.iota(etab[:, :], pattern=[[1, NE]], base=0, channel_multiplier=0, allow_small_or_imprecise_dtypes=True).then_inc(S["zeroed"], 1)
            gp.dma_start(list_d.rearrange("(p n) a -> p (n a)", p=P), zi).then_inc(S["list_zero"], 16)
            gp.wait_ge(S["w_table"], 1)
            for s in range(PR // SB):
                sl = slice(SB * s, SB * s + SB)
                if s == 0:
                    gp.wait_ge(S["xt_ps"], NT)
                    gp.wait_ge(S["e_done"], 1)
                    gp.wait_ge(S["ub_out0"], 16 * KG // 2)
                    gp.wait_ge(S["ub_out1"], 16 * KG // 2)
                else:
                    gp.wait_ge(S["g_ps"], s)
                for r in range(2):
                    lam0 = LR[:, 0, sl].unsqueeze(3).to_broadcast([P, SB, L, SQ])
                    lam1 = LR[:, 1, sl].unsqueeze(3).to_broadcast([P, SB, L, SQ])
                    b0 = bb[:, r, sl].unsqueeze(2).to_broadcast([P, SB, L, SQ])
                    b1 = bb[:, 1 - r, sl].unsqueeze(2).to_broadcast([P, SB, L, SQ])
                    t0, t1 = gtm[:, 0], gtm[:, 1]
                    lk(g.tensor_tensor(t0, lam0, b0, ALU.mult))
                    lk(g.tensor_tensor(t1, lam1, b1, ALU.mult))
                    last = g.tensor_tensor(gnat[:, r], t0, t1, ALU.subtract if r == 0 else ALU.add)
                    if r == 0:
                        lk(last)
                    else:
                        last.then_inc(S["g_nat"], 1)
                        gp.wait_ge(S["g_nat"], s + 1)
            gp.wait_ge(S["g_ps"], PR // SB)
            g.memset(wS, 0.0).then_inc(S["ws_zero"], 1)
            gp.wait_ge(S["list_zero"], 16)
            gp.wait_ge(S["pos_done"], 1)
            for t in range(NT):
                for k in range(2):
                    gp.indirect_dma_start(out=list_d, out_offset=bass.IndirectOffsetOnAxis(ap=lst[:, k, t:t + 1], axis=0),
                                          in_=tokid[:, t:t + 1], in_offset=None).then_inc(S["scat"], 16)
            gp.wait_ge(S["scat"], 16 * 2 * NT)
            gp.wait_ge(S["h2_out0"], 16 * 5)
            gp.wait_ge(S["h2_out1"], 16 * 4)
            gp.wait_ge(S["tab_done"], 1)
            n_blocks = gp.value_load(nblk[0:1, 0:1], min_val=NE, max_val=NE + EXTRA)
            gp.sem_inc(S["rows_free"], 1)
            with gp.Fori(0, n_blocks + 1) as i:
                gp.wait_ge(S["rows_free"], i + 1)
                gp.dma_start(idx[:, :], list_d[bass.ds(i * BN, BN)].rearrange("(h p) a -> p (h a)", p=HB)).then_inc(S["idx_in"], 16)
                gp.wait_ge(S["idx_in"], 16 * i + 16)
                gp.sem_inc(S["idx_seen"], 1)
                for h in range(2):
                    gp.indirect_dma_start(out=XR[:, h], out_offset=None, in_=h2_d,
                                          in_offset=bass.IndirectOffsetOnAxis(ap=idx[:, h:h + 1], axis=0)).then_inc(S["rows_in"], 16)
                gp.wait_ge(S["rows_in"], 32 * i + 32)
            gp.wait_ge(S["out_d"], 32 * n_blocks + 16)
            gp.sem_inc(S["idx_seen"], 1)
            gp.wait_ge(S["wd_free"], n_blocks)
            gp.sem_inc(S["idx_seen"], 1)
            for t in range(NT):
                if t >= 2:
                    gp.wait_ge(S["comb_used"], t - 1)
                for k in range(2):
                    gp.indirect_dma_start(out=YA[:, t % 2, k], out_offset=None, in_=ys_d,
                                          in_offset=bass.IndirectOffsetOnAxis(ap=lst[:, k, t:t + 1], axis=0)).then_inc(S[f"comb_in{t % 2}"], 16)


        @block.scalar
        def _(act):
            a = nc.scalar
            lk = chained(act, S["chain_s"])
            act.dma_start(wsrow, w_sp[0].rearrange("h i j -> i h j")).then_inc(S["ld_mlp"], 16)
            act.dma_start(wr[:, :, :], w_router.rearrange("(k p) n -> p k n", p=P)).then_inc(S["ld_mlp"], 16)
            act.dma_start(brt[:, :], b_router.partition_broadcast(P)).then_inc(S["ld_mlp"], 16)
            c_rows(act, 0, c_re)
            for t in range(2):
                act.dma_start(xin[:, t], x_tile(t)).then_inc(S[f"ld_x{t}"], 16)

            def modulation_rows(c):
                act.wait_ge(S["ring_used"], place["ada", c] + 1)
                if c:
                    act.wait_ge(S["ada_ps"], c)
                a.copy(arows, B[c % 2][0:NC, :]).then_inc(S["ada_rows"], 1)
            act.wait_ge(S["cols_t"], 1)
            a.activation(cT[:, :, :], B[0][:, 128:200].rearrange("p (j k) -> p j k", k=KD), ACT.Silu).then_inc(S["cond_done"], 1)
            a.copy(vecT[:, :], B[0][:, 0:68]).then_inc(S["cond_done"], 1)
            act.wait_ge(S["ws_t"], 1)
            a.copy(wT[:, :, :], B[3][:, :].rearrange("p (h i) -> p h i", h=GH)).then_inc(S["ws_done"], 1)
            act.wait_ge(S["s5_t"], 1)
            a.copy(aT[:, :, :], B[1][:, 0:32].rearrange("p (r g) -> p r g", r=2)).then_inc(S["cond_t"], 1)
            a.copy(h0[:, :, :, :], B[1][:, 128:384].rearrange("p (r b g) -> p r b g", r=2, b=DB)).then_inc(S["cond_t"], 1)
            a.copy(cc, B[2][:, :].rearrange("p (r g q) -> p r g q", r=2, g=PR)).then_inc(S["cond_t"], 1)
            act.wait_ge(S["ld_s5"], 16 * 8)
            a.activation(q[:, 1], q[:, 0], ACT.Exp).then_inc(S["dt_in"], 1)
            modulation_rows(0)
            act.wait_ge(S["mg_in"], 1)
            a.activation(q[:, 4], q[:, 2], ACT.Exp).then_inc(S["dt_in"], 1)
            a.activation(q[:, 5], q[:, 2], ACT.Exp, scale=float(L)).then_inc(S["dt_in"], 1)
            act.wait_ge(S["ang_in"], 1)
            a.activation(q[:, 8], q[:, 6], ACT.Sin).then_inc(S["cs_in"], 1)
            a.activation(q[:, 9], q[:, 7], ACT.Sin).then_inc(S["cs_in"], 1)
            for c in range(1, 4):
                modulation_rows(c)
            act.wait_ge(S["consts"], 3)

            def x_sumsq(t):
                act.wait_ge(S[f"ld_x{t % 2}"], 16 * (t // 2 + 1))
                lk(a.activation(junk_x, xin[:, t % 2], ACT.Square, accum_out=st[:, 0, t:t + 1]))
                a.activation(st[:, 1, t:t + 1], st[:, 0, t:t + 1], ACT.Sqrt, scale=1.0 / D, bias=eps[:, 0:1]).then_inc(S["sq_done"], 1)
            x_sumsq(0)
            for t in range(NT):
                if t + 1 < NT:
                    x_sumsq(t + 1)
                act.wait_ge(S["am_done"], 1)
                act.wait_ge(S["xt_ps"], t + 1)
                if t + 2 < NT:
                    act.dma_start(xin[:, t % 2], x_tile(t + 2)).then_inc(S[f"ld_x{t % 2}"], 16)
                if t < TP:
                    for k in range(4, KD):
                        last = a.activation(hT[:, k, P * t:P * t + P], B[2 * (t % 2) + k // 4][:, P * (k % 4):P * (k % 4) + P],
                                            ACT.Identity, scale=Am[:, k, 0:1], bias=modT[:, k, 0:1])
                    last.then_inc(S["ht_sb_s"], 1)
            act.wait_ge(S["ys_zero"], 16)
            for n in range(12):
                j, tb = divmod(n, 3)
                act.wait_ge(S["ub_ps"], n + 1)
                if tb == 0 and j >= 2:
                    act.wait_ge(S[f"ub_out{j % 2}"], 16 * (j // 2))
                a.copy(ubT[:, j % 2, :, 48 * tb:48 * tb + 48],
                       B[4 + n % 4][:, 0:384].rearrange("p (c s) -> p s c", s=L)).then_inc(S["ub_sb"], 1)
                if tb == 2:
                    act.wait_ge(S["ub_sb"], n + 1)
                    act.dma_start(ub_d[P * j:P * j + P], ubT[:, j % 2]).then_inc(S[f"ub_out{j % 2}"], 16)
            for n in range(SG // 8):
                act.wait_ge(S["kt_ps"], n + 1)
                for o in range(2):
                    last = a.copy(KT[:, 8 * n + o:8 * n + 8:2], B[4 + 2 * (n % 2) + o][0:SQ, :].rearrange("p (g m) -> p g m", g=4))
                last.then_inc(S["kt_sb"], 1)
            act.wait_ge(S["kt_done"], 1)
            act.wait_ge(S["zeroed"], 1)
            for s in range(L):
                act.dma_start(MT[SQ * s:SQ * s + SQ, :, SQ * s:P], KT[:, :, 0:P - SQ * s]).then_inc(S["mt_placed"], 16)
            act.wait_ge(S["mt_placed"], 16 * L)
            act.wait_ge(S["ub_out0"], 16 * KG // 2)
            act.wait_ge(S["ub_out1"], 16 * KG // 2)
            for s in range(L):
                act.dma_start(U[SQ * s:SQ * s + SQ], ub_d[:, s].rearrange("(g q) c -> q g c", q=SQ)).then_inc(S["u_in"], 16)
            act.dma_start(vgain, v_gain[0].partition_broadcast(P)).then_inc(S["ld_gain"], 16)
            act.dma_start(bsp, b_sp[0].partition_broadcast(P)).then_inc(S["ld_gain"], 16)
            for t in range(NT):
                act.wait_ge(S["v_ps"], t + 1)
                a.activation(vn[:, t], B[4 + (12 + t) % 4][:, :], ACT.Gelu_apprx_tanh).then_inc(S["v_gelu"], 1)
            act.wait_ge(S["stats_v"], NT)
            a.activation(st[:, 2], st[:, 3], ACT.Sqrt, bias=eps[:, 0:1]).then_inc(S["std_v"], 1)
            act.wait_ge(S["list_zero"], 16)
            for n in range(12):
                j, tb = divmod(n, 3)
                act.wait_ge(S["uu_ps"], n + 1)
                a.activation(uT[:, j, 384 * tb:384 * tb + 384], B[4 + (21 + n) % 4][:, 0:384], ACT.Gelu_apprx_tanh).then_inc(S["u_sb"], 1)
            act.wait_ge(S["uu_ps"], 12)
            act.wait_ge(S["e_done"], 1)
            for r in range(2):
                a.copy(H[:, r, :, 0:SS], EH[:, r]).then_inc(S["e_out"], 1)
            act.wait_ge(S["e_out"], 3)
            for s in range(PR // SB):
                act.wait_ge(S["g_ps"], s + 1)
                if s:
                    act.wait_ge(S["v5_ps"], s)
                a.copy(gt, B[2 + s % 2][:, :].rearrange("p (r g m) -> p r g m", r=2, g=SB)).then_inc(S["g_sb"], 1)
                modulation_rows(4 + s)
            act.wait_ge(S["ws_zero"], 1)
            act.wait_ge(S["ws_done"], 2)
            for b in range(DB):
                act.dma_start(wS[DS * b:DS * b + DS, :, DS * b:DS * b + DS], wT[0:DS, :, 0:DS]).then_inc(S["wdiag"], 16)
            for n in range(6):
                act.wait_ge(S["y_ps"], n + 1)
                m = min(3, PR - 3 * n)
                for o in range(2):
                    last = a.activation(Y[:, 6 * n + o:6 * n + 2 * m:2], B[4 + 2 * (n % 2) + o][:, 0:m * CH].rearrange("p (g c) -> p g c", g=m),
                                        ACT.Gelu_apprx_tanh)
                last.then_inc(S["y_sb"], 1)
            act.wait_ge(S["y_sb"], 6)
            for s in range(L):
                act.dma_start(y_d[:, s].rearrange("(g q) c -> q g c", q=SQ), Y[SQ * s:SQ * s + SQ]).then_inc(S["y_out"], 16)
            act.wait_ge(S["y_out"], 16 * L)
            act.dma_start(yT, y_d.rearrange("(j p) s c -> p j (s c)", p=P)).then_inc(S["y_in"], 16)
            act.wait_ge(S["fs_t"], 1)
            a.copy(fsr, B[2][:, :].rearrange("p (r m) -> p r m", r=4)).then_inc(S["fs_sb"], 1)
            act.wait_ge(S["fs_sb"], 1)
            for r, (o_p, o_s) in enumerate(((sp_re, ss_re), (sp_im, ss_im))):
                act.dma_start(o_s[0].rearrange("b (g a) p -> (b g) (a p)", a=2), fsr[:, r]).then_inc(S["fs_out"], 16)
                act.dma_start(o_p[0, 0].rearrange("(g a) p -> g (a p)", a=2), fsr[0:PR, 2 + r]).then_inc(S["fs_out"], 16)
            act.wait_ge(S["v_done"], 1)
            act.dma_start(v_new[0].rearrange("b s d -> (b s) d"), vn[:, NT - 1]).then_inc(S["v_out"], 16)
            act.wait_ge(S["mix_ps"], NT)
            act.wait_ge(S["mod_all"], 1)

            def widen(dst, src, first):
                a.copy(dst.rearrange("p (k b s) -> p k b s", k=KD, b=DB),
                       src[:, first:first + KD, 1:NC].unsqueeze(3).to_broadcast([P, KD, DB, DS])).then_inc(S["wide_in"], 1)
            for n, (src, first) in ((1, (Af, 0)), (3, (modT, 24)), (5, (modT, 16))):
                widen(bc[:, n], src, first)
            for n in range(6):
                act.wait_ge(S["bc_ps"], n + 1)
                for h in range(2):
                    last = a.copy(bc[:, n, 512 * h:512 * h + 512], B[2 * (n % 2) + h][:, :])
                last.then_inc(S["bc_sb"], 1)
            for n in range(16):
                j = n // 4
                act.wait_ge(S["glu_ps"], n + 1)
                if n >= 2:
                    act.wait_ge(S["b_done"], n - 1)
                a.activation(ytm[:, n % 2], B[4 + n % 4][:, 0:288], ACT.Sigmoid, bias=vecT[:, 64 + j:65 + j]).then_inc(S["sig_sb"], 1)
            act.wait_ge(S["b_done"], 16)
            act.dma_start(X1[:, 0:TP], x_prompt[0].rearrange("(t p) d -> p t d", p=P)).then_inc(S["ld_xres"], 16)
            act.dma_start(X1[:, TP], xs_rows).then_inc(S["ld_xres"], 16)
            act.wait_ge(S["fs_out"], 64)
            widen(gfb[:, 1], modT, 40)
            for n in range(6, 8):
                act.wait_ge(S["bc_ps"], n + 1)
                for h in range(2):
                    last = a.copy(gfb[:, n - 6, 512 * h:512 * h + 512], B[2 * (n % 2) + h][:, :])
                last.then_inc(S["bc_sb"], 1)

            def h2_columns(t):
                act.wait_ge(S["h2t_ps"], t + 1)
                if t >= 2:
                    act.wait_ge(S["lg_ps"], t - 1)
                for h in range(2):
                    last = a.copy(h2T[:, t % 2, 4 * h:4 * h + 4], B[h][:, :].rearrange("p (k m) -> p k m", k=4))
                last.then_inc(S["h2t_sb"], 1)
                act.dma_start(h2_d[P * t:P * t + P], h2r[:, t % 2]).then_inc(S[f"h2_out{t % 2}"], 16)

            for t in range(NT):
                act.wait_ge(S["x1_done"], t + 1)
                lk(a.activation(junk_h, X1[:, t], ACT.Square, accum_out=st[:, 0, t:t + 1]))
                a.activation(st[:, 1, t:t + 1], st[:, 0, t:t + 1], ACT.Sqrt, scale=1.0 / D, bias=eps[:, 0:1]).then_inc(S["ss_done"], 1)
                if t:
                    h2_columns(t - 1)
            h2_columns(NT - 1)
            act.dma_start(gfin, g_final.partition_broadcast(P)).then_inc(S["ld_gates"], 16)
            act.wait_ge(S["e_in"], 1)
            a.activation(rt[:, 1], rt[:, 0], ACT.Exp).then_inc(S["exp_done"], 1)
            act.wait_ge(S["tab_done"], 1)
            n_blocks = act.value_load(nblk[0:1, 0:1], min_val=NE, max_val=NE + EXTRA)

            def rows_to_columns(i):
                for h in range(2):
                    act.wait_ge(S["xt2_ps"], 2 * i + h + 1)
                    for m in range(2):
                        last = a.copy(xT[:, 4 * m:4 * m + 4, HB * h:HB * h + HB],
                                      B[4 + 2 * h + m][:, 0:4 * HB].rearrange("p (k n) -> p k n", k=4))
                    last.then_inc(S["xt2_sb"], 1)
            rows_to_columns(0)
            with act.Fori(0, n_blocks) as i:
                for f in range(KE):
                    act.wait_ge(S["gate_ps"], KE * i + f + 1)
                    if f >= 2:
                        act.wait_ge(S["he_done"], KE * i + f)
                    a.activation(sil[:, f % 2], B[f % 2][:, 0:BN], ACT.Silu).then_inc(S["silu_done"], 1)
                rows_to_columns(i + 1)
                for h in range(2):
                    act.wait_ge(S["out_sb"], 2 * i + h + 2)
                    act.dma_start(ys_d[bass.ds(i * BN + HB * h, HB)], OUT[:, h]).then_inc(S["out_d"], 16)
            for t in range(NT):
                act.wait_ge(S["fin_ss"], t + 1)
                lk(a.activation(junk_h, X1[:, t], ACT.Square, accum_out=st[:, 0, t:t + 1]))
                a.activation(st[:, 1, t:t + 1], st[:, 0, t:t + 1], ACT.Sqrt, scale=1.0 / D, bias=eps[:, 0:1]).then_inc(S["fin_rs"], 1)

        @block.tensor
        def _(pe):
            T = nc.tensor
            pe.wait_ge(S["consts"], 1)
            pe.wait_ge(S["ld_vec"], 16 * 6)
            T.transpose(B[0][:, 0:68], rows[0:68, 1], ident[0:68, 0:68])
            T.transpose(B[0][:, 128:200], rows[0:72, 0], ident[0:72, 0:72]).then_inc(S["cols_t"], 1)
            pe.wait_ge(S["ld_mlp"], 16 * 3)
            for h in range(GH):
                last = T.transpose(B[3][:, P * h:P * h + P], wsrow[:, h], ident[:, :])
            last.then_inc(S["ws_t"], 1)
            def modulation(c):
                w = arrived(pe, ("ada", c))
                if c >= 2:
                    pe.wait_ge(S["ada_sb"], c - 1)
                for k in range(KD):
                    last = T.matmul(B[c % 2][0:NC, :], cT[:, :, k], w[:, k], start=(k == 0), stop=(k == KD - 1))
                last.then_inc(S["ring_used"], 1)

            def modulation_turned(c):
                pe.wait_ge(S["ada_rows"], c + 1)
                for j in range(4):
                    last = T.transpose(B[c % 2][:, NC * j:NC * j + NC], arows[:, P * j:P * j + P], ident[0:NC, 0:NC])
                last.then_inc(S["ada_ps"], 1)

            def turned(x, t, banks):
                for k in range(KD):
                    last = T.transpose(B[banks + k // 4][:, P * (k % 4):P * (k % 4) + P], x[:, P * k:P * k + P], ident[:, :])
                return last

            pe.wait_ge(S["cond_done"], 2)
            modulation(0)
            pe.wait_ge(S["ld_s5"], 16 * 8)
            pe.wait_ge(S["ld_c"], 16 * 32)
            for r in range(2):
                T.transpose(B[1][:, PR * r:PR * r + PR], arow[0:PR, r], ident[0:PR, 0:PR])
                T.transpose(B[1][:, P + P * r:2 * P + P * r], srow[:, r], ident[:, :])
            for n in range(4):
                last = T.transpose(B[2][:, P * n:P * n + P], crow[:, n], ident[:, :])
            last.then_inc(S["s5_t"], 1)
            pe.wait_ge(S["cond_t"], 3)
            for c in range(1, 4):
                modulation(c)
                modulation_turned(c - 1)
            modulation_turned(3)
            pe.wait_ge(S["ada_sb"], 4)
            pe.wait_ge(S["ws_done"], 1)
            for t in range(NT):
                pe.wait_ge(S["x_norm"], t + 1)
                if t >= 2:
                    pe.wait_ge(S["ht_sb_v"], t - 1)
                    pe.wait_ge(S["ht_sb_s"], t - 1)
                turned(xin[:, t % 2], t, 2 * (t % 2)).then_inc(S["xt_ps"], 1)
            pe.wait_ge(S["ht_sb_v"], NT)
            pe.wait_ge(S["ht_sb_s"], TP)
            w = arrived(pe, ("in", 2))
            for n in range(12):
                j, tb = divmod(n, 3)
                if n >= 4:
                    pe.wait_ge(S["ub_sb"], n - 3)
                for k in range(KD):
                    last = T.matmul(B[4 + n % 4][:, 0:384], w[:, k, P * j:P * j + P], hT[:, k, 384 * tb:384 * tb + 384],
                                    start=(k == 0), stop=(k == KD - 1))
                last.then_inc(S["ub_ps"], 1)
            pe.wait_ge(S["ub_ps"], 12)
            pe.sem_inc(S["ring_used"], 1)
            pe.wait_ge(S["ub_sb"], 12)
            pe.wait_ge(S["w_table"], 1)
            for g in range(SG):
                n, gp, lo = g // 8, g // 2, SS * (g % 2)
                if g % 8 == 0 and n >= 2:
                    pe.wait_ge(S["kt_sb"], n - 1)
                for r in range(2):
                    last = T.matmul(B[4 + 2 * (n % 2) + g % 2][0:SQ, P * (gp % 4):P * (gp % 4) + P], bb[lo:lo + SS, r, gp, :],
                                    W[lo:lo + SS, r, gp, 0:L, :], start=(r == 0), stop=(r == 1))
                if g % 8 == 7:
                    last.then_inc(S["kt_ps"], 1)
            w = arrived(pe, ("in", 1))
            pe.wait_ge(S["kt_sb"], SG // 8)
            for t in range(NT):
                if t >= 4:
                    pe.wait_ge(S["v_gelu"], t - 3)
                for k in range(KD):
                    last = T.matmul(B[4 + (12 + t) % 4][:, :], hT[:, k, P * t:P * t + P], w[:, k], start=(k == 0), stop=(k == KD - 1))
                last.then_inc(S["v_ps"], 1)
            pe.wait_ge(S["v_ps"], NT)
            pe.sem_inc(S["ring_used"], 1)
            w = arrived(pe, ("in", 0))
            for n in range(12):
                j, tb = divmod(n, 3)
                pe.wait_ge(S["v_gelu"], min(NT, 6 + n))
                if n >= 4:
                    pe.wait_ge(S["u_sb"], n - 3)
                for k in range(KD):
                    last = T.matmul(B[4 + (21 + n) % 4][:, 0:384], w[:, k, P * j:P * j + P], hT[:, k, 384 * tb:384 * tb + 384],
                                    start=(k == 0), stop=(k == KD - 1))
                last.then_inc(S["uu_ps"], 1)
            pe.wait_ge(S["uu_ps"], 12)
            pe.sem_inc(S["ring_used"], 1)
            pe.wait_ge(S["u_in"], 16 * L)
            pe.wait_ge(S["u_sb"], 12)

            def g_turned(s):
                pe.wait_ge(S["g_nat"], s + 1)
                if s >= 2:
                    pe.wait_ge(S["g_sb"], s - 1)
                for r in range(2):
                    for i in range(SB):
                        last = T.transpose(B[2 + s % 2][:, P * (SB * r + i):P * (SB * r + i) + P],
                                           gnat[:, r, i].rearrange("p l q -> p (l q)"), ident[:, :])
                last.then_inc(S["g_ps"], 1)
            g_turned(0)
            for s in range(PR // SB):
                pe.wait_ge(S["g_sb"], s + 1)
                if s >= 2:
                    pe.wait_ge(S["v5_used"], s - 1)
                for r in range(2):
                    for i in range(SB):
                        for lo in (0, SS):
                            last = T.matmul(B[4 + 2 * (s % 2) + r][lo:lo + SS, CH * i:CH * i + CH], gt[:, r, i, lo:lo + SS],
                                            U[:, 2 * (SB * s + i) + lo // SS], start=True, stop=True)
                last.then_inc(S["v5_ps"], 1)
                if s + 1 < PR // SB:
                    g_turned(s + 1)
                modulation(4 + s)
                if s:
                    modulation_turned(3 + s)
            modulation_turned(11)
            pe.wait_ge(S["v_done"], 1)
            pe.wait_ge(S["ws_done"], 2)
            pe.wait_ge(S["wdiag"], 16 * DB)
            pe.wait_ge(S["ada_sb"], 12)
            for t in range(NT):
                if t >= 2:
                    pe.wait_ge(S["mix_sb"], t - 1)
                for h in range(GH):
                    last = T.matmul(B[t % 2][:, P * h:P * h + P], vn[:, t, P * h:P * h + P], (wT if t < TP else wS)[:, h],
                                    start=True, stop=True)
                last.then_inc(S["mix_ps"], 1)
            pe.wait_ge(S["v5_used"], PR // SB)
            pe.wait_ge(S["mt_placed"], 16 * L)
            pe.wait_ge(S["h_done"], 1)
            for g in range(SG):
                n, gp, lo = g // 6, g // 2, SS * (g % 2)
                if g % 6 == 0 and n >= 2:
                    pe.wait_ge(S["y_sb"], n - 1)
                o = B[4 + 2 * (n % 2) + g % 2][:, CH * (gp % 3):CH * (gp % 3) + CH]
                T.matmul(o, MT[:, g], U[:, g], start=True, stop=False)
                for r in range(2):
                    last = T.matmul(o, W[lo:lo + SS, r, gp, 1:L + 1, :], H[lo:lo + SS, r, gp], start=False, stop=(r == 1))
                if g % 6 == 5 or g == SG - 1:
                    last.then_inc(S["y_ps"], 1)
            pe.wait_ge(S["g_sb"], PR // SB)
            for r in range(2):
                T.transpose(B[2][:, P * r:P * r + P], fs[:, r, 1:NC].rearrange("p b g -> p (b g)"), ident[:, :])
            for r in range(2):
                last = T.transpose(B[2][0:PR, P * (2 + r):P * (2 + r) + P], fs[:, r, 0], ident[:, :])
            last.then_inc(S["fs_t"], 1)
            pe.wait_ge(S["mix_sb"], NT)
            pe.wait_ge(S["mod_all"], 1)

            def spread(n, src, first, own):
                if n >= 2:
                    pe.wait_ge(S["bc_sb"], n - 1)
                if n % 2:
                    pe.wait_ge(S["wide_in"], n // 2 + 1)
                for k in range(KD):
                    col = src[:, first + k]
                    wide = col[:, 0:1].to_broadcast([P, P]) if n % 2 == 0 else own[:, P * k:P * k + P]
                    last = T.transpose(B[2 * (n % 2) + k // 4][:, P * (k % 4):P * (k % 4) + P], wide, ident[:, :])
                last.then_inc(S["bc_ps"], 1)
            pe.wait_ge(S["fs_sb"], 1)
            for n, (src, first) in enumerate(((Af, 0), (Af, 0), (modT, 24), (modT, 24), (modT, 16), (modT, 16))):
                spread(n, src, first, bc[:, n])
            w = arrived(pe, ("glu", 0))
            pe.wait_ge(S["y_sb"], 6)
            pe.wait_ge(S["y_in"], 16)
            for n in range(16):
                j, tb = divmod(n, 4)
                if n >= 4:
                    pe.wait_ge(S["sig_sb"], n - 3)
                for k in range(KG):
                    last = T.matmul(B[4 + n % 4][:, 0:288], w[:, k, P * j:P * j + P], yT[:, k, 288 * tb:288 * tb + 288],
                                    start=(k == 0), stop=(k == KG - 1))
                last.then_inc(S["glu_ps"], 1)
            pe.wait_ge(S["glu_ps"], 16)
            pe.sem_inc(S["ring_used"], 1)
            for n in (6, 7):
                spread(n, modT, 40, gfb[:, 1])
            pe.wait_ge(S["bc_sb"], 8)
            w2 = [arrived(pe, ("out", 0)), arrived(pe, ("out", 1))]
            pe.wait_ge(S["b_done"], 16)
            pe.wait_ge(S["sig_sb"], 16)

            def h2_turn(t):
                pe.wait_ge(S["h2_rows"], t + 1)
                if t:
                    pe.wait_ge(S["h2t_sb"], t)
                turned(h2r[:, t % 2], t, 0).then_inc(S["h2t_ps"], 1)

            def router(t):
                pe.wait_ge(S["h2t_sb"], t + 1)
                for k in range(KD):
                    last = T.matmul(B[2][:, NE * t:NE * t + NE], h2T[:, t % 2, k], wr[:, k], start=(k == 0), stop=(k == KD - 1))
                last.then_inc(S["lg_ps"], 1)

            for t in range(NT):
                for h in range(2):
                    n = 2 * t + h
                    if n >= 4:
                        pe.wait_ge(S["wo_used"], n - 3)
                    for k in range(KD):
                        m = (uT if k < KG else bT)[:, k % KG, P * t:P * t + P]
                        last = T.matmul(B[4 + n % 4][:, :], m, w2[h][:, k], start=(k == 0), stop=(k == KD - 1))
                    last.then_inc(S["wo_ps"], 1)
                if t >= 1:
                    h2_turn(t - 1)
                if t >= 2:
                    router(t - 2)
            pe.wait_ge(S["wo_ps"], 2 * NT)
            pe.sem_inc(S["ring_used"], 1)
            pe.sem_inc(S["ring_used"], 1)
            h2_turn(NT - 1)
            router(NT - 2)
            router(NT - 1)
            pe.wait_ge(S["consts"], 3)
            pe.wait_ge(S["oh_done"], 1)
            oh = ohb[:, :, :].rearrange("p t e -> p (t e)")
            T.matmul(B[3][:, 0:NT * NE], tri[:, :], oh, start=True, stop=False)
            for d in range(1, NT):
                T.matmul(B[3][:, NE * d:NT * NE], ones[:, :], oh[:, 0:(NT - d) * NE], start=False, stop=(d == NT - 1))
            for t in range(NT):
                last = T.matmul(B[2][:, 256:256 + NE], ones[:, :], oh[:, NE * t:NE * t + NE], start=(t == 0), stop=(t == NT - 1))
            last.then_inc(S["pre_ps"], 1)
            pe.wait_ge(S["tab_done"], 1)
            n_blocks = pe.value_load(nblk[0:1, 0:1], min_val=NE, max_val=NE + EXTRA)

            def turn_rows(i):
                pe.wait_ge(S["rows_in"], 32 * i + 32)
                for h in range(2):
                    for k in range(KD):
                        last = T.transpose(B[4 + 2 * h + k // 4][:, HB * (k % 4):HB * (k % 4) + HB], XR[:, h, P * k:P * k + P],
                                           ident[0:HB, 0:HB])
                    last.then_inc(S["xt2_ps"], 1)
            turn_rows(0)
            pe.wait_ge(S["xt2_ps"], 2)
            pe.sem_inc(S["rows_free"], 1)
            with pe.Fori(0, n_blocks) as i:
                pe.wait_ge(S["ld_gu"], 32 * i + 32)
                pe.wait_ge(S["xt2_sb"], 2 * i + 2)
                for f in range(KE):
                    pe.wait_ge(S["he_done"], KE * i + (f if f >= 2 else 1))
                    for k in range(KD):
                        last = T.matmul(B[f % 2][:, 0:BN], wg[:, k, P * f:P * f + P], xT[:, k], start=(k == 0), stop=(k == KD - 1))
                    last.then_inc(S["gate_ps"], 1)
                    for k in range(KD):
                        last = T.matmul(B[2 + f % 2][:, 0:BN], wu[:, k, P * f:P * f + P], xT[:, k], start=(k == 0), stop=(k == KD - 1))
                    last.then_inc(S["up_ps"], 1)
                pe.wait_ge(S["up_ps"], KE * i + KE)
                pe.sem_inc(S["gu_free"], 1)
                pe.wait_ge(S["out_sb"], 2 * i + 1)
                turn_rows(i + 1)
                pe.wait_ge(S["xt2_ps"], 2 * i + 4)
                pe.sem_inc(S["rows_free"], 1)
                pe.wait_ge(S["ld_wd"], 16 * i + 16)
                pe.wait_ge(S["he_done"], KE * i + KE + 1)
                for h in range(2):
                    pe.wait_ge(S["xt2_sb"], 2 * i + 3 + h)
                    for n in range(2):
                        for f in range(KE):
                            last = T.matmul(B[4 + 2 * h + n][0:HB, :], heT[:, f, HB * h:HB * h + HB], wd[:, f, 512 * n:512 * n + 512],
                                            start=(f == 0), stop=(f == KE - 1))
                        last.then_inc(S["down_ps"], 1)
                pe.wait_ge(S["down_ps"], 4 * i + 4)
                pe.sem_inc(S["wd_free"], 1)

        @block.vector
        def _(dve):
            v = nc.vector
            lk = chained(dve, S["chain_v"])

            def tt(o, a, b, op):
                return v.tensor_tensor(o, a, b, op)

            dve.wait_ge(S["ws_done"], 1)
            v.memset(wT[64:P, :, 0:64], 0.0).then_inc(S["ws_done"], 1)
            dve.wait_ge(S["cond_t"], 3)
            dve.wait_ge(S["dt_in"], 1)
            tt(q[:, 2], aT[:, 0], q[:, 1], ALU.mult).then_inc(S["mg_in"], 1)
            lk(tt(q[:, 3], aT[:, 1], q[:, 1], ALU.mult))
            lk(v.tensor_scalar(q[:, 10], q[:, 3], 1.0 / (2 * PI), None, ALU.mult))
            lk(v.tensor_copy(qi[:, :], q[:, 10]))
            lk(v.tensor_copy(q[:, 10], qi[:, :]))
            for part in (TWO_PI_HI, TWO_PI_MID, TWO_PI_LO):
                lk(v.scalar_tensor_tensor(out=q[:, 3], in0=q[:, 10], scalar=-part, in1=q[:, 3], op0=ALU.mult, op1=ALU.add))

            def wrap(x):
                for op, lim, add in ((ALU.is_gt, PI, -2 * PI), (ALU.is_lt, -PI, 2 * PI)):
                    lk(v.tensor_scalar(q[:, 10], x, lim, add, op, ALU.mult))
                    lk(tt(x, x, q[:, 10], ALU.add))
            wrap(q[:, 3])
            lk(v.tensor_scalar(q[:, 7], q[:, 3], PI / 2, None, ALU.add))
            wrap(q[:, 7])
            lk(v.tensor_scalar(q[:, 7], q[:, 7], 3.1415925, -3.1415925, ALU.min, ALU.max))
            v.tensor_scalar(q[:, 6], q[:, 3], 3.1415925, -3.1415925, ALU.min, ALU.max).then_inc(S["ang_in"], 1)

            def cmul(o, x, y, t):
                lk(tt(t[0], x[0], y[0], ALU.mult))
                lk(tt(t[1], x[1], y[1], ALU.mult))
                lk(tt(o[0], t[0], t[1], ALU.subtract))
                lk(tt(t[0], x[0], y[1], ALU.mult))
                lk(tt(t[1], x[1], y[0], ALU.mult))
                lk(tt(o[1], t[0], t[1], ALU.add))

            def modulation(c):
                dve.wait_ge(S["ada_ps"], c + 1)
                tt(modT[:, 4 * c:4 * c + 4], B[c % 2][:, 0:4 * NC].rearrange("p (j c) -> p j c", j=4),
                   vecT[:, 4 * c:4 * c + 4].unsqueeze(2).to_broadcast([P, 4, NC]), ALU.add).then_inc(S["ada_sb"], 1)

            for c in range(4):
                modulation(c)
            dve.wait_ge(S["ada_sb"], 4)
            v.scalar_tensor_tensor(out=Am[:, :, :], in0=modT[:, 8:16], scalar=1.0,
                                   in1=vecT[:, 48:56].unsqueeze(2).to_broadcast([P, KD, NC]),
                                   op0=ALU.add, op1=ALU.mult).then_inc(S["am_done"], 1)
            def x_normalised(t):
                dve.wait_ge(S["sq_done"], t + 1)
                lk(v.reciprocal(st[:, 4, t:t + 1], st[:, 1, t:t + 1]))
                v.tensor_scalar(xin[:, t % 2], xin[:, t % 2], st[:, 4, t:t + 1], None, ALU.mult).then_inc(S["x_norm"], 1)
            x_normalised(0)
            for t in range(NT):
                if t + 1 < NT:
                    x_normalised(t + 1)
                dve.wait_ge(S["xt_ps"], t + 1)
                dve.wait_ge(S["am_done"], 1)
                if t < TP:
                    for k in range(4):
                        last = v.tensor_scalar(hT[:, k, P * t:P * t + P], B[2 * (t % 2) + k // 4][:, P * (k % 4):P * (k % 4) + P],
                                               Am[:, k, 0:1], modT[:, k, 0:1], ALU.mult, ALU.add)
                else:
                    for k in range(KD):
                        src = B[2 * (t % 2) + k // 4][:, P * (k % 4):P * (k % 4) + P].rearrange("p (b s) -> p b s", b=DB)
                        o = hT[:, k, P * t:P * t + P].rearrange("p (b s) -> p b s", b=DB)
                        lk(tt(o, src, Am[:, k, 1:NC].unsqueeze(2).to_broadcast([P, DB, DS]), ALU.mult))
                        last = tt(o, o, modT[:, k, 1:NC].unsqueeze(2).to_broadcast([P, DB, DS]), ALU.add)
                last.then_inc(S["ht_sb_v"], 1)
            dve.wait_ge(S["cs_in"], 2)
            dve.wait_ge(S["dt_in"], 3)
            lk(v.memset(LP[:, 0, :, 0], 1.0))
            lk(v.memset(LP[:, 1, :, 0], 0.0))
            lk(tt(LP[:, 0, :, 1], q[:, 4], q[:, 9], ALU.mult))
            lk(tt(LP[:, 1, :, 1], q[:, 4], q[:, 8], ALU.mult))
            n = 1
            while n < L:
                x = (LP[:, 0, :, 1:n + 1], LP[:, 1, :, 1:n + 1])
                y = tuple(LP[:, r, :, n:n + 1].to_broadcast([P, PR, n]) for r in range(2))
                o = (LP[:, 0, :, n + 1:2 * n + 1], LP[:, 1, :, n + 1:2 * n + 1])
                t = tuple(wtmp2[:, :, r, 0:n] for r in range(2))
                cmul(o, x, y, t)
                n *= 2
            for r in range(2):
                for s in range(L):
                    lk(v.tensor_copy(LR[:, r, :, s], LP[:, r, :, L - 1 - s]))
            lk(v.tensor_copy(q[:, 11], q[:, 9]))
            lk(v.tensor_copy(q[:, 12], q[:, 8]))

            def square(c, s, t0, t1):
                lk(tt(t0, c, c, ALU.mult))
                lk(tt(t1, s, s, ALU.mult))
                lk(v.scalar_tensor_tensor(out=s, in0=s, scalar=2.0, in1=c, op0=ALU.mult, op1=ALU.mult))
                lk(tt(c, t0, t1, ALU.subtract))
                lk(tt(t0, c, c, ALU.mult))
                lk(tt(t1, s, s, ALU.mult))
                lk(tt(t0, t0, t1, ALU.add))
                lk(v.tensor_scalar(t0, t0, -0.5, 1.5, ALU.mult, ALU.add))
                lk(tt(c, c, t0, ALU.mult))
                lk(tt(s, s, t0, ALU.mult))
            for _ in range(3):
                square(q[:, 11], q[:, 12], q[:, 13], q[:, 14])
            lk(v.tensor_scalar(q[:, 13], LP[:, 0, :, 1], -1.0, None, ALU.add))
            lk(tt(q[:, 14], aT[:, 0], aT[:, 0], ALU.mult))
            lk(tt(q[:, 15], aT[:, 1], aT[:, 1], ALU.mult))
            lk(tt(q[:, 14], q[:, 14], q[:, 15], ALU.add))
            lk(v.reciprocal(q[:, 14], q[:, 14]))
            lk(tt(q[:, 15], q[:, 13], aT[:, 0], ALU.mult))
            lk(tt(q[:, 16], LP[:, 1, :, 1], aT[:, 1], ALU.mult))
            lk(tt(q[:, 15], q[:, 15], q[:, 16], ALU.add))
            lk(tt(q[:, 15], q[:, 15], q[:, 14], ALU.mult))
            lk(tt(q[:, 16], LP[:, 1, :, 1], aT[:, 0], ALU.mult))
            lk(tt(q[:, 17], q[:, 13], aT[:, 1], ALU.mult))
            lk(tt(q[:, 16], q[:, 16], q[:, 17], ALU.subtract))
            lk(tt(q[:, 16], q[:, 16], q[:, 14], ALU.mult))
            coef = tuple(q[:, 15 + r].unsqueeze(2).to_broadcast([P, PR, SQ]) for r in range(2))
            cmul((bb[:, 0], bb[:, 1]), (bnat[:, 0], bnat[:, 1]), coef,
                 tuple(wtmp2[:, :, r, :] for r in range(2)))
            wide = [P, PR, L + 1, SQ]
            lam = tuple(LP[:, r].unsqueeze(3).to_broadcast(wide) for r in range(2))
            cx = tuple(cc[:, r].unsqueeze(2).to_broadcast(wide) for r in range(2))
            lk(tt(wtmp, lam[0], cx[0], ALU.mult))
            lk(tt(wtmp2, lam[1], cx[1], ALU.mult))
            lk(tt(W[:, 0], wtmp, wtmp2, ALU.subtract))
            lk(tt(wtmp, lam[1], cx[0], ALU.mult))
            lk(tt(wtmp2, lam[0], cx[1], ALU.mult))
            v.scalar_tensor_tensor(out=W[:, 1], in0=wtmp, scalar=-1.0, in1=wtmp2, op0=ALU.mult,
                                   op1=ALU.subtract).then_inc(S["w_table"], 1)

            dve.wait_ge(S["kt_sb"], 4)
            dve.wait_ge(S["ldq"], 16)
            dd = dtmp[0:SQ]
            lk(tt(dd, ident[0:SQ, 0:SQ].unsqueeze(1).to_broadcast([SQ, SG, SQ]), dq[:, :].unsqueeze(2).to_broadcast([SQ, SG, SQ]), ALU.mult))
            tt(KT[:, :, 0:SQ], KT[:, :, 0:SQ], dd, ALU.add).then_inc(S["kt_done"], 1)
            for t in range(NT):
                dve.wait_ge(S["v_gelu"], t + 1)
                lk(v.bn_stats(bn6[:, t % 2], vn[:, t]))
                lk(v.bn_aggr(mv[:, t], bn6[:, t % 2]))
                v.tensor_copy(st[:, 3, t:t + 1], mv[:, t, 1:2]).then_inc(S["stats_v"], 1)
            dve.wait_ge(S["std_v"], 1)
            dve.wait_ge(S["ld_gain"], 32)
            lk(v.reciprocal(st[:, 5], st[:, 2]))
            for t in range(NT):
                lk(v.tensor_scalar(vn[:, t], vn[:, t], mv[:, t, 0:1], st[:, 5, t:t + 1], ALU.subtract, ALU.mult))
                last = tt(vn[:, t], vn[:, t], vgain, ALU.mult)
            last.then_inc(S["v_done"], 1)
            E = tuple(H[:, r, :, 0:P] for r in range(2))
            lk(v.memset(EH[:, 0, :, 0], 1.0))
            lk(v.memset(EH[:, 1, :, 0], 0.0))
            n = 1
            while n < P:
                u = tuple(q[:, 11 + r].unsqueeze(2).to_broadcast([P, PR, n]) for r in range(2))
                if n == SS:
                    dve.sem_inc(S["e_done"], 1)
                    dve.wait_ge(S["uu_ps"], 12)
                    t0, t1 = (area("RA", 4608 + 1024 * r, PR, n) for r in range(2))
                    out = tuple(E[r][:, :, n:2 * n] for r in range(2))
                else:
                    t0, t1 = (area("RD", 1024 * r, PR, n) for r in range(2))
                    out = tuple(EH[:, r, :, n:2 * n] for r in range(2))
                cmul(out, tuple(EH[:, r, :, 0:n] for r in range(2)), u, (t0, t1))
                if n < SS:
                    square(q[:, 11], q[:, 12], q[:, 13], q[:, 14])
                n *= 2
            dve.sem_inc(S["e_out"], 1)
            dve.wait_ge(S["e_out"], 3)
            for s in range(PR // SB):
                sl = slice(SB * s, SB * s + SB)
                Er, Ei = E[0][:, sl], E[1][:, sl]
                dve.wait_ge(S["v5_ps"], s + 1)
                Vr, Vi = (B[4 + 2 * (s % 2) + r][:, 0:SB * CH].rearrange("p (i c) -> p i c", i=SB) for r in range(2))
                lk(v.tensor_copy(H[:, 0, sl, CP:CH], Vr[:, :, CP:CH]))
                lk(v.tensor_copy(H[:, 1, sl, CP:CH], Vi[:, :, CP:CH]))
                lk(tt(tm[:, 0], Er, Vr[:, :, 0:CP], ALU.mult))
                lk(tt(tm[:, 1], Ei, Vi[:, :, 0:CP], ALU.mult))
                lk(tt(tm[:, 2], Er, Vi[:, :, 0:CP], ALU.mult))
                tt(tm[:, 3], Ei, Vr[:, :, 0:CP], ALU.mult).then_inc(S["v5_used"], 1)
                lk(tt(tm[:, 0], tm[:, 0], tm[:, 1], ALU.add))
                dve.wait_ge(S["v5_used"], s + 1)
                lk(tt(tm[:, 2], tm[:, 2], tm[:, 3], ALU.subtract))
                for i in range(SB):
                    decay = q[:, 5, SB * s + i:SB * s + i + 1].to_broadcast([P, CP])
                    lk(v.tensor_tensor_scan(tm[:, 1, i], decay, tm[:, 0, i], 0.0, ALU.mult, ALU.add))
                    lk(v.tensor_tensor_scan(tm[:, 3, i], decay, tm[:, 2, i], 0.0, ALU.mult, ALU.add))
                lk(tt(tm[:, 0], Er, tm[:, 1], ALU.mult))
                lk(tt(tm[:, 2], Ei, tm[:, 3], ALU.mult))
                lk(tt(tm[:, 4], Er, tm[:, 3], ALU.mult))
                lk(tt(tm[:, 5], Ei, tm[:, 1], ALU.mult))
                lk(tt(H[:, 0, sl, 1:CP], tm[:, 0, :, 0:CP - 1], tm[:, 2, :, 0:CP - 1], ALU.subtract))
                lk(tt(H[:, 1, sl, 1:CP], tm[:, 4, :, 0:CP - 1], tm[:, 5, :, 0:CP - 1], ALU.add))
                lk(tt(fs[:, 0, 0, sl], tm[:, 0, :, CP - 1], tm[:, 2, :, CP - 1], ALU.subtract))
                lk(tt(fs[:, 1, 0, sl], tm[:, 4, :, CP - 1], tm[:, 5, :, CP - 1], ALU.add))
                if s:
                    modulation(3 + s)
            modulation(11)
            dve.wait_ge(S["ada_sb"], 12)
            v.scalar_tensor_tensor(out=Af[:, :, :], in0=modT[:, 32:40], scalar=1.0,
                                   in1=vecT[:, 56:64].unsqueeze(2).to_broadcast([P, KD, NC]),
                                   op0=ALU.add, op1=ALU.mult).then_inc(S["mod_all"], 1)
            lk(v.memset(H[:, :, :, 0], 0.0))
            lam8 = tuple(LP[:, r, :, L:L + 1].to_broadcast([P, PR, DB]) for r in range(2))
            hs = tuple(h0[:, r].rearrange("p b g -> p g b") for r in range(2))
            mid = tuple(smp[:, r] for r in range(2))
            ts = tuple(smp[:, 2 + r] for r in range(2))
            cmul(mid, hs, lam8, ts)
            for r in range(2):
                lk(tt(mid[r], mid[r], H[:, r, :, CP:CH:2], ALU.add))
            out = tuple(smp[:, 4 + r] for r in range(2))
            cmul(out, mid, lam8, ts)
            for r in range(2):
                lk(tt(fs[:, r, 1:NC].rearrange("p b g -> p g b"), out[r], H[:, r, :, CP + 1:CH:2], ALU.add))
            for r in range(2):
                lk(v.tensor_copy(H[:, r, :, CP:CH:2], hs[r]))
                last = v.tensor_copy(H[:, r, :, CP + 1:CH:2], mid[r])
            last.then_inc(S["h_done"], 1)
            for t in range(NT):
                dve.wait_ge(S["mix_ps"], t + 1)
                if t:
                    dve.wait_ge(S["mix_sb"], t)
                src = B[t % 2][:, :]
                if t < TP:
                    lk(tt(mtm, src.rearrange("p (h i) -> p h i", h=GH), bsp, ALU.add))
                else:
                    for h in range(GH):
                        lk(tt(mtm[:, h].rearrange("p (b s) -> p b s", b=DB), src[:, P * h:P * h + P].rearrange("p (b s) -> p b s", b=DB),
                              bsp[:, h, 0:DS].unsqueeze(1).to_broadcast([P, DB, DS]), ALU.add))
                tt(uT[:, :, P * t:P * t + P], uT[:, :, P * t:P * t + P], mtm, ALU.mult).then_inc(S["mix_sb"], 1)
            dve.wait_ge(S["v_out"], 16)
            for n in range(16):
                j, tb = divmod(n, 4)
                dve.wait_ge(S["sig_sb"], n + 1)
                o = bT[:, j].rearrange("p (c s) -> p s c", s=L)[:, 2 * tb:2 * tb + 2]
                tt(o, ytm[:, n % 2].rearrange("p (s c) -> p s c", s=2),
                   yT[:, j, 288 * tb:288 * tb + 288].rearrange("p (s c) -> p s c", s=2), ALU.mult).then_inc(S["b_done"], 1)
            dve.wait_ge(S["ld_xres"], 32)
            dve.wait_ge(S["bc_sb"], 6)
            dve.wait_ge(S["y_out"], 16 * L)
            for t in range(NT):
                c = 0 if t < TP else 1
                for h in range(2):
                    n = 2 * t + h
                    sl = slice(512 * h, 512 * h + 512)
                    dve.wait_ge(S["wo_ps"], n + 1)
                    tt(wtm[:, h], B[4 + n % 4][:, :], bc[:, 4 + c, sl], ALU.mult).then_inc(S["wo_used"], 1)
                    dve.wait_ge(S["wo_used"], n + 1)
                    last = tt(X1[:, t, sl], X1[:, t, sl], wtm[:, h], ALU.add)
                    if h == 0:
                        lk(last)
                last.then_inc(S["x1_done"], 1)
                dve.wait_ge(S["ss_done"], t + 1)
                lk(v.reciprocal(st[:, 4, t:t + 1], st[:, 1, t:t + 1]))
                if t >= 2:
                    dve.wait_ge(S[f"h2_out{t % 2}"], 16 * (t // 2))
                    dve.wait_ge(S["h2t_ps"], t - 1)
                lk(v.scalar_tensor_tensor(out=h2r[:, t % 2], in0=X1[:, t], scalar=st[:, 4, t:t + 1], in1=bc[:, c],
                                          op0=ALU.mult, op1=ALU.mult))
                tt(h2r[:, t % 2], h2r[:, t % 2], bc[:, 2 + c], ALU.add).then_inc(S["h2_rows"], 1)
            dve.wait_ge(S["lg_ps"], NT)
            dve.wait_ge(S["v_out"], 16)
            r3 = [rt[:, n].rearrange("p (t e) -> p t e", e=NE) for n in range(16)]
            r4 = [rt[:, n].rearrange("p (g e) -> p g e", e=EG) for n in range(16)]
            n9 = small[:, 0:8]
            col = lambda n: n9[:, n]
            spread = lambda x: x.unsqueeze(2).to_broadcast([P, NT, NE])
            lk(tt(r3[0], B[2][:, 0:NT * NE].rearrange("p (t e) -> p t e", e=NE),
                  brt[:, :].unsqueeze(1).to_broadcast([P, NT, NE]), ALU.add))
            lk(v.tensor_reduce(col(0), r3[0], AX.X, ALU.max))
            tt(r3[0], r3[0], spread(col(0)), ALU.subtract).then_inc(S["e_in"], 1)
            dve.wait_ge(S["exp_done"], 1)
            lk(v.tensor_reduce(col(1), r3[1], AX.X, ALU.add))
            lk(v.reciprocal(col(1), col(1)))
            lk(tt(r3[1], r3[1], spread(col(1)), ALU.mult))

            def rank(o, x, t, w):
                for i in range(4):
                    lk(v.memset(o[:, :, i], float(i)))
                for d in (1, 2, 3):
                    lk(tt(t[:, :, 0:4 - d], x[:, :, d:4], x[:, :, 0:4 - d], ALU.is_gt))
                    lk(tt(o[:, :, 0:4 - d], o[:, :, 0:4 - d], t[:, :, 0:4 - d], ALU.add))
                    lk(tt(o[:, :, d:4], o[:, :, d:4], t[:, :, 0:4 - d], ALU.subtract))
            rank(r4[2], r4[1], r4[3], NT * NG)
            lk(v.tensor_scalar(rt[:, 4], rt[:, 2], 1.5, None, ALU.is_lt))
            lk(tt(rt[:, 5], rt[:, 4], rt[:, 1], ALU.mult))
            gsum = small[:, 8:12].rearrange("p a b -> p (a b)")
            g3 = [small[:, 8 + 4 * n:12 + 4 * n].rearrange("p a b -> p (a b)").rearrange("p (t g) -> p t g", g=NG) for n in range(3)]
            lk(v.tensor_reduce(gsum, r4[5], AX.X, ALU.add))
            rank(g3[1], g3[0], g3[2], NT)
            g1f = small[:, 12:16].rearrange("p a b -> p (a b)")
            lk(v.tensor_scalar(g1f, g1f, 0.5, None, ALU.is_lt))
            gsel = g1f.unsqueeze(2).to_broadcast([P, NT * NG, EG])
            lk(v.tensor_scalar(rt[:, 6], rt[:, 2], 0.5, None, ALU.is_lt))
            lk(tt(rt[:, 7], rt[:, 4], rt[:, 6], ALU.subtract))
            for n in (6, 7):
                lk(tt(r4[n], r4[n], gsel, ALU.mult))
            tt(ohb[:, :, :], r3[6], r3[7], ALU.add).then_inc(S["oh_done"], 1)
            for k in range(2):
                lk(tt(rt[:, 8], rt[:, 6 + k], rt[:, 1], ALU.mult))
                lk(v.tensor_reduce(col(2 + k), r3[8], AX.X, ALU.add))
            lk(tt(col(4), col(2), col(3), ALU.add))
            lk(v.reciprocal(col(4), col(4)))
            for k in range(2):
                lk(tt(gates[:, k], col(2 + k), col(4), ALU.mult))
            dve.wait_ge(S["zeroed"], 5)
            dve.wait_ge(S["pre_ps"], 1)
            cnt = B[2][:, 256:256 + NE]
            nb, cum, shift = rt[:, 10, 0:NE], rt[:, 11, 0:NE], rt[:, 12, 0:NE]
            lk(v.tensor_scalar(nb, cnt, BN + 0.5, None, ALU.is_gt))
            for r in range(2, ROUNDS):
                lk(v.tensor_scalar(cum, cnt, r * BN + 0.5, None, ALU.is_gt))
                lk(tt(nb, nb, cum, ALU.add))
            lk(v.memset(shift, 1.0))
            lk(v.tensor_tensor_scan(cum, shift, nb, 0.0, ALU.mult, ALU.add))
            lk(tt(shift, cum, nb, ALU.subtract))
            lk(v.tensor_scalar(shift, shift, NE - 1.0, float(BN), ALU.add, ALU.mult))
            lk(tt(shift, shift, ebase[:, :], ALU.subtract))
            wide = lambda x: x.unsqueeze(1).to_broadcast([P, NT, NE])
            before = B[3][:, 0:NT * NE].rearrange("p (t e) -> p t e", e=NE)
            lk(v.tensor_scalar(r3[9], before, BN - 0.5, None, ALU.is_gt))
            lk(tt(r3[9], r3[9], wide(shift), ALU.mult))
            lk(tt(r3[9], r3[9], before, ALU.add))
            lk(tt(r3[9], r3[9], wide(ebase[:, :]), ALU.add))
            for k in range(2):
                lk(tt(rt[:, 8], rt[:, 6 + k], rt[:, 9], ALU.mult))
                lk(v.tensor_reduce(col(5), r3[8], AX.X, ALU.add))
                last = v.tensor_copy(lst[:, k], col(5))
                if k == 0:
                    lk(last)
            last.then_inc(S["pos_done"], 1)
            big = rt[0:1, 13:15].rearrange("p a b -> p (a b)")[:, 0:EXTRA * NE].rearrange("p (x e) -> p x e", e=NE)
            lk(tt(big, cum[0:1].unsqueeze(1).to_broadcast([1, EXTRA, NE]), iot[:, :].unsqueeze(2).to_broadcast([1, EXTRA, NE]), ALU.is_le))
            lk(v.tensor_copy(b64[:, 0:NE], etab[:, :]))
            lk(v.tensor_reduce(b64[:, NE:MAXB], big, AX.X, ALU.add))
            lk(v.tensor_scalar(b64[:, NE:MAXB], b64[:, NE:MAXB], NE - 1.0, None, ALU.min))
            lk(v.tensor_copy(tab[:, 0:MAXB], b64[:, 0:MAXB]))
            lk(v.tensor_scalar(shift[0:1, 0:1], cum[0:1, NE - 1:NE], float(NE), None, ALU.add))
            v.tensor_copy(nblk[:, :], shift[0:1, 0:1]).then_inc(S["tab_done"], 1)
            dve.wait_ge(S["tab_done"], 1)
            n_blocks = dve.value_load(nblk[0:1, 0:1], min_val=NE, max_val=NE + EXTRA)
            dve.sem_inc(S["he_done"], 1)
            dve.sem_inc(S["out_sb"], 1)
            dve.sem_inc(S["out_d"], 16)
            with dve.Fori(0, n_blocks) as i:
                for f in range(KE):
                    dve.wait_ge(S["silu_done"], KE * i + f + 1)
                    dve.wait_ge(S["up_ps"], KE * i + f + 1)
                    tt(heT[:, f], sil[:, f % 2], B[2 + f % 2][:, 0:BN], ALU.mult).then_inc(S["he_done"], 1)
                dve.wait_ge(S["out_d"], 32 * i + 16)
                for h in range(2):
                    for n in range(2):
                        dve.wait_ge(S["down_ps"], 4 * i + 2 * h + n + 1)
                        last = v.tensor_copy(OUT[:, h, 512 * n:512 * n + 512], B[4 + 2 * h + n][0:HB, :])
                    last.then_inc(S["out_sb"], 1)
            dve.wait_ge(S["ld_gates"], 16)
            for t in range(NT):
                c = 0 if t < TP else 1
                dve.wait_ge(S[f"comb_in{t % 2}"], 32 * (t // 2) + 32)
                y0, y1 = YA[:, t % 2, 0], YA[:, t % 2, 1]
                lk(v.tensor_scalar(y0, y0, gates[:, 0, t:t + 1], None, ALU.mult))
                lk(v.scalar_tensor_tensor(out=y0, in0=y1, scalar=gates[:, 1, t:t + 1], in1=y0, op0=ALU.mult, op1=ALU.add))
                lk(tt(y0, y0, gfb[:, c], ALU.mult))
                tt(X1[:, t], X1[:, t], y0, ALU.add).then_inc(S["fin_ss"], 1)
                dve.wait_ge(S["fin_ss"], t + 1)
                dve.sem_inc(S["comb_used"], 1)
                dve.wait_ge(S["fin_rs"], t + 1)
                lk(v.reciprocal(st[:, 4, t:t + 1], st[:, 1, t:t + 1]))
                if t >= 2:
                    dve.wait_ge(S[f"y_done{t % 2}"], 16 * (t // 2))
                v.scalar_tensor_tensor(out=fin[:, t % 2], in0=X1[:, t], scalar=st[:, 4, t:t + 1], in1=gfin,
                                       op0=ALU.mult, op1=ALU.mult).then_inc(S["fin_done"], 1)


_INS = ['x_prompt', 'x_sample', 'c_prompt', 'c_sample', 'state_s5_re', 'state_s5_im', 'w_ada', 'b_ada', 'g_norm_mix',
        'g_norm_ffn', 'w_in', 'gmlp_v_gain', 'gmlp_w_spatial', 'gmlp_b_spatial', 's5_a_re', 's5_a_im', 's5_log_dt',
        's5_b_re', 's5_b_im', 's5_c_re', 's5_c_im', 's5_d', 's5_w_glu', 's5_b_glu', 'w_out', 'w_router', 'b_router',
        'w_gate', 'w_up', 'w_down', 'g_final']
_OUTS = [(1, SEQ, D), (DB, DS, D), (1, 1, SG, SS), (1, 1, SG, SS), (1, DB, SG, SS), (1, DB, SG, SS), (1, DB, DS, GW)]


def kernel(**inputs):
    import numpy as _np
    import concourse.bacc as _bacc
    from concourse import mybir as _mybir
    from concourse.bass_utils import run_bass_kernel_spmd as _run

    nc = _bacc.Bacc("TRN2", target_bir_lowering=False, num_devices=1)
    arrays, args = {}, []
    for name in _INS:
        a = _np.ascontiguousarray(inputs[name])
        arrays[f"in_{name}_dram"] = a
        args.append(nc.dram_tensor(f"in_{name}_dram", a.shape, _mybir.dt.from_np(a.dtype), kind="ExternalInput").ap())
    for i, shape in enumerate(_OUTS):
        args.append(nc.dram_tensor(f"out_{i}_dram", shape, _mybir.dt.float32, kind="ExternalOutput").ap())
    hybrid_step(nc, *args)
    r = _run(nc, [arrays], core_ids=[0])
    return tuple(r.results[0][f"out_{i}_dram"] for i in range(len(_OUTS)))
```

```python
import math
from contextlib import ExitStack

import concourse.bass as bass
from concourse import mybir

ALU = mybir.AluOpType
ACT = mybir.ActivationFunctionType
AX = mybir.AxisListType
F32 = mybir.dt.float32
I32 = mybir.dt.int32
BF16 = mybir.dt.bfloat16
F32R = mybir.dt.float32r

P = 128
D = 1024
KD = D // P
SEQ, DB, DS = 1024, 8, 16
NT = (SEQ + DB * DS) // P
TP = SEQ // P
TOK = NT * P
NC = 1 + DB
GW = D // 2
GH = 4
KG = GW // P
SG, SQ, SS = 32, 16, 64
PR = SG // 2
L = 8
CH = TOK // L
CP = SEQ // L
SB = 2
NE, NG, EG = 16, 4, 4
DE = D // 2
KE = DE // P
BN = 192
HB = BN // 2
CAP = TOK
ROUNDS = CAP // BN
EXTRA = 2 * TOK // (BN + 1)
MAXB = NE + EXTRA
LROWS = (MAXB + 1) * BN
SLOTS, SLW = 2 * KE + KE, D
EPS = 1e-6
PI = math.pi
TWO_PI_HI = 6.28125
TWO_PI_MID = 0.0019340515136718750
TWO_PI_LO = 2 * math.pi - TWO_PI_HI - TWO_PI_MID
assert CAP % BN == 0 and L * SQ == P


def hybrid_step(nc, x_prompt, x_sample, c_prompt, c_sample, state_re, state_im, w_ada, b_ada, g_mix, g_ffn,
                w_in, v_gain, w_sp, b_sp, a_re, a_im, log_dt, b_re, b_im, c_re, c_im, d_skip, w_glu, b_glu,
                w_out, w_router, b_router, w_gate, w_up, w_down, g_final,
                y_prompt, y_sample, sp_re, sp_im, ss_re, ss_im, v_new):
    ctx = ExitStack()
    with ctx:
        def sb(name, shape, dt=F32):
            return ctx.enter_context(nc.sbuf_tensor(name, shape, dt))

        def sem(name):
            return ctx.enter_context(nc.semaphore(name))

        ctx.enter_context(nc.allow_non_contiguous_dma(reason="small parameter tables"))

        ub_d = nc.dram_tensor("ub_scratch", (GW, L, CH), F32).ap()
        y_d = nc.dram_tensor("y_scratch", (GW, L, CH), F32).ap()
        h2_d = nc.dram_tensor("h2_scratch", (TOK, D), F32).ap()
        list_d = nc.dram_tensor("list_scratch", (LROWS, 1), I32).ap()
        ys_d = nc.dram_tensor("expert_rows", (MAXB * BN, D), F32).ap()

        sizes = dict(RA=9216, RB=4608, RC=4608, RD=2304, RE=4608, RF=4608, RG=4096, RT=2560, RW=12288)
        arena_at = -(-nc.sbuf_base // 32) * 32
        arena = sb("arena", [P, sum(sizes.values())])
        off = {}
        at = 0
        for name, n in sizes.items():
            off[name] = at
            at += n

        def area(region, start, *shape, parts=P):
            n = math.prod(shape)
            a = off[region] + start
            flat = arena[0:parts, a:a + n]
            if len(shape) == 1:
                return flat
            names = ["i", "j", "k", "l"][:len(shape)]
            return flat.rearrange("p (" + " ".join(names) + ") -> p " + " ".join(names),
                                  **dict(zip(names[1:], shape[1:])))

        ring = area("RW", 0, 3, KD, 512)
        hT = area("RA", 0, KD, TOK)
        H = area("RA", 0, 2, PR, CH)
        Y = area("RA", 4608, SG, CH)
        dtmp = area("RC", 0, SG, SQ)
        uT = area("RB", 0, KG, TOK)
        vn = area("RC", 0, NT, GW)
        bT = area("RC", 0, KG, TOK)
        ubT = area("RD", 0, 2, L, CH)
        U = area("RE", 0, SG, CH)
        yT = area("RE", 0, KG, L * CH)
        W = area("RF", 0, 2, PR, L + 1, SQ)
        X1 = area("RE", 0, NT, D)
        MT = area("RG", 0, SG, P)
        xin = [area("RT", 0, D), area("RT", D, D), area("RC", 0, D), area("RC", D, D)]
        rows = area("RB", 0, 2, P)
        arow = area("RB", 256, 2, P)
        srow = area("RB", 512, 2, P)
        crow = area("RB", 768, 4, P)
        wsrow = area("RB", 1280, GH, P)
        junk_x = area("RB", 2304, 512).bitcast(BF16)
        junk_h = area("RA", 5120, 512).bitcast(BF16)
        zi = area("RB", 2816, LROWS // P).bitcast(I32)
        zf = area("RT", 2048, 512)
        vgain = area("RD", 1536, GW)
        bsp = area("RD", 512, GH, P)
        smp = area("RT", 1024, 6, PR, DB)
        cc = area("RT", 2048, 2, PR, SQ)
        arows = area("RD", 1024, 512, parts=NC)
        EH = area("RT", 512, 2, PR, SS)
        wS = area("RT", 0, GH, P)
        bnat = area("RB", 1792, 2, PR, SQ)
        wtmp = area("RC", 0, 2, PR, L + 1, SQ)[:, 0]
        wtmp2 = area("RC", 2304, PR, L + 1, SQ)
        KT = area("RE", 0, SG, P, parts=SQ)
        gnat = area("RT", 0, 2, SB, L, SQ)
        gt = area("RT", 512, 2, SB, P)
        tm = area("RT", 1024, 6, SB, P)
        bc = area("RG", 0, 6, D)
        gfb = area("RD", 0, 2, D)
        h2r = area("RA", 0, 2, D)
        h2T = area("RA", 2048, 2, KD, P)
        wtm = area("RA", 4096, 2, 512)
        ytm = area("RD", 0, 2, 288)
        gtm = area("RD", 0, 2, SB, L * SQ).rearrange("p i s (l q) -> p i s l q", l=L)
        mtm = area("RD", 1024, GH, P)
        fsr = area("RD", 1536, 4, P)
        XR = area("RB", 0, 2, D, parts=HB)
        OUT = area("RB", 2048, 2, D, parts=HB)
        gate = area("RC", 3072, 2, BN)
        up = area("RC", 3072 + 2 * BN, 2, BN)
        sil = area("RC", 3072 + 4 * BN, 2, BN)
        he = area("RC", 3072 + 6 * BN, 2, BN)

        def rounded(name, region, start, *shape, dt=F32R):
            return nc.alloc_sbuf_tensor_at(name, [P, *shape], dt, offset=arena_at + 4 * (off[region] + start))
        w_raw = [rounded(f"w_raw{n}", "RW", n * SLW, SLW, dt=F32)[:, :] for n in range(SLOTS)]
        w_lo = [rounded(f"w_lo{n}", "RW", n * SLW, SLW)[:, :] for n in range(SLOTS)]
        w_hi = [rounded(f"w_hi{n}", "RA", n * SLW, SLW)[:, :] if n < 9 else rounded(f"w_hi{n}", "RG", D + (n - 9) * SLW, SLW)[:, :]
                for n in range(SLOTS)]
        x_hl = rounded("x_hl", "RC", 0, KD, 2, BN)
        he_hl = rounded("he_hl", "RT", 0, 2, KE, HB + P)
        SLICE_ORDER = [("gate", 0), ("up", 0), ("gate", 1), ("up", 1), ("gate", 2), ("up", 2), ("gate", 3), ("up", 3)] \
            + [("down", f) for f in range(KE)]

        YA = area("RW", 0, 4, 2, D)
        fin = area("RW", 8192, 2, D)
        gfin = area("RG", 0, D)
        rt = area("RC", 0, 16, NT * NE)

        ident = sb("ident", [P, P])
        tri = sb("tri", [P, P], BF16)
        ones = sb("ones", [P, P], BF16)
        modT = sb("modT", [P, 48, NC])
        Am = sb("Am", [P, KD, NC])
        Af = sb("Af", [P, KD, NC])
        vecT = sb("vecT", [P, 68])
        cT = sb("cT", [P, NC, KD])
        wT = sb("wT", [P, GH, P])
        LP = sb("LP", [P, 2, PR, L + 1])
        LR = sb("LR", [P, 2, PR, L])
        aT = sb("aT", [P, 2, PR])
        h0 = sb("h0", [P, 2, DB, PR])
        q = sb("q", [P, 24, PR])
        qi = sb("qi", [P, PR], I32)
        bb = sb("bb", [P, 2, PR, SQ])
        dq = sb("dq", [SQ, SG])
        fs = sb("fs", [P, 2, NC, PR])
        st = sb("st", [P, 6, NT])
        bn6 = sb("bn6", [P, 2, 6])
        wr = sb("wr", [P, KD, NE])
        brt = sb("brt", [P, NE])
        mv = sb("mv", [P, NT, 2])
        small = area("RC", 2304, 20, NT)
        ohb = sb("ohb", [P, NT, NE], BF16)
        ebase = sb("ebase", [P, NE])
        iot = sb("iot", [1, EXTRA])
        etab = sb("etab", [1, NE])
        lst = sb("lst", [P, 2, NT], I32)
        tokid = sb("tokid", [P, NT], I32)
        gates = sb("gates", [P, 2, NT])
        tab = sb("tab", [1, 32], I32)
        nblk = sb("nblk", [1, 2], I32)
        idx = sb("idx", [HB, 2], I32)
        eps = sb("eps", [P, 1])
        b64 = area("RC", 2560, 32, parts=1)

        B = [ctx.enter_context(nc.psum_tensor(f"bank{i}", [P, 512], F32)) for i in range(8)]

        names = ("ys_zero idx_seen wide_in ws_zero ld_gain ld_vec ld_s5 ld_c ld_mlp ld_x0 ld_x1 ld_x2 ld_x3 ld_w0 ld_w1 ld_w2 ld_xres ld_gates "
                 "consts zeroed cols_t cond_t s5_t ws_t cond_done cT_done w_table kt_ps kt_sb kt_done mt_placed "
                 "ada_rows ada_ps ada_sb am_done sq_done x_rs x_norm x_used xt_ps ht_sb_v ht_sb_s ring_used ub_ps ub_sb ub_out0 ub_out1 u_in "
                 "v_ps v_gelu v_done v_out uu_ps u_sb e_done g_nat g_ps g_sb v5_ps v5_used h_done ws_done "
                 "mix_ps mix_sb y_ps y_sb y_out y_in glu_ps sig_sb b_done bc_ps bc_sb wo_ps wo_used x1_done ss_done rs_done "
                 "h2_rows h2_out0 h2_out1 h2t_ps h2t_sb lg_ps exp_done e_in oh_done pre_ps pos_done list_zero scat tab_done "
                 "idx_in rows_in xt2_ps xt2_sb gate_done up_done he_full silu_done he_done w_used hi_done lo_done xh_done down_ps out_sb out_d rows_free "
                 "comb_in0 comb_in1 comb_in2 comb_in3 comb_used comb_scaled fin_ss fin_rs fin_done y_done0 y_done1 fs_t fs_sb fs_out chain_v chain_s chain_g chain_p smp wdiag "
                 "x_scale e_out dt_in mg_in ang_in cs_in stats_v std_v ldq mod_all").split()
        S = {n: sem(n) for n in names}
        LDS = [sem(f"ld_slice{n}") for n in range(SLOTS)]

        block = ctx.enter_context(nc.Block())

        def chained(eng, s):
            count = [0]

            def link(ins):
                count[0] += 1
                ins.then_inc(s, 1)
                eng.wait_ge(s, count[0])
            return link

        def cols(w, c):
            return w.rearrange("(k p) n -> p k n", p=P)[:, :, c * 512:(c + 1) * 512]
        ORDER = [("ada", c) for c in range(4)] + [("in", 2), ("in", 1), ("in", 0)] \
            + [("ada", c) for c in range(4, 12)] + [("glu", 0), ("out", 0), ("out", 1)]
        WSRC = {"ada": w_ada[0], "in": w_in[0], "glu": w_glu[0], "out": w_out[0]}
        place = {item: n for n, item in enumerate(ORDER)}
        LDW = [S["ld_w0"], S["ld_w1"], S["ld_w2"]]

        def arrived(eng, item):
            n = place[item]
            eng.wait_ge(LDW[n % 3], 16 * (n // 3 + 1))
            return ring[:, n % 3]

        def ada_bank(c):
            return B[(4 if c < 4 else 0) + c % 2]

        x_rows = x_prompt[0].rearrange("(t p) d -> t p d", p=P)
        xs_rows = x_sample.rearrange("b s d -> (b s) d")

        def x_tile(t):
            return x_rows[t] if t < TP else xs_rows

        def c_rows(eng, r, c_in):
            for h in range(2):
                for gg in range(8):
                    src = c_in[0, 16 * h + 2 * gg:16 * h + 2 * gg + 2].rearrange("a q p -> q a p")
                    eng.dma_start(crow[16 * gg:16 * gg + 16, 2 * r + h].rearrange("q (a p) -> q a p", a=2), src).then_inc(S["ld_c"], 16)

        @block.sync
        def _(sp):
            sp.dma_start(rows[0:8, 0], c_prompt.rearrange("a (k p) -> (a k) p", p=P)).then_inc(S["ld_vec"], 16)
            sp.dma_start(rows[8:72, 0], c_sample.rearrange("a (k p) -> (a k) p", p=P)).then_inc(S["ld_vec"], 16)
            sp.dma_start(rows[0:48, 1], b_ada.rearrange("a (k p) -> (a k) p", p=P)).then_inc(S["ld_vec"], 16)
            sp.dma_start(rows[48:56, 1], g_mix.rearrange("a (k p) -> (a k) p", p=P)).then_inc(S["ld_vec"], 16)
            sp.dma_start(rows[56:64, 1], g_ffn.rearrange("a (k p) -> (a k) p", p=P)).then_inc(S["ld_vec"], 16)
            sp.dma_start(rows[64:68, 1], b_glu.rearrange("a (k p) -> (a k) p", p=P)).then_inc(S["ld_vec"], 16)
            for n in range(3):
                kind, c = ORDER[n]
                sp.dma_start(ring[:, n], cols(WSRC[kind], c)).then_inc(LDW[n], 16)
            for n in range(3, len(ORDER)):
                kind, c = ORDER[n]
                sp.wait_ge(S["ring_used"], n - 2)
                dst = ring[:, n % 3, 0:4] if kind == "glu" else ring[:, n % 3]
                sp.dma_start(dst, cols(WSRC[kind], c)).then_inc(LDW[n % 3], 16)
            def slices(e, used):
                for n, (kind, f) in enumerate(SLICE_ORDER):
                    if used is not None:
                        sp.wait_ge(S["w_used"], used + n + 1)
                    if kind == "down":
                        sp.dma_start(w_raw[n], w_down[0, e].rearrange("a (f p) n -> p (a f) n", p=P)[:, f]).then_inc(LDS[n], 16)
                    else:
                        w = w_gate if kind == "gate" else w_up
                        src = w[0, e].rearrange("a (k p) n -> p (a k) n", p=P)[:, :, P * f:P * f + P]
                        sp.dma_start(w_raw[n].rearrange("p (k n) -> p k n", k=KD), src).then_inc(LDS[n], 16)
            sp.wait_ge(S["ring_used"], len(ORDER))
            slices(slice(0, 1), None)
            sp.wait_ge(S["tab_done"], 1)
            n_blocks = sp.value_load(nblk[0:1, 0:1], min_val=NE, max_val=NE + EXTRA)
            with sp.Fori(1, n_blocks) as i:
                e = sp.value_load(tab[0:1, bass.ds(i, 1)], min_val=0, max_val=NE - 1)
                slices(bass.ds(e, 1), SLOTS * (i - 1))
            for t in range(NT):
                sp.wait_ge(S["fin_done"], t + 1)
                dst = y_prompt[0].rearrange("(t p) d -> t p d", p=P)[t] if t < TP else y_sample.rearrange("b s d -> (b s) d")
                sp.dma_start(dst, fin[:, t % 2]).then_inc(S[f"y_done{t % 2}"], 16)
            sp.wait_ge(S["y_done0"], 16 * 5)
            sp.wait_ge(S["y_done1"], 16 * 4)
            sp.wait_ge(S["fs_out"], 64)
            sp.wait_ge(S["v_out"], 16)

        @block.gpsimd
        def _(gp):
            g = nc.gpsimd
            lk = chained(gp, S["chain_g"])
            lk(g.memset(ident[:, :], 0.0))
            lk(g.affine_select(out=ident[:, :], in_=ident[:, :], compare_op=ALU.not_equal, fill=1.0, base=0,
                               pattern=[[-1, P]], channel_multiplier=1))
            g.memset(eps[:, :], EPS).then_inc(S["consts"], 1)
            g.memset(ones[:, :], 1.0).then_inc(S["consts"], 1)
            lk(g.memset(tri[:, :], 1.0))
            g.affine_select(out=tri[:, :], in_=tri[:, :], compare_op=ALU.is_gt, fill=0.0, base=0,
                            pattern=[[1, P]], channel_multiplier=-1).then_inc(S["consts"], 1)
            gp.dma_start(arow[0:PR, 0], a_re[0].rearrange("(g a) p -> g (a p)", a=2)).then_inc(S["ld_s5"], 16)
            gp.dma_start(arow[0:PR, 1], a_im[0].rearrange("(g a) p -> g (a p)", a=2)).then_inc(S["ld_s5"], 16)
            for r, (s_in, b_in) in enumerate(((state_re, b_re), (state_im, b_im))):
                gp.dma_start(srow[:, r], s_in[0].rearrange("b (g a) p -> (b g) (a p)", a=2)).then_inc(S["ld_s5"], 16)
                gp.dma_start(bnat[:, r], b_in[0].rearrange("(g a) p q -> (a p) g q", a=2)).then_inc(S["ld_s5"], 16)
            for a in range(2):
                gp.dma_start(q[SS * a:SS * a + SS, 0], log_dt[0].rearrange("(g a) -> a g", a=2)[a].partition_broadcast(SS)).then_inc(S["ld_s5"], 16)
            gp.dma_start(dq[:, :], d_skip[0].rearrange("g q -> q g")).then_inc(S["ldq"], 16)
            c_rows(gp, 0, c_re)
            c_rows(gp, 1, c_im)
            g.memset(MT, 0.0).then_inc(S["zeroed"], 1)
            lk(g.memset(zi, 0))
            g.iota(tokid[:, :], pattern=[[P, NT]], base=0, channel_multiplier=1).then_inc(S["zeroed"], 1)
            g.iota(ebase[:, :], pattern=[[BN, NE]], base=0, channel_multiplier=0, allow_small_or_imprecise_dtypes=True).then_inc(S["zeroed"], 1)
            g.iota(iot[:, :], pattern=[[1, EXTRA]], base=0, channel_multiplier=0, allow_small_or_imprecise_dtypes=True).then_inc(S["zeroed"], 1)
            g.iota(etab[:, :], pattern=[[1, NE]], base=0, channel_multiplier=0, allow_small_or_imprecise_dtypes=True).then_inc(S["zeroed"], 1)
            gp.dma_start(list_d.rearrange("(p n) a -> p (n a)", p=P), zi).then_inc(S["list_zero"], 16)
            gp.wait_ge(S["w_table"], 1)
            for s in range(PR // SB):
                sl = slice(SB * s, SB * s + SB)
                if s == 0:
                    gp.wait_ge(S["xt_ps"], NT)
                    gp.wait_ge(S["e_done"], 1)
                    gp.wait_ge(S["ub_out0"], 16 * KG // 2)
                    gp.wait_ge(S["ub_out1"], 16 * KG // 2)
                else:
                    gp.wait_ge(S["g_ps"], s)
                for r in range(2):
                    lam0 = LR[:, 0, sl].unsqueeze(3).to_broadcast([P, SB, L, SQ])
                    lam1 = LR[:, 1, sl].unsqueeze(3).to_broadcast([P, SB, L, SQ])
                    b0 = bb[:, r, sl].unsqueeze(2).to_broadcast([P, SB, L, SQ])
                    b1 = bb[:, 1 - r, sl].unsqueeze(2).to_broadcast([P, SB, L, SQ])
                    t0, t1 = gtm[:, 0], gtm[:, 1]
                    lk(g.tensor_tensor(t0, lam0, b0, ALU.mult))
                    lk(g.tensor_tensor(t1, lam1, b1, ALU.mult))
                    last = g.tensor_tensor(gnat[:, r], t0, t1, ALU.subtract if r == 0 else ALU.add)
                    if r == 0:
                        lk(last)
                    else:
                        last.then_inc(S["g_nat"], 1)
                        gp.wait_ge(S["g_nat"], s + 1)
            gp.wait_ge(S["g_ps"], PR // SB)
            g.memset(wS, 0.0).then_inc(S["ws_zero"], 1)
            gp.wait_ge(S["mix_ps"], NT)
            gp.wait_ge(S["h_done"], 1)
            gp.wait_ge(S["ld_xres"], 32)
            lk(g.memset(zf, 0.0))
            gp.dma_start(ys_d[NE * BN:MAXB * BN].rearrange("(p a) (b n) -> p (a b) n", p=64, n=512),
                         zf[0:64].unsqueeze(1).to_broadcast([64, EXTRA * BN // 64 * 2, 512])).then_inc(S["ys_zero"], 16)
            gp.wait_ge(S["list_zero"], 16)
            gp.wait_ge(S["pos_done"], 1)
            for t in range(NT):
                for k in range(2):
                    gp.indirect_dma_start(out=list_d, out_offset=bass.IndirectOffsetOnAxis(ap=lst[:, k, t:t + 1], axis=0),
                                          in_=tokid[:, t:t + 1], in_offset=None).then_inc(S["scat"], 16)
            gp.wait_ge(S["scat"], 16 * 2 * NT)
            gp.wait_ge(S["h2_out0"], 16 * 5)
            gp.wait_ge(S["h2_out1"], 16 * 4)
            gp.wait_ge(S["tab_done"], 1)
            n_blocks = gp.value_load(nblk[0:1, 0:1], min_val=NE, max_val=NE + EXTRA)
            gp.sem_inc(S["rows_free"], 1)
            with gp.Fori(0, n_blocks) as i:
                gp.wait_ge(S["rows_free"], i + 1)
                gp.dma_start(idx[:, :], list_d[bass.ds(i * BN, BN)].rearrange("(h p) a -> p (h a)", p=HB)).then_inc(S["idx_in"], 16)
                gp.wait_ge(S["idx_in"], 16 * i + 16)
                gp.sem_inc(S["idx_seen"], 1)
                for h in range(2):
                    gp.indirect_dma_start(out=XR[:, h], out_offset=None, in_=h2_d,
                                          in_offset=bass.IndirectOffsetOnAxis(ap=idx[:, h:h + 1], axis=0)).then_inc(S["rows_in"], 16)
                gp.wait_ge(S["rows_in"], 32 * i + 32)
            gp.wait_ge(S["ys_zero"], 16)
            gp.wait_ge(S["out_d"], 32 * n_blocks + 16)
            gp.sem_inc(S["idx_seen"], 1)
            gp.wait_ge(S["w_used"], SLOTS * n_blocks)
            gp.sem_inc(S["idx_seen"], 1)
            for t in range(NT):
                if t >= 4:
                    gp.wait_ge(S["comb_used"], t - 3)
                for k in range(2):
                    gp.indirect_dma_start(out=YA[:, t % 4, k], out_offset=None, in_=ys_d,
                                          in_offset=bass.IndirectOffsetOnAxis(ap=lst[:, k, t:t + 1], axis=0)).then_inc(S[f"comb_in{t % 4}"], 16)


        @block.scalar
        def _(act):
            a = nc.scalar
            lk = chained(act, S["chain_s"])
            act.dma_start(wsrow, w_sp[0].rearrange("h i j -> i h j")).then_inc(S["ld_mlp"], 16)
            act.dma_start(wr[:, :, :], w_router.rearrange("(k p) n -> p k n", p=P)).then_inc(S["ld_mlp"], 16)
            act.dma_start(brt[:, :], b_router.partition_broadcast(P)).then_inc(S["ld_mlp"], 16)

            def x_sumsq(t):
                act.wait_ge(S[f"ld_x{t % 4}"], 16 * (t // 4 + 1))
                lk(a.activation(junk_x, xin[t % 4], ACT.Square, accum_out=st[:, 0, t:t + 1]))
                a.activation(st[:, 1, t:t + 1], st[:, 0, t:t + 1], ACT.Sqrt, scale=1.0 / D, bias=eps[:, 0:1]).then_inc(S["sq_done"], 1)

            def modulation_rows(c):
                act.wait_ge(S["ring_used"], place["ada", c] + 1)
                if c:
                    act.wait_ge(S["ada_ps"], c)
                a.copy(arows, ada_bank(c)[0:NC, :]).then_inc(S["ada_rows"], 1)
            act.wait_ge(S["cols_t"], 1)
            a.activation(cT[:, :, :], B[0][:, 128:200].rearrange("p (j k) -> p j k", k=KD), ACT.Silu).then_inc(S["cond_done"], 1)
            a.copy(vecT[:, :], B[0][:, 0:68]).then_inc(S["cond_done"], 1)
            for t in range(4):
                act.dma_start(xin[t], x_tile(t)).then_inc(S[f"ld_x{t}"], 16)
            act.wait_ge(S["ws_t"], 1)
            a.copy(wT[:, :, :], B[3][:, :].rearrange("p (h i) -> p h i", h=GH)).then_inc(S["ws_done"], 1)
            act.wait_ge(S["consts"], 3)
            x_sumsq(0)
            x_sumsq(1)
            modulation_rows(0)
            x_sumsq(2)
            modulation_rows(1)
            x_sumsq(3)
            modulation_rows(2)
            act.wait_ge(S["s5_t"], 1)
            a.copy(aT[:, :, :], B[6][:, 0:32].rearrange("p (r g) -> p r g", r=2)).then_inc(S["cond_t"], 1)
            a.copy(h0[:, :, :, :], B[6][:, 128:384].rearrange("p (r b g) -> p r b g", r=2, b=DB)).then_inc(S["cond_t"], 1)
            a.copy(cc, B[7][:, :].rearrange("p (r g q) -> p r g q", r=2, g=PR)).then_inc(S["cond_t"], 1)
            modulation_rows(3)
            act.wait_ge(S["am_done"], 1)
            for t in range(NT):
                act.wait_ge(S["xt_ps"], t + 1)
                if t + 4 < NT:
                    act.dma_start(xin[t % 4], x_tile(t + 4)).then_inc(S[f"ld_x{t % 4}"], 16)
                if t < TP:
                    for k in range(4, KD):
                        last = a.activation(hT[:, k, P * t:P * t + P], B[2 * (t % 2) + k // 4][:, P * (k % 4):P * (k % 4) + P],
                                            ACT.Identity, scale=Am[:, k, 0:1], bias=modT[:, k, 0:1])
                    last.then_inc(S["ht_sb_s"], 1)
                if 1 <= t and t + 3 < NT:
                    x_sumsq(t + 3)
            act.wait_ge(S["ld_s5"], 16 * 8)
            a.activation(q[:, 1], q[:, 0], ACT.Exp).then_inc(S["dt_in"], 1)
            act.wait_ge(S["mg_in"], 1)
            a.activation(q[:, 4], q[:, 2], ACT.Exp).then_inc(S["dt_in"], 1)
            a.activation(q[:, 5], q[:, 2], ACT.Exp, scale=float(L)).then_inc(S["dt_in"], 1)
            act.wait_ge(S["ang_in"], 1)
            a.activation(q[:, 8], q[:, 6], ACT.Sin).then_inc(S["cs_in"], 1)
            a.activation(q[:, 9], q[:, 7], ACT.Sin).then_inc(S["cs_in"], 1)
            for n in range(12):
                j, tb = divmod(n, 3)
                act.wait_ge(S["ub_ps"], n + 1)
                if tb == 0 and j >= 2:
                    act.wait_ge(S[f"ub_out{j % 2}"], 16 * (j // 2))
                a.copy(ubT[:, j % 2, :, 48 * tb:48 * tb + 48],
                       B[4 + n % 4][:, 0:384].rearrange("p (c s) -> p s c", s=L)).then_inc(S["ub_sb"], 1)
                if tb == 2:
                    act.wait_ge(S["ub_sb"], n + 1)
                    act.dma_start(ub_d[P * j:P * j + P], ubT[:, j % 2]).then_inc(S[f"ub_out{j % 2}"], 16)
            for n in range(SG // 8):
                act.wait_ge(S["kt_ps"], n + 1)
                for o in range(2):
                    last = a.copy(KT[:, 8 * n + o:8 * n + 8:2], B[4 + 2 * (n % 2) + o][0:SQ, :].rearrange("p (g m) -> p g m", g=4))
                last.then_inc(S["kt_sb"], 1)
            act.wait_ge(S["kt_done"], 1)
            act.wait_ge(S["zeroed"], 1)
            for s in range(L):
                act.dma_start(MT[SQ * s:SQ * s + SQ, :, SQ * s:P], KT[:, :, 0:P - SQ * s]).then_inc(S["mt_placed"], 16)
            act.wait_ge(S["mt_placed"], 16 * L)
            act.wait_ge(S["ub_out0"], 16 * KG // 2)
            act.wait_ge(S["ub_out1"], 16 * KG // 2)
            for s in range(L):
                act.dma_start(U[SQ * s:SQ * s + SQ], ub_d[:, s].rearrange("(g q) c -> q g c", q=SQ)).then_inc(S["u_in"], 16)
            act.dma_start(vgain, v_gain[0].partition_broadcast(P)).then_inc(S["ld_gain"], 16)
            act.dma_start(bsp, b_sp[0].partition_broadcast(P)).then_inc(S["ld_gain"], 16)
            for t in range(NT):
                act.wait_ge(S["v_ps"], t + 1)
                a.activation(vn[:, t], B[4 + (12 + t) % 4][:, :], ACT.Gelu_apprx_tanh).then_inc(S["v_gelu"], 1)
            act.wait_ge(S["stats_v"], NT)
            a.activation(st[:, 2], st[:, 3], ACT.Sqrt, bias=eps[:, 0:1]).then_inc(S["std_v"], 1)
            act.wait_ge(S["list_zero"], 16)
            for n in range(12):
                j, tb = divmod(n, 3)
                act.wait_ge(S["uu_ps"], n + 1)
                a.activation(uT[:, j, 384 * tb:384 * tb + 384], B[4 + (21 + n) % 4][:, 0:384], ACT.Gelu_apprx_tanh).then_inc(S["u_sb"], 1)
            act.wait_ge(S["uu_ps"], 12)
            act.wait_ge(S["e_done"], 1)
            for r in range(2):
                a.copy(H[:, r, :, 0:SS], EH[:, r]).then_inc(S["e_out"], 1)
            act.wait_ge(S["e_out"], 3)
            for s in range(PR // SB):
                act.wait_ge(S["g_ps"], s + 1)
                if s:
                    act.wait_ge(S["v5_ps"], s)
                a.copy(gt, B[2 + s % 2][:, :].rearrange("p (r g m) -> p r g m", r=2, g=SB)).then_inc(S["g_sb"], 1)
                modulation_rows(4 + s)
            act.wait_ge(S["ws_zero"], 1)
            act.wait_ge(S["ws_done"], 2)
            for b in range(DB):
                act.dma_start(wS[DS * b:DS * b + DS, :, DS * b:DS * b + DS], wT[0:DS, :, 0:DS]).then_inc(S["wdiag"], 16)
            for n in range(6):
                act.wait_ge(S["y_ps"], n + 1)
                m = min(3, PR - 3 * n)
                for o in range(2):
                    last = a.activation(Y[:, 6 * n + o:6 * n + 2 * m:2], B[4 + 2 * (n % 2) + o][:, 0:m * CH].rearrange("p (g c) -> p g c", g=m),
                                        ACT.Gelu_apprx_tanh)
                last.then_inc(S["y_sb"], 1)
            act.wait_ge(S["y_sb"], 6)
            for s in range(L):
                act.dma_start(y_d[:, s].rearrange("(g q) c -> q g c", q=SQ), Y[SQ * s:SQ * s + SQ]).then_inc(S["y_out"], 16)
            act.wait_ge(S["y_out"], 16 * L)
            act.dma_start(yT, y_d.rearrange("(j p) s c -> p j (s c)", p=P)).then_inc(S["y_in"], 16)
            act.wait_ge(S["fs_t"], 1)
            a.copy(fsr, B[2][:, :].rearrange("p (r m) -> p r m", r=4)).then_inc(S["fs_sb"], 1)
            act.wait_ge(S["fs_sb"], 1)
            for r, (o_p, o_s) in enumerate(((sp_re, ss_re), (sp_im, ss_im))):
                act.dma_start(o_s[0].rearrange("b (g a) p -> (b g) (a p)", a=2), fsr[:, r]).then_inc(S["fs_out"], 16)
                act.dma_start(o_p[0, 0].rearrange("(g a) p -> g (a p)", a=2), fsr[0:PR, 2 + r]).then_inc(S["fs_out"], 16)
            act.wait_ge(S["v_done"], 1)
            act.dma_start(v_new[0].rearrange("b s d -> (b s) d"), vn[:, NT - 1]).then_inc(S["v_out"], 16)
            act.wait_ge(S["mix_ps"], NT)
            act.wait_ge(S["mod_all"], 1)

            def widen(dst, src, first):
                a.copy(dst.rearrange("p (k b s) -> p k b s", k=KD, b=DB),
                       src[:, first:first + KD, 1:NC].unsqueeze(3).to_broadcast([P, KD, DB, DS])).then_inc(S["wide_in"], 1)
            for n, (src, first) in ((1, (Af, 0)), (3, (modT, 24)), (5, (modT, 16))):
                widen(bc[:, n], src, first)
            for n in range(6):
                act.wait_ge(S["bc_ps"], n + 1)
                for h in range(2):
                    last = a.copy(bc[:, n, 512 * h:512 * h + 512], B[2 * (n % 2) + h][:, :])
                last.then_inc(S["bc_sb"], 1)
            for n in range(16):
                j = n // 4
                act.wait_ge(S["glu_ps"], n + 1)
                if n >= 2:
                    act.wait_ge(S["b_done"], n - 1)
                a.activation(ytm[:, n % 2], B[4 + n % 4][:, 0:288], ACT.Sigmoid, bias=vecT[:, 64 + j:65 + j]).then_inc(S["sig_sb"], 1)
            act.wait_ge(S["b_done"], 16)
            act.dma_start(X1[:, 0:TP], x_prompt[0].rearrange("(t p) d -> p t d", p=P)).then_inc(S["ld_xres"], 16)
            act.dma_start(X1[:, TP], xs_rows).then_inc(S["ld_xres"], 16)
            act.wait_ge(S["fs_out"], 64)
            widen(gfb[:, 1], modT, 40)
            for n in range(6, 8):
                act.wait_ge(S["bc_ps"], n + 1)
                for h in range(2):
                    last = a.copy(gfb[:, n - 6, 512 * h:512 * h + 512], B[2 * (n % 2) + h][:, :])
                last.then_inc(S["bc_sb"], 1)

            def h2_columns(t):
                act.wait_ge(S["h2t_ps"], t + 1)
                if t >= 2:
                    act.wait_ge(S["lg_ps"], t - 1)
                for h in range(2):
                    last = a.copy(h2T[:, t % 2, 4 * h:4 * h + 4], B[h][:, :].rearrange("p (k m) -> p k m", k=4))
                last.then_inc(S["h2t_sb"], 1)
                act.dma_start(h2_d[P * t:P * t + P], h2r[:, t % 2]).then_inc(S[f"h2_out{t % 2}"], 16)

            for t in range(NT):
                act.wait_ge(S["x1_done"], t + 1)
                lk(a.activation(junk_h, X1[:, t], ACT.Square, accum_out=st[:, 0, t:t + 1]))
                a.activation(st[:, 1, t:t + 1], st[:, 0, t:t + 1], ACT.Sqrt, scale=1.0 / D, bias=eps[:, 0:1]).then_inc(S["ss_done"], 1)
                if t:
                    h2_columns(t - 1)
            h2_columns(NT - 1)
            act.dma_start(gfin, g_final.partition_broadcast(P)).then_inc(S["ld_gates"], 16)
            act.wait_ge(S["e_in"], 1)
            a.activation(rt[:, 1], rt[:, 0], ACT.Exp).then_inc(S["exp_done"], 1)
            def high_parts(i, *slots):
                for n in slots:
                    act.wait_ge(LDS[n], 16 * i + 16)
                    a.copy(w_hi[n], w_raw[n]).then_inc(S["hi_done"], 1)
            act.wait_ge(S["h2_out0"], 16 * 5)
            act.wait_ge(S["h2_out1"], 16 * 4)
            high_parts(0, *range(8))
            act.wait_ge(S["tab_done"], 1)
            n_blocks = act.value_load(nblk[0:1, 0:1], min_val=NE, max_val=NE + EXTRA)
            last_block = act.value_load(nblk[0:1, 1:2], min_val=NE - 1, max_val=NE + EXTRA - 1)

            def rows_to_columns(i, h):
                act.wait_ge(S["xt2_ps"], 2 * i + h + 1)
                for m in range(2):
                    last = a.copy(x_hl[:, 4 * m:4 * m + 4, 0, HB * h:HB * h + HB],
                                  B[2 * h + m][:, 0:4 * HB].rearrange("p (k n) -> p k n", k=4))
                last.then_inc(S["xh_done"], 1)

            def block_on_act(i, more):
                for f in range(KE):
                    here = (i, 8 + 2 * f) if f < 2 else (i + 1, 2 * f - 4)
                    split = f < 2 or more
                    if split:
                        high_parts(here[0], here[1])
                    act.wait_ge(S["gate_done"], KE * i + f + 1)
                    a.activation(sil[:, f % 2], gate[:, f % 2], ACT.Silu).then_inc(S["silu_done"], 1)
                    if split:
                        high_parts(here[0], here[1] + 1)
                if more:
                    high_parts(i + 1, 4)
                    rows_to_columns(i + 1, 0)
                    rows_to_columns(i + 1, 1)
                    high_parts(i + 1, 5, 6, 7)
                for h in range(2):
                    act.wait_ge(S["out_sb"], 2 * i + h + 2)
                    act.dma_start(ys_d[bass.ds(i * BN + HB * h, HB)], OUT[:, h]).then_inc(S["out_d"], 16)
            for h in range(2):
                rows_to_columns(0, h)
            with act.Fori(0, last_block) as i:
                block_on_act(i, True)
            block_on_act(last_block, False)
            def first_choice(t):
                act.wait_ge(S[f"comb_in{t % 4}"], 32 * (t // 4) + 32)
                a.activation(YA[:, t % 4, 0], YA[:, t % 4, 0], ACT.Copy, scale=gates[:, 0, t:t + 1]).then_inc(S["comb_scaled"], 1)
            first_choice(0)
            first_choice(1)
            for t in range(NT):
                act.wait_ge(S["fin_ss"], t + 1)
                lk(a.activation(junk_h, X1[:, t], ACT.Square, accum_out=st[:, 0, t:t + 1]))
                a.activation(st[:, 1, t:t + 1], st[:, 0, t:t + 1], ACT.Sqrt, scale=1.0 / D, bias=eps[:, 0:1]).then_inc(S["fin_rs"], 1)
                if t + 2 < NT:
                    first_choice(t + 2)

        @block.tensor
        def _(pe):
            T = nc.tensor
            pe.wait_ge(S["consts"], 1)
            pe.wait_ge(S["ld_vec"], 16 * 6)
            T.transpose(B[0][:, 0:68], rows[0:68, 1], ident[0:68, 0:68])
            T.transpose(B[0][:, 128:200], rows[0:72, 0], ident[0:72, 0:72]).then_inc(S["cols_t"], 1)
            pe.wait_ge(S["ld_mlp"], 16 * 3)
            for h in range(GH):
                last = T.transpose(B[3][:, P * h:P * h + P], wsrow[:, h], ident[:, :])
            last.then_inc(S["ws_t"], 1)
            def modulation(c):
                w = arrived(pe, ("ada", c))
                if c >= 2:
                    pe.wait_ge(S["ada_sb"], c - 1)
                for k in range(KD):
                    last = T.matmul(ada_bank(c)[0:NC, :], cT[:, :, k], w[:, k], start=(k == 0), stop=(k == KD - 1))
                last.then_inc(S["ring_used"], 1)

            def modulation_turned(c):
                pe.wait_ge(S["ada_rows"], c + 1)
                for j in range(4):
                    last = T.transpose(ada_bank(c)[:, NC * j:NC * j + NC], arows[:, P * j:P * j + P], ident[0:NC, 0:NC])
                last.then_inc(S["ada_ps"], 1)

            def turned(x, t, banks):
                for k in range(KD):
                    last = T.transpose(B[banks + k // 4][:, P * (k % 4):P * (k % 4) + P], x[:, P * k:P * k + P], ident[:, :])
                return last

            def x_turned(t):
                pe.wait_ge(S["x_norm"], t + 1)
                if t >= 2:
                    pe.wait_ge(S["ht_sb_v"], t - 1)
                    pe.wait_ge(S["ht_sb_s"], t - 1)
                turned(xin[t % 4], t, 2 * (t % 2)).then_inc(S["xt_ps"], 1)

            pe.wait_ge(S["cond_done"], 2)
            pe.wait_ge(S["ws_done"], 1)
            modulation(0)
            x_turned(0)
            modulation(1)
            modulation_turned(0)
            x_turned(1)
            modulation(2)
            modulation_turned(1)
            pe.wait_ge(S["ld_s5"], 16 * 8)
            pe.wait_ge(S["ld_c"], 16 * 32)
            for r in range(2):
                T.transpose(B[6][:, PR * r:PR * r + PR], arow[0:PR, r], ident[0:PR, 0:PR])
                T.transpose(B[6][:, P + P * r:2 * P + P * r], srow[:, r], ident[:, :])
            for n in range(4):
                last = T.transpose(B[7][:, P * n:P * n + P], crow[:, n], ident[:, :])
            last.then_inc(S["s5_t"], 1)
            modulation(3)
            modulation_turned(2)
            modulation_turned(3)
            for t in range(2, NT):
                x_turned(t)
            pe.wait_ge(S["ada_sb"], 4)
            pe.wait_ge(S["cond_t"], 3)
            w = arrived(pe, ("in", 2))
            for n in range(12):
                j, tb = divmod(n, 3)
                if n < 3:
                    pe.wait_ge(S["ht_sb_v"], 3 * (n + 1))
                    pe.wait_ge(S["ht_sb_s"], min(TP, 3 * (n + 1)))
                if n >= 4:
                    pe.wait_ge(S["ub_sb"], n - 3)
                for k in range(KD):
                    last = T.matmul(B[4 + n % 4][:, 0:384], w[:, k, P * j:P * j + P], hT[:, k, 384 * tb:384 * tb + 384],
                                    start=(k == 0), stop=(k == KD - 1))
                last.then_inc(S["ub_ps"], 1)
            pe.wait_ge(S["ub_ps"], 12)
            pe.sem_inc(S["ring_used"], 1)
            pe.wait_ge(S["ub_sb"], 12)
            pe.wait_ge(S["w_table"], 1)
            for g in range(SG):
                n, gp, lo = g // 8, g // 2, SS * (g % 2)
                if g % 8 == 0 and n >= 2:
                    pe.wait_ge(S["kt_sb"], n - 1)
                for r in range(2):
                    last = T.matmul(B[4 + 2 * (n % 2) + g % 2][0:SQ, P * (gp % 4):P * (gp % 4) + P], bb[lo:lo + SS, r, gp, :],
                                    W[lo:lo + SS, r, gp, 0:L, :], start=(r == 0), stop=(r == 1))
                if g % 8 == 7:
                    last.then_inc(S["kt_ps"], 1)
            w = arrived(pe, ("in", 1))
            pe.wait_ge(S["kt_sb"], SG // 8)
            for t in range(NT):
                if t >= 4:
                    pe.wait_ge(S["v_gelu"], t - 3)
                for k in range(KD):
                    last = T.matmul(B[4 + (12 + t) % 4][:, :], hT[:, k, P * t:P * t + P], w[:, k], start=(k == 0), stop=(k == KD - 1))
                last.then_inc(S["v_ps"], 1)
            pe.wait_ge(S["v_ps"], NT)
            pe.sem_inc(S["ring_used"], 1)
            w = arrived(pe, ("in", 0))
            for n in range(12):
                j, tb = divmod(n, 3)
                pe.wait_ge(S["v_gelu"], min(NT, 6 + n))
                if n >= 4:
                    pe.wait_ge(S["u_sb"], n - 3)
                for k in range(KD):
                    last = T.matmul(B[4 + (21 + n) % 4][:, 0:384], w[:, k, P * j:P * j + P], hT[:, k, 384 * tb:384 * tb + 384],
                                    start=(k == 0), stop=(k == KD - 1))
                last.then_inc(S["uu_ps"], 1)
            pe.wait_ge(S["uu_ps"], 12)
            pe.sem_inc(S["ring_used"], 1)
            pe.wait_ge(S["u_in"], 16 * L)
            pe.wait_ge(S["u_sb"], 12)

            def g_turned(s):
                pe.wait_ge(S["g_nat"], s + 1)
                if s >= 2:
                    pe.wait_ge(S["g_sb"], s - 1)
                for r in range(2):
                    for i in range(SB):
                        last = T.transpose(B[2 + s % 2][:, P * (SB * r + i):P * (SB * r + i) + P],
                                           gnat[:, r, i].rearrange("p l q -> p (l q)"), ident[:, :])
                last.then_inc(S["g_ps"], 1)
            g_turned(0)
            for s in range(PR // SB):
                pe.wait_ge(S["g_sb"], s + 1)
                if s >= 2:
                    pe.wait_ge(S["v5_used"], s - 1)
                for r in range(2):
                    for i in range(SB):
                        for lo in (0, SS):
                            last = T.matmul(B[4 + 2 * (s % 2) + r][lo:lo + SS, CH * i:CH * i + CH], gt[:, r, i, lo:lo + SS],
                                            U[:, 2 * (SB * s + i) + lo // SS], start=True, stop=True)
                last.then_inc(S["v5_ps"], 1)
                if s + 1 < PR // SB:
                    g_turned(s + 1)
                modulation(4 + s)
                if s:
                    modulation_turned(3 + s)
            modulation_turned(11)
            def mix(t):
                if t >= 2:
                    pe.wait_ge(S["mix_sb"], t - 1)
                for h in range(GH):
                    last = T.matmul(B[t % 2][:, P * h:P * h + P], vn[:, t, P * h:P * h + P], (wT if t < TP else wS)[:, h],
                                    start=True, stop=True)
                last.then_inc(S["mix_ps"], 1)
            pe.wait_ge(S["v5_used"], PR // SB)
            pe.wait_ge(S["mt_placed"], 16 * L)
            pe.wait_ge(S["v_done"], 1)
            pe.wait_ge(S["ws_done"], 2)
            pe.wait_ge(S["ada_sb"], 12)
            mix(0)
            mix(1)
            pe.wait_ge(S["h_done"], 1)
            for g in range(SG):
                n, gp, lo = g // 6, g // 2, SS * (g % 2)
                if g % 6 == 0 and n >= 2:
                    pe.wait_ge(S["y_sb"], n - 1)
                o = B[4 + 2 * (n % 2) + g % 2][:, CH * (gp % 3):CH * (gp % 3) + CH]
                T.matmul(o, MT[:, g], U[:, g], start=True, stop=False)
                for r in range(2):
                    last = T.matmul(o, W[lo:lo + SS, r, gp, 1:L + 1, :], H[lo:lo + SS, r, gp], start=False, stop=(r == 1))
                if g % 6 == 5 or g == SG - 1:
                    last.then_inc(S["y_ps"], 1)
                    mix(n + 2)
            pe.wait_ge(S["wdiag"], 16 * DB)
            mix(TP)
            pe.wait_ge(S["g_sb"], PR // SB)
            for r in range(2):
                T.transpose(B[2][:, P * r:P * r + P], fs[:, r, 1:NC].rearrange("p b g -> p (b g)"), ident[:, :])
            for r in range(2):
                last = T.transpose(B[2][0:PR, P * (2 + r):P * (2 + r) + P], fs[:, r, 0], ident[:, :])
            last.then_inc(S["fs_t"], 1)
            pe.wait_ge(S["mix_sb"], NT)
            pe.wait_ge(S["mod_all"], 1)

            def spread(n, src, first, own):
                if n >= 2:
                    pe.wait_ge(S["bc_sb"], n - 1)
                if n % 2:
                    pe.wait_ge(S["wide_in"], n // 2 + 1)
                for k in range(KD):
                    col = src[:, first + k]
                    wide = col[:, 0:1].to_broadcast([P, P]) if n % 2 == 0 else own[:, P * k:P * k + P]
                    last = T.transpose(B[2 * (n % 2) + k // 4][:, P * (k % 4):P * (k % 4) + P], wide, ident[:, :])
                last.then_inc(S["bc_ps"], 1)
            pe.wait_ge(S["fs_sb"], 1)
            for n, (src, first) in enumerate(((Af, 0), (Af, 0), (modT, 24), (modT, 24), (modT, 16), (modT, 16))):
                spread(n, src, first, bc[:, n])
            w = arrived(pe, ("glu", 0))
            pe.wait_ge(S["y_sb"], 6)
            pe.wait_ge(S["y_in"], 16)
            for n in range(16):
                j, tb = divmod(n, 4)
                if n >= 4:
                    pe.wait_ge(S["sig_sb"], n - 3)
                for k in range(KG):
                    last = T.matmul(B[4 + n % 4][:, 0:288], w[:, k, P * j:P * j + P], yT[:, k, 288 * tb:288 * tb + 288],
                                    start=(k == 0), stop=(k == KG - 1))
                last.then_inc(S["glu_ps"], 1)
            pe.wait_ge(S["glu_ps"], 16)
            pe.sem_inc(S["ring_used"], 1)
            pe.wait_ge(S["bc_sb"], 6)
            w2 = [arrived(pe, ("out", 0)), arrived(pe, ("out", 1))]
            pe.wait_ge(S["b_done"], 16)
            pe.wait_ge(S["sig_sb"], 16)

            def h2_turn(t):
                pe.wait_ge(S["h2_rows"], t + 1)
                if t:
                    pe.wait_ge(S["h2t_sb"], t)
                turned(h2r[:, t % 2], t, 0).then_inc(S["h2t_ps"], 1)

            def router(t):
                pe.wait_ge(S["h2t_sb"], t + 1)
                for k in range(KD):
                    last = T.matmul(B[2][:, NE * t:NE * t + NE], h2T[:, t % 2, k], wr[:, k], start=(k == 0), stop=(k == KD - 1))
                last.then_inc(S["lg_ps"], 1)

            for t in range(NT):
                for h in range(2):
                    n = 2 * t + h
                    if n >= 4:
                        pe.wait_ge(S["wo_used"], n - 3)
                    for k in range(KD):
                        m = (uT if k < KG else bT)[:, k % KG, P * t:P * t + P]
                        last = T.matmul(B[4 + n % 4][:, :], m, w2[h][:, k], start=(k == 0), stop=(k == KD - 1))
                    last.then_inc(S["wo_ps"], 1)
                if t == 0:
                    for n in (6, 7):
                        spread(n, modT, 40, gfb[:, 1])
                    pe.wait_ge(S["bc_sb"], 8)
                if t >= 1:
                    h2_turn(t - 1)
                if t >= 2:
                    router(t - 2)
            pe.wait_ge(S["wo_ps"], 2 * NT)
            pe.sem_inc(S["ring_used"], 1)
            pe.sem_inc(S["ring_used"], 1)
            router(NT - 2)
            h2_turn(NT - 1)
            router(NT - 1)
            pe.wait_ge(S["consts"], 3)
            pe.wait_ge(S["oh_done"], 1)
            oh = ohb[:, :, :].rearrange("p t e -> p (t e)")
            T.matmul(B[3][:, 0:NT * NE], tri[:, :], oh, start=True, stop=False)
            for d in range(1, NT):
                T.matmul(B[3][:, NE * d:NT * NE], ones[:, :], oh[:, 0:(NT - d) * NE], start=False, stop=(d == NT - 1))
            for t in range(NT):
                last = T.matmul(B[2][:, 256:256 + NE], ones[:, :], oh[:, NE * t:NE * t + NE], start=(t == 0), stop=(t == NT - 1))
            last.then_inc(S["pre_ps"], 1)
            pe.wait_ge(S["tab_done"], 1)
            n_blocks = pe.value_load(nblk[0:1, 0:1], min_val=NE, max_val=NE + EXTRA)
            last_block = pe.value_load(nblk[0:1, 1:2], min_val=NE - 1, max_val=NE + EXTRA - 1)

            def turn_rows(i):
                pe.wait_ge(S["rows_in"], 32 * i + 32)
                for h in range(2):
                    for k in range(KD):
                        last = T.transpose(B[2 * h + k // 4][:, HB * (k % 4):HB * (k % 4) + HB], XR[:, h, P * k:P * k + P],
                                           ident[0:HB, 0:HB])
                    last.then_inc(S["xt2_ps"], 1)
            turn_rows(0)
            pe.wait_ge(S["xt2_ps"], 2)
            pe.sem_inc(S["rows_free"], 1)

            def products(o, w_h, w_l, k, first, last):
                T.matmul(o[:, 0:2 * BN], w_h, x_hl[:, k].rearrange("p r n -> p (r n)"), start=first, stop=False)
                return T.matmul(o[:, 0:BN], w_l, x_hl[:, k, 0], start=False, stop=last)

            def block_on_pe(i, more):
                pe.wait_ge(S["xt2_sb"], 2 * i + 2)
                for f in range(KE):
                    for m, (bank, name) in enumerate(((f % 2, "gate_ps"), (2 + f % 2, "up_ps"))):
                        n = 2 * f + m
                        pe.wait_ge(S["lo_done"], SLOTS * i + n + 1)
                        if m == 0:
                            pe.wait_ge(S["he_done"], KE * i + (f if f >= 2 else 1))
                        for k in range(KD):
                            last = products(B[bank], w_hi[n][:, P * k:P * k + P], w_lo[n][:, P * k:P * k + P], k, k == 0, k == KD - 1)
                        last.then_inc(S["w_used"], 1)
                pe.wait_ge(S["out_sb"], 2 * i + 1)
                for f in range(KE):
                    pe.wait_ge(S["lo_done"], SLOTS * i + 8 + f + 1)
                    pe.wait_ge(S["he_done"], KE * i + f + 2)
                    for h in range(2):
                        rows_h, rows_l = (he_hl[:, r, f, HB * h:HB * h + P] for r in range(2))
                        for n in range(2):
                            o = B[4 + 2 * h + n][:, :]
                            w_h, w_l = w_hi[8 + f][:, 512 * n:512 * n + 512], w_lo[8 + f][:, 512 * n:512 * n + 512]
                            T.matmul(o, rows_h, w_h, start=(f == 0), stop=False)
                            T.matmul(o, rows_h, w_l, start=False, stop=False)
                            last = T.matmul(o, rows_l, w_h, start=False, stop=(f == KE - 1))
                            if f == KE - 1 and not (h == 1 and n == 1):
                                last.then_inc(S["down_ps"], 1)
                    last.then_inc(S["w_used"], 1)
                    if f == 0 and more:
                        pe.wait_ge(S["he_done"], KE * i + KE + 1)
                        turn_rows(i + 1)
                    if f == 1 and more:
                        pe.wait_ge(S["xt2_ps"], 2 * i + 4)
                        pe.sem_inc(S["rows_free"], 1)
            with pe.Fori(0, last_block) as i:
                block_on_pe(i, True)
            block_on_pe(last_block, False)

        @block.vector
        def _(dve):
            v = nc.vector
            lk = chained(dve, S["chain_v"])

            def tt(o, a, b, op):
                return v.tensor_tensor(o, a, b, op)

            dve.wait_ge(S["ws_done"], 1)
            v.memset(wT[64:P, :, 0:64], 0.0).then_inc(S["ws_done"], 1)
            def cmul(o, x, y, t):
                lk(tt(t[0], x[0], y[0], ALU.mult))
                lk(tt(t[1], x[1], y[1], ALU.mult))
                lk(tt(o[0], t[0], t[1], ALU.subtract))
                lk(tt(t[0], x[0], y[1], ALU.mult))
                lk(tt(t[1], x[1], y[0], ALU.mult))
                lk(tt(o[1], t[0], t[1], ALU.add))

            def modulation(c):
                dve.wait_ge(S["ada_ps"], c + 1)
                tt(modT[:, 4 * c:4 * c + 4], ada_bank(c)[:, 0:4 * NC].rearrange("p (j c) -> p j c", j=4),
                   vecT[:, 4 * c:4 * c + 4].unsqueeze(2).to_broadcast([P, 4, NC]), ALU.add).then_inc(S["ada_sb"], 1)

            def x_normalised(t):
                dve.wait_ge(S["sq_done"], t + 1)
                lk(v.reciprocal(st[:, 4, t:t + 1], st[:, 1, t:t + 1]))
                v.tensor_scalar(xin[t % 4], xin[t % 4], st[:, 4, t:t + 1], None, ALU.mult).then_inc(S["x_norm"], 1)
            x_normalised(0)
            x_normalised(1)
            for c in range(4):
                modulation(c)
                if c < 2:
                    x_normalised(c + 2)
            dve.wait_ge(S["ada_sb"], 4)
            v.scalar_tensor_tensor(out=Am[:, :, :], in0=modT[:, 8:16], scalar=1.0,
                                   in1=vecT[:, 48:56].unsqueeze(2).to_broadcast([P, KD, NC]),
                                   op0=ALU.add, op1=ALU.mult).then_inc(S["am_done"], 1)
            for t in range(NT):
                dve.wait_ge(S["xt_ps"], t + 1)
                dve.wait_ge(S["am_done"], 1)
                if t < TP:
                    for k in range(4):
                        last = v.tensor_scalar(hT[:, k, P * t:P * t + P], B[2 * (t % 2) + k // 4][:, P * (k % 4):P * (k % 4) + P],
                                               Am[:, k, 0:1], modT[:, k, 0:1], ALU.mult, ALU.add)
                else:
                    for k in range(KD):
                        src = B[2 * (t % 2) + k // 4][:, P * (k % 4):P * (k % 4) + P].rearrange("p (b s) -> p b s", b=DB)
                        o = hT[:, k, P * t:P * t + P].rearrange("p (b s) -> p b s", b=DB)
                        lk(tt(o, src, Am[:, k, 1:NC].unsqueeze(2).to_broadcast([P, DB, DS]), ALU.mult))
                        last = tt(o, o, modT[:, k, 1:NC].unsqueeze(2).to_broadcast([P, DB, DS]), ALU.add)
                last.then_inc(S["ht_sb_v"], 1)
                if 1 <= t and t + 3 < NT:
                    x_normalised(t + 3)
            dve.wait_ge(S["cond_t"], 3)
            dve.wait_ge(S["dt_in"], 1)
            tt(q[:, 2], aT[:, 0], q[:, 1], ALU.mult).then_inc(S["mg_in"], 1)
            lk(tt(q[:, 3], aT[:, 1], q[:, 1], ALU.mult))
            lk(v.tensor_scalar(q[:, 10], q[:, 3], 1.0 / (2 * PI), None, ALU.mult))
            lk(v.tensor_copy(qi[:, :], q[:, 10]))
            lk(v.tensor_copy(q[:, 10], qi[:, :]))
            for part in (TWO_PI_HI, TWO_PI_MID, TWO_PI_LO):
                lk(v.scalar_tensor_tensor(out=q[:, 3], in0=q[:, 10], scalar=-part, in1=q[:, 3], op0=ALU.mult, op1=ALU.add))

            def wrap(x):
                for op, lim, add in ((ALU.is_gt, PI, -2 * PI), (ALU.is_lt, -PI, 2 * PI)):
                    lk(v.tensor_scalar(q[:, 10], x, lim, add, op, ALU.mult))
                    lk(tt(x, x, q[:, 10], ALU.add))
            wrap(q[:, 3])
            lk(v.tensor_scalar(q[:, 7], q[:, 3], PI / 2, None, ALU.add))
            wrap(q[:, 7])
            lk(v.tensor_scalar(q[:, 7], q[:, 7], 3.1415925, -3.1415925, ALU.min, ALU.max))
            v.tensor_scalar(q[:, 6], q[:, 3], 3.1415925, -3.1415925, ALU.min, ALU.max).then_inc(S["ang_in"], 1)

            dve.wait_ge(S["cs_in"], 2)
            dve.wait_ge(S["dt_in"], 3)
            lk(v.memset(LP[:, 0, :, 0], 1.0))
            lk(v.memset(LP[:, 1, :, 0], 0.0))
            lk(tt(LP[:, 0, :, 1], q[:, 4], q[:, 9], ALU.mult))
            lk(tt(LP[:, 1, :, 1], q[:, 4], q[:, 8], ALU.mult))
            n = 1
            while n < L:
                x = (LP[:, 0, :, 1:n + 1], LP[:, 1, :, 1:n + 1])
                y = tuple(LP[:, r, :, n:n + 1].to_broadcast([P, PR, n]) for r in range(2))
                o = (LP[:, 0, :, n + 1:2 * n + 1], LP[:, 1, :, n + 1:2 * n + 1])
                t = tuple(wtmp2[:, :, r, 0:n] for r in range(2))
                cmul(o, x, y, t)
                n *= 2
            for r in range(2):
                for s in range(L):
                    lk(v.tensor_copy(LR[:, r, :, s], LP[:, r, :, L - 1 - s]))
            lk(v.tensor_copy(q[:, 11], q[:, 9]))
            lk(v.tensor_copy(q[:, 12], q[:, 8]))

            def square(c, s, t0, t1):
                lk(tt(t0, c, c, ALU.mult))
                lk(tt(t1, s, s, ALU.mult))
                lk(v.scalar_tensor_tensor(out=s, in0=s, scalar=2.0, in1=c, op0=ALU.mult, op1=ALU.mult))
                lk(tt(c, t0, t1, ALU.subtract))
                lk(tt(t0, c, c, ALU.mult))
                lk(tt(t1, s, s, ALU.mult))
                lk(tt(t0, t0, t1, ALU.add))
                lk(v.tensor_scalar(t0, t0, -0.5, 1.5, ALU.mult, ALU.add))
                lk(tt(c, c, t0, ALU.mult))
                lk(tt(s, s, t0, ALU.mult))
            for _ in range(3):
                square(q[:, 11], q[:, 12], q[:, 13], q[:, 14])
            lk(v.tensor_scalar(q[:, 13], LP[:, 0, :, 1], -1.0, None, ALU.add))
            lk(tt(q[:, 14], aT[:, 0], aT[:, 0], ALU.mult))
            lk(tt(q[:, 15], aT[:, 1], aT[:, 1], ALU.mult))
            lk(tt(q[:, 14], q[:, 14], q[:, 15], ALU.add))
            lk(v.reciprocal(q[:, 14], q[:, 14]))
            lk(tt(q[:, 15], q[:, 13], aT[:, 0], ALU.mult))
            lk(tt(q[:, 16], LP[:, 1, :, 1], aT[:, 1], ALU.mult))
            lk(tt(q[:, 15], q[:, 15], q[:, 16], ALU.add))
            lk(tt(q[:, 15], q[:, 15], q[:, 14], ALU.mult))
            lk(tt(q[:, 16], LP[:, 1, :, 1], aT[:, 0], ALU.mult))
            lk(tt(q[:, 17], q[:, 13], aT[:, 1], ALU.mult))
            lk(tt(q[:, 16], q[:, 16], q[:, 17], ALU.subtract))
            lk(tt(q[:, 16], q[:, 16], q[:, 14], ALU.mult))
            coef = tuple(q[:, 15 + r].unsqueeze(2).to_broadcast([P, PR, SQ]) for r in range(2))
            cmul((bb[:, 0], bb[:, 1]), (bnat[:, 0], bnat[:, 1]), coef,
                 tuple(wtmp2[:, :, r, :] for r in range(2)))
            wide = [P, PR, L + 1, SQ]
            lam = tuple(LP[:, r].unsqueeze(3).to_broadcast(wide) for r in range(2))
            cx = tuple(cc[:, r].unsqueeze(2).to_broadcast(wide) for r in range(2))
            lk(tt(wtmp, lam[0], cx[0], ALU.mult))
            lk(tt(wtmp2, lam[1], cx[1], ALU.mult))
            lk(tt(W[:, 0], wtmp, wtmp2, ALU.subtract))
            lk(tt(wtmp, lam[1], cx[0], ALU.mult))
            lk(tt(wtmp2, lam[0], cx[1], ALU.mult))
            v.scalar_tensor_tensor(out=W[:, 1], in0=wtmp, scalar=-1.0, in1=wtmp2, op0=ALU.mult,
                                   op1=ALU.subtract).then_inc(S["w_table"], 1)

            dve.wait_ge(S["kt_sb"], 4)
            dve.wait_ge(S["ldq"], 16)
            dd = dtmp[0:SQ]
            lk(tt(dd, ident[0:SQ, 0:SQ].unsqueeze(1).to_broadcast([SQ, SG, SQ]), dq[:, :].unsqueeze(2).to_broadcast([SQ, SG, SQ]), ALU.mult))
            tt(KT[:, :, 0:SQ], KT[:, :, 0:SQ], dd, ALU.add).then_inc(S["kt_done"], 1)
            for t in range(NT):
                dve.wait_ge(S["v_gelu"], t + 1)
                lk(v.bn_stats(bn6[:, t % 2], vn[:, t]))
                lk(v.bn_aggr(mv[:, t], bn6[:, t % 2]))
                v.tensor_copy(st[:, 3, t:t + 1], mv[:, t, 1:2]).then_inc(S["stats_v"], 1)
            dve.wait_ge(S["std_v"], 1)
            dve.wait_ge(S["ld_gain"], 32)
            lk(v.reciprocal(st[:, 5], st[:, 2]))
            for t in range(NT):
                lk(v.tensor_scalar(vn[:, t], vn[:, t], mv[:, t, 0:1], st[:, 5, t:t + 1], ALU.subtract, ALU.mult))
                last = tt(vn[:, t], vn[:, t], vgain, ALU.mult)
            last.then_inc(S["v_done"], 1)
            E = tuple(H[:, r, :, 0:P] for r in range(2))
            lk(v.memset(EH[:, 0, :, 0], 1.0))
            lk(v.memset(EH[:, 1, :, 0], 0.0))
            n = 1
            while n < P:
                u = tuple(q[:, 11 + r].unsqueeze(2).to_broadcast([P, PR, n]) for r in range(2))
                if n == SS:
                    dve.sem_inc(S["e_done"], 1)
                    dve.wait_ge(S["uu_ps"], 12)
                    t0, t1 = (area("RA", 4608 + 1024 * r, PR, n) for r in range(2))
                    out = tuple(E[r][:, :, n:2 * n] for r in range(2))
                else:
                    t0, t1 = (area("RD", 1024 * r, PR, n) for r in range(2))
                    out = tuple(EH[:, r, :, n:2 * n] for r in range(2))
                cmul(out, tuple(EH[:, r, :, 0:n] for r in range(2)), u, (t0, t1))
                if n < SS:
                    square(q[:, 11], q[:, 12], q[:, 13], q[:, 14])
                n *= 2
            dve.sem_inc(S["e_out"], 1)
            dve.wait_ge(S["e_out"], 3)
            for s in range(PR // SB):
                sl = slice(SB * s, SB * s + SB)
                Er, Ei = E[0][:, sl], E[1][:, sl]
                dve.wait_ge(S["v5_ps"], s + 1)
                Vr, Vi = (B[4 + 2 * (s % 2) + r][:, 0:SB * CH].rearrange("p (i c) -> p i c", i=SB) for r in range(2))
                lk(v.tensor_copy(H[:, 0, sl, CP:CH], Vr[:, :, CP:CH]))
                lk(v.tensor_copy(H[:, 1, sl, CP:CH], Vi[:, :, CP:CH]))
                lk(tt(tm[:, 0], Er, Vr[:, :, 0:CP], ALU.mult))
                lk(tt(tm[:, 1], Ei, Vi[:, :, 0:CP], ALU.mult))
                lk(tt(tm[:, 2], Er, Vi[:, :, 0:CP], ALU.mult))
                tt(tm[:, 3], Ei, Vr[:, :, 0:CP], ALU.mult).then_inc(S["v5_used"], 1)
                lk(tt(tm[:, 0], tm[:, 0], tm[:, 1], ALU.add))
                dve.wait_ge(S["v5_used"], s + 1)
                lk(tt(tm[:, 2], tm[:, 2], tm[:, 3], ALU.subtract))
                for i in range(SB):
                    decay = q[:, 5, SB * s + i:SB * s + i + 1].to_broadcast([P, CP])
                    lk(v.tensor_tensor_scan(tm[:, 1, i], decay, tm[:, 0, i], 0.0, ALU.mult, ALU.add))
                    lk(v.tensor_tensor_scan(tm[:, 3, i], decay, tm[:, 2, i], 0.0, ALU.mult, ALU.add))
                lk(tt(tm[:, 0], Er, tm[:, 1], ALU.mult))
                lk(tt(tm[:, 2], Ei, tm[:, 3], ALU.mult))
                lk(tt(tm[:, 4], Er, tm[:, 3], ALU.mult))
                lk(tt(tm[:, 5], Ei, tm[:, 1], ALU.mult))
                lk(tt(H[:, 0, sl, 1:CP], tm[:, 0, :, 0:CP - 1], tm[:, 2, :, 0:CP - 1], ALU.subtract))
                lk(tt(H[:, 1, sl, 1:CP], tm[:, 4, :, 0:CP - 1], tm[:, 5, :, 0:CP - 1], ALU.add))
                lk(tt(fs[:, 0, 0, sl], tm[:, 0, :, CP - 1], tm[:, 2, :, CP - 1], ALU.subtract))
                lk(tt(fs[:, 1, 0, sl], tm[:, 4, :, CP - 1], tm[:, 5, :, CP - 1], ALU.add))
                if s:
                    modulation(3 + s)
            modulation(11)
            dve.wait_ge(S["ada_sb"], 12)
            v.scalar_tensor_tensor(out=Af[:, :, :], in0=modT[:, 32:40], scalar=1.0,
                                   in1=vecT[:, 56:64].unsqueeze(2).to_broadcast([P, KD, NC]),
                                   op0=ALU.add, op1=ALU.mult).then_inc(S["mod_all"], 1)
            lk(v.memset(H[:, :, :, 0], 0.0))
            lam8 = tuple(LP[:, r, :, L:L + 1].to_broadcast([P, PR, DB]) for r in range(2))
            hs = tuple(h0[:, r].rearrange("p b g -> p g b") for r in range(2))
            mid = tuple(smp[:, r] for r in range(2))
            ts = tuple(smp[:, 2 + r] for r in range(2))
            cmul(mid, hs, lam8, ts)
            for r in range(2):
                lk(tt(mid[r], mid[r], H[:, r, :, CP:CH:2], ALU.add))
            out = tuple(smp[:, 4 + r] for r in range(2))
            cmul(out, mid, lam8, ts)
            for r in range(2):
                lk(tt(fs[:, r, 1:NC].rearrange("p b g -> p g b"), out[r], H[:, r, :, CP + 1:CH:2], ALU.add))
            for r in range(2):
                lk(v.tensor_copy(H[:, r, :, CP:CH:2], hs[r]))
                last = v.tensor_copy(H[:, r, :, CP + 1:CH:2], mid[r])
            last.then_inc(S["h_done"], 1)
            for t in range(NT):
                dve.wait_ge(S["mix_ps"], t + 1)
                if t:
                    dve.wait_ge(S["mix_sb"], t)
                src = B[t % 2][:, :]
                if t < TP:
                    lk(tt(mtm, src.rearrange("p (h i) -> p h i", h=GH), bsp, ALU.add))
                else:
                    for h in range(GH):
                        lk(tt(mtm[:, h].rearrange("p (b s) -> p b s", b=DB), src[:, P * h:P * h + P].rearrange("p (b s) -> p b s", b=DB),
                              bsp[:, h, 0:DS].unsqueeze(1).to_broadcast([P, DB, DS]), ALU.add))
                tt(uT[:, :, P * t:P * t + P], uT[:, :, P * t:P * t + P], mtm, ALU.mult).then_inc(S["mix_sb"], 1)
            dve.wait_ge(S["v_out"], 16)
            for n in range(16):
                j, tb = divmod(n, 4)
                dve.wait_ge(S["sig_sb"], n + 1)
                o = bT[:, j].rearrange("p (c s) -> p s c", s=L)[:, 2 * tb:2 * tb + 2]
                tt(o, ytm[:, n % 2].rearrange("p (s c) -> p s c", s=2),
                   yT[:, j, 288 * tb:288 * tb + 288].rearrange("p (s c) -> p s c", s=2), ALU.mult).then_inc(S["b_done"], 1)
            dve.wait_ge(S["ld_xres"], 32)
            dve.wait_ge(S["bc_sb"], 6)
            dve.wait_ge(S["y_out"], 16 * L)
            for t in range(NT):
                c = 0 if t < TP else 1
                for h in range(2):
                    n = 2 * t + h
                    sl = slice(512 * h, 512 * h + 512)
                    dve.wait_ge(S["wo_ps"], n + 1)
                    tt(wtm[:, h], B[4 + n % 4][:, :], bc[:, 4 + c, sl], ALU.mult).then_inc(S["wo_used"], 1)
                    dve.wait_ge(S["wo_used"], n + 1)
                    last = tt(X1[:, t, sl], X1[:, t, sl], wtm[:, h], ALU.add)
                    if h == 0:
                        lk(last)
                last.then_inc(S["x1_done"], 1)
                dve.wait_ge(S["ss_done"], t + 1)
                lk(v.reciprocal(st[:, 4, t:t + 1], st[:, 1, t:t + 1]))
                if t >= 2:
                    dve.wait_ge(S[f"h2_out{t % 2}"], 16 * (t // 2))
                    dve.wait_ge(S["h2t_ps"], t - 1)
                lk(v.scalar_tensor_tensor(out=h2r[:, t % 2], in0=X1[:, t], scalar=st[:, 4, t:t + 1], in1=bc[:, c],
                                          op0=ALU.mult, op1=ALU.mult))
                tt(h2r[:, t % 2], h2r[:, t % 2], bc[:, 2 + c], ALU.add).then_inc(S["h2_rows"], 1)
            dve.wait_ge(S["lg_ps"], NT)
            dve.wait_ge(S["v_out"], 16)
            r3 = [rt[:, n].rearrange("p (t e) -> p t e", e=NE) for n in range(16)]
            r4 = [rt[:, n].rearrange("p (g e) -> p g e", e=EG) for n in range(16)]
            n9 = small[:, 0:8]
            col = lambda n: n9[:, n]
            spread = lambda x: x.unsqueeze(2).to_broadcast([P, NT, NE])
            lk(tt(r3[0], B[2][:, 0:NT * NE].rearrange("p (t e) -> p t e", e=NE),
                  brt[:, :].unsqueeze(1).to_broadcast([P, NT, NE]), ALU.add))
            lk(v.tensor_reduce(col(0), r3[0], AX.X, ALU.max))
            tt(r3[0], r3[0], spread(col(0)), ALU.subtract).then_inc(S["e_in"], 1)
            dve.wait_ge(S["exp_done"], 1)
            lk(v.tensor_reduce(col(1), r3[1], AX.X, ALU.add))
            lk(v.reciprocal(col(1), col(1)))
            lk(tt(r3[1], r3[1], spread(col(1)), ALU.mult))

            def rank(o, x, t, w):
                for i in range(4):
                    lk(v.memset(o[:, :, i], float(i)))
                for d in (1, 2, 3):
                    lk(tt(t[:, :, 0:4 - d], x[:, :, d:4], x[:, :, 0:4 - d], ALU.is_gt))
                    lk(tt(o[:, :, 0:4 - d], o[:, :, 0:4 - d], t[:, :, 0:4 - d], ALU.add))
                    lk(tt(o[:, :, d:4], o[:, :, d:4], t[:, :, 0:4 - d], ALU.subtract))
            rank(r4[2], r4[1], r4[3], NT * NG)
            lk(v.tensor_scalar(rt[:, 4], rt[:, 2], 1.5, None, ALU.is_lt))
            lk(tt(rt[:, 5], rt[:, 4], rt[:, 1], ALU.mult))
            gsum = small[:, 8:12].rearrange("p a b -> p (a b)")
            g3 = [small[:, 8 + 4 * n:12 + 4 * n].rearrange("p a b -> p (a b)").rearrange("p (t g) -> p t g", g=NG) for n in range(3)]
            lk(v.tensor_reduce(gsum, r4[5], AX.X, ALU.add))
            rank(g3[1], g3[0], g3[2], NT)
            g1f = small[:, 12:16].rearrange("p a b -> p (a b)")
            lk(v.tensor_scalar(g1f, g1f, 0.5, None, ALU.is_lt))
            gsel = g1f.unsqueeze(2).to_broadcast([P, NT * NG, EG])
            lk(v.tensor_scalar(rt[:, 6], rt[:, 2], 0.5, None, ALU.is_lt))
            lk(tt(rt[:, 7], rt[:, 4], rt[:, 6], ALU.subtract))
            for n in (6, 7):
                lk(tt(r4[n], r4[n], gsel, ALU.mult))
            tt(ohb[:, :, :], r3[6], r3[7], ALU.add).then_inc(S["oh_done"], 1)
            dve.wait_ge(S["zeroed"], 5)
            dve.wait_ge(S["pre_ps"], 1)
            cnt = B[2][:, 256:256 + NE]
            nb, cum, shift = rt[:, 10, 0:NE], rt[:, 11, 0:NE], rt[:, 12, 0:NE]
            lk(v.tensor_scalar(nb, cnt, BN + 0.5, None, ALU.is_gt))
            for r in range(2, ROUNDS):
                lk(v.tensor_scalar(cum, cnt, r * BN + 0.5, None, ALU.is_gt))
                lk(tt(nb, nb, cum, ALU.add))
            lk(v.memset(shift, 1.0))
            lk(v.tensor_tensor_scan(cum, shift, nb, 0.0, ALU.mult, ALU.add))
            lk(tt(shift, cum, nb, ALU.subtract))
            lk(v.tensor_scalar(shift, shift, NE - 1.0, float(BN), ALU.add, ALU.mult))
            lk(tt(shift, shift, ebase[:, :], ALU.subtract))
            wide = lambda x: x.unsqueeze(1).to_broadcast([P, NT, NE])
            before = B[3][:, 0:NT * NE].rearrange("p (t e) -> p t e", e=NE)
            lk(v.tensor_scalar(r3[9], before, BN - 0.5, None, ALU.is_gt))
            lk(tt(r3[9], r3[9], wide(shift), ALU.mult))
            lk(tt(r3[9], r3[9], before, ALU.add))
            lk(tt(r3[9], r3[9], wide(ebase[:, :]), ALU.add))
            for k in range(2):
                lk(tt(rt[:, 8], rt[:, 6 + k], rt[:, 9], ALU.mult))
                lk(v.tensor_reduce(col(5), r3[8], AX.X, ALU.add))
                last = v.tensor_copy(lst[:, k], col(5))
                if k == 0:
                    lk(last)
            last.then_inc(S["pos_done"], 1)
            for k in range(2):
                lk(tt(rt[:, 8], rt[:, 6 + k], rt[:, 1], ALU.mult))
                lk(v.tensor_reduce(col(2 + k), r3[8], AX.X, ALU.add))
            lk(tt(col(4), col(2), col(3), ALU.add))
            lk(v.reciprocal(col(4), col(4)))
            for k in range(2):
                lk(tt(gates[:, k], col(2 + k), col(4), ALU.mult))
            big = rt[0:1, 13:15].rearrange("p a b -> p (a b)")[:, 0:EXTRA * NE].rearrange("p (x e) -> p x e", e=NE)
            lk(tt(big, cum[0:1].unsqueeze(1).to_broadcast([1, EXTRA, NE]), iot[:, :].unsqueeze(2).to_broadcast([1, EXTRA, NE]), ALU.is_le))
            lk(v.tensor_copy(b64[:, 0:NE], etab[:, :]))
            lk(v.tensor_reduce(b64[:, NE:MAXB], big, AX.X, ALU.add))
            lk(v.tensor_scalar(b64[:, NE:MAXB], b64[:, NE:MAXB], NE - 1.0, None, ALU.min))
            lk(v.tensor_copy(tab[:, 0:MAXB], b64[:, 0:MAXB]))
            lk(v.tensor_scalar(shift[0:1, 0:1], cum[0:1, NE - 1:NE], float(NE), None, ALU.add))
            lk(v.tensor_scalar(shift[0:1, 1:2], cum[0:1, NE - 1:NE], float(NE - 1), None, ALU.add))
            v.tensor_copy(nblk[:, :], shift[0:1, 0:2]).then_inc(S["tab_done"], 1)
            dve.wait_ge(S["tab_done"], 1)
            n_blocks = dve.value_load(nblk[0:1, 0:1], min_val=NE, max_val=NE + EXTRA)
            last_block = dve.value_load(nblk[0:1, 1:2], min_val=NE - 1, max_val=NE + EXTRA - 1)
            dve.sem_inc(S["he_done"], 1)
            dve.sem_inc(S["out_sb"], 1)
            dve.sem_inc(S["out_d"], 16)

            def low_parts(i, *slots):
                for n in slots:
                    dve.wait_ge(S["hi_done"], SLOTS * i + n + 1)
                    tt(w_lo[n], w_raw[n], w_hi[n], ALU.subtract).then_inc(S["lo_done"], 1)

            def both_halves(o, bank):
                return v.tensor_reduce(o, bank[:, 0:2 * BN].rearrange("p (r n) -> p n r", r=2), AX.X, ALU.add)

            def columns_low(i, h):
                dve.wait_ge(S["xh_done"], 2 * i + h + 1)
                for m in range(2):
                    sl = slice(HB * h, HB * h + HB)
                    last = tt(x_hl[:, 4 * m:4 * m + 4, 1, sl], B[2 * h + m][:, 0:4 * HB].rearrange("p (k n) -> p k n", k=4),
                              x_hl[:, 4 * m:4 * m + 4, 0, sl], ALU.subtract)
                last.then_inc(S["xt2_sb"], 1)

            def block_on_dve(i, more):
                for f in range(KE):
                    here = (i, 8 + 2 * f) if f < 2 else (i + 1, 2 * f - 4)
                    split = f < 2 or more
                    dve.wait_ge(S["w_used"], SLOTS * i + 2 * f + 1)
                    both_halves(gate[:, f % 2], B[f % 2]).then_inc(S["gate_done"], 1)
                    if split:
                        low_parts(*here)
                    dve.wait_ge(S["w_used"], SLOTS * i + 2 * f + 2)
                    both_halves(up[:, f % 2], B[2 + f % 2]).then_inc(S["up_done"], 1)
                    dve.wait_ge(S["up_done"], KE * i + f + 1)
                    dve.wait_ge(S["silu_done"], KE * i + f + 1)
                    tt(he[:, f % 2], sil[:, f % 2], up[:, f % 2], ALU.mult).then_inc(S["he_full"], 1)
                    tt(he_hl[:, 0, f, 0:BN], sil[:, f % 2], up[:, f % 2], ALU.mult).then_inc(S["he_full"], 1)
                    dve.wait_ge(S["he_full"], 2 * (KE * i + f) + 2)
                    tt(he_hl[:, 1, f, 0:BN], he[:, f % 2], he_hl[:, 0, f, 0:BN], ALU.subtract).then_inc(S["he_done"], 1)
                    if split:
                        low_parts(here[0], here[1] + 1)
                if more:
                    low_parts(i + 1, 4)
                    columns_low(i + 1, 0)
                    columns_low(i + 1, 1)
                    low_parts(i + 1, 5, 6, 7)
                dve.wait_ge(S["out_d"], 32 * i + 16)
                for h in range(2):
                    for n in range(2):
                        if h == 1 and n == 1:
                            dve.wait_ge(S["w_used"], SLOTS * i + SLOTS)
                        else:
                            dve.wait_ge(S["down_ps"], 3 * i + 2 * h + n + 1)
                        last = v.tensor_copy(OUT[:, h, 512 * n:512 * n + 512], B[4 + 2 * h + n][0:HB, :])
                    last.then_inc(S["out_sb"], 1)
            for r in range(2):
                lk(v.tensor_scalar(he_hl[:, r, :, BN:], ident[:, 0:P - HB].unsqueeze(1).to_broadcast([P, KE, P - HB]), 0.0, None, ALU.mult))
            low_parts(0, *range(8))
            for h in range(2):
                columns_low(0, h)
            with dve.Fori(0, last_block) as i:
                block_on_dve(i, True)
            block_on_dve(last_block, False)
            dve.wait_ge(S["ld_gates"], 16)

            def combined(t):
                dve.wait_ge(S["comb_scaled"], t + 1)
                y0, y1 = YA[:, t % 4, 0], YA[:, t % 4, 1]
                lk(v.scalar_tensor_tensor(out=y0, in0=y1, scalar=gates[:, 1, t:t + 1], in1=y0, op0=ALU.mult, op1=ALU.add))
                lk(tt(y0, y0, gfb[:, 0 if t < TP else 1], ALU.mult))
                tt(X1[:, t], X1[:, t], y0, ALU.add).then_inc(S["fin_ss"], 1)
            combined(0)
            for t in range(NT):
                if t + 1 < NT:
                    combined(t + 1)
                dve.wait_ge(S["fin_ss"], t + 1)
                dve.sem_inc(S["comb_used"], 1)
                dve.wait_ge(S["fin_rs"], t + 1)
                lk(v.reciprocal(st[:, 4, t:t + 1], st[:, 1, t:t + 1]))
                if t >= 2:
                    dve.wait_ge(S[f"y_done{t % 2}"], 16 * (t // 2))
                v.scalar_tensor_tensor(out=fin[:, t % 2], in0=X1[:, t], scalar=st[:, 4, t:t + 1], in1=gfin,
                                       op0=ALU.mult, op1=ALU.mult).then_inc(S["fin_done"], 1)


_INS = ['x_prompt', 'x_sample', 'c_prompt', 'c_sample', 'state_s5_re', 'state_s5_im', 'w_ada', 'b_ada', 'g_norm_mix',
        'g_norm_ffn', 'w_in', 'gmlp_v_gain', 'gmlp_w_spatial', 'gmlp_b_spatial', 's5_a_re', 's5_a_im', 's5_log_dt',
        's5_b_re', 's5_b_im', 's5_c_re', 's5_c_im', 's5_d', 's5_w_glu', 's5_b_glu', 'w_out', 'w_router', 'b_router',
        'w_gate', 'w_up', 'w_down', 'g_final']
_OUTS = [(1, SEQ, D), (DB, DS, D), (1, 1, SG, SS), (1, 1, SG, SS), (1, DB, SG, SS), (1, DB, SG, SS), (1, DB, DS, GW)]


def kernel(**inputs):
    import numpy as _np
    import concourse.bacc as _bacc
    from concourse import mybir as _mybir
    from concourse.bass_utils import run_bass_kernel_spmd as _run

    nc = _bacc.Bacc("TRN2", target_bir_lowering=False, num_devices=1)
    arrays, args = {}, []
    for name in _INS:
        a = _np.ascontiguousarray(inputs[name])
        arrays[f"in_{name}_dram"] = a
        args.append(nc.dram_tensor(f"in_{name}_dram", a.shape, _mybir.dt.from_np(a.dtype), kind="ExternalInput").ap())
    for i, shape in enumerate(_OUTS):
        args.append(nc.dram_tensor(f"out_{i}_dram", shape, _mybir.dt.float32, kind="ExternalOutput").ap())
    hybrid_step(nc, *args)
    r = _run(nc, [arrays], core_ids=[0])
    return tuple(r.results[0][f"out_{i}_dram"] for i in range(len(_OUTS)))
```

```python
import math
from contextlib import ExitStack

import concourse.bass as bass
from concourse import mybir

ALU = mybir.AluOpType
ACT = mybir.ActivationFunctionType
AX = mybir.AxisListType
F32 = mybir.dt.float32
I32 = mybir.dt.int32
BF16 = mybir.dt.bfloat16
F32R = mybir.dt.float32r

P = 128
D = 1024
KD = D // P
SEQ, DB, DS = 1024, 8, 16
NT = (SEQ + DB * DS) // P
TP = SEQ // P
TOK = NT * P
NC = 1 + DB
GW = D // 2
GH = 4
KG = GW // P
SG, SQ, SS = 32, 16, 64
PR = SG // 2
L = 8
CH = TOK // L
CP = SEQ // L
SB = 2
NE, NG, EG = 16, 4, 4
DE = D // 2
KE = DE // P
BN = 192
HB = BN // 2
CAP = TOK
ROUNDS = CAP // BN
EXTRA = 2 * TOK // (BN + 1)
MAXB = NE + EXTRA
SLOTS, SLW = 2 * KE + KE, D
EPS = 1e-6
PI = math.pi
TWO_PI_HI = 6.28125
TWO_PI_MID = 0.0019340515136718750
TWO_PI_LO = 2 * math.pi - TWO_PI_HI - TWO_PI_MID
assert CAP % BN == 0 and L * SQ == P


def hybrid_step(nc, x_prompt, x_sample, c_prompt, c_sample, state_re, state_im, w_ada, b_ada, g_mix, g_ffn,
                w_in, v_gain, w_sp, b_sp, a_re, a_im, log_dt, b_re, b_im, c_re, c_im, d_skip, w_glu, b_glu,
                w_out, w_router, b_router, w_gate, w_up, w_down, g_final,
                y_prompt, y_sample, sp_re, sp_im, ss_re, ss_im, v_new):
    ctx = ExitStack()
    with ctx:
        def sb(name, shape, dt=F32):
            return ctx.enter_context(nc.sbuf_tensor(name, shape, dt))

        def sem(name):
            return ctx.enter_context(nc.semaphore(name))

        ctx.enter_context(nc.allow_non_contiguous_dma(reason="small parameter tables"))

        ub_d = nc.dram_tensor("ub_scratch", (GW, L, CH), F32).ap()
        y_d = nc.dram_tensor("y_scratch", (GW, L, CH), F32).ap()
        h2_d = nc.dram_tensor("h2_scratch", (TOK, D), F32).ap()
        list_d = nc.dram_tensor("list_scratch", (MAXB * BN, 1), I32).ap()
        ys_d = nc.dram_tensor("expert_rows", (MAXB * BN, D), F32).ap()

        sizes = dict(RA=9216, RB=4608, RC=4608, RD=2304, RE=4608, RF=4608, RG=4096, RT=2560, RW=12288)
        arena_at = -(-nc.sbuf_base // 32) * 32
        arena = sb("arena", [P, sum(sizes.values())])
        off = {}
        at = 0
        for name, n in sizes.items():
            off[name] = at
            at += n

        def area(region, start, *shape, parts=P):
            n = math.prod(shape)
            a = off[region] + start
            flat = arena[0:parts, a:a + n]
            if len(shape) == 1:
                return flat
            names = ["i", "j", "k", "l"][:len(shape)]
            return flat.rearrange("p (" + " ".join(names) + ") -> p " + " ".join(names),
                                  **dict(zip(names[1:], shape[1:])))

        ring = area("RW", 0, 3, KD, 512)
        hT = area("RA", 0, KD, TOK)
        H = area("RA", 0, 2, PR, CH)
        Y = area("RA", 4608, SG, CH)
        dtmp = area("RC", 0, SG, SQ)
        uT = area("RB", 0, KG, TOK)
        vn = area("RC", 0, NT, GW)
        bT = area("RC", 0, KG, TOK)
        ubT = area("RD", 0, 2, L, CH)
        U = area("RE", 0, SG, CH)
        yT = area("RE", 0, KG, L * CH)
        W = area("RF", 0, 2, PR, L + 1, SQ)
        X1 = area("RE", 0, NT, D)
        MT = area("RG", 0, SG, P)
        xin = [area(r, D * n, D) for r, n in (("RT", 0), ("RT", 1), ("RC", 0), ("RC", 1), ("RE", 0), ("RE", 1), ("RE", 2), ("RE", 3))]
        rows = area("RB", 0, 2, P)
        arow = area("RB", 256, 2, P)
        srow = area("RB", 512, 2, P)
        crow = area("RB", 768, 4, P)
        wsrow = area("RB", 1280, GH, P)
        junk_x = area("RB", 2304, 512).bitcast(BF16)
        junk_h = area("RT", 2048, 512).bitcast(BF16)
        zf = area("RD", 2048, 256)
        vgain = area("RD", 1536, GW)
        bsp = area("RD", 512, GH, P)
        smp = area("RT", 1024, 6, PR, DB)
        cc = area("RT", 2048, 2, PR, SQ)
        arows = area("RD", 1024, 512, parts=NC)
        EH = area("RT", 512, 2, PR, SS)
        wS = area("RT", 0, GH, P)
        bnat = area("RB", 1792, 2, PR, SQ)
        wtmp = area("RC", 0, 2, PR, L + 1, SQ)[:, 0]
        wtmp2 = area("RC", 2304, PR, L + 1, SQ)
        KT = area("RE", 0, SG, P, parts=SQ)
        gnat = area("RT", 0, 2, SB, L, SQ)
        gt = area("RD", 1536, 2, SB, P)
        tm = area("RT", 1024, 6, SB, P)
        bc = area("RG", 0, 6, D)
        gfb = area("RD", 0, 2, D)
        h2r = area("RA", 0, 2, D)
        h2T = area("RA", 2048, 2, KD, P)
        wtm = area("RA", 4096, 2, 512)
        ytm = area("RD", 0, 2, 288)
        gtm = area("RD", 0, 2, SB, L * SQ).rearrange("p i s (l q) -> p i s l q", l=L)
        mtm = area("RD", 1024, GH, P)
        fsr = area("RD", 1536, 4, P)
        XR = area("RB", 0, 2, D, parts=HB)
        OUT = area("RB", 2048, 2, D, parts=HB)
        gate = area("RC", 3072, 2, BN)
        up = area("RC", 3072 + 2 * BN, 2, BN)
        sil = area("RC", 3072 + 4 * BN, 2, BN)
        he = area("RC", 3072 + 6 * BN, 2, BN)

        def rounded(name, region, start, *shape, dt=F32R):
            return nc.alloc_sbuf_tensor_at(name, [P, *shape], dt, offset=arena_at + 4 * (off[region] + start))
        w_raw = [rounded(f"w_raw{n}", "RW", n * SLW, SLW, dt=F32)[:, :] for n in range(SLOTS)]
        w_lo = [rounded(f"w_lo{n}", "RW", n * SLW, SLW)[:, :] for n in range(SLOTS)]
        w_hi = [rounded(f"w_hi{n}", "RA", n * SLW, SLW)[:, :] if n < 9 else rounded(f"w_hi{n}", "RG", D + (n - 9) * SLW, SLW)[:, :]
                for n in range(SLOTS)]
        x_hl = rounded("x_hl", "RC", 0, KD, 2, BN)
        he_hl = rounded("he_hl", "RT", 0, 2, KE, HB + P)
        wv_raw, wv_lo = rounded("wv_raw", "RW", 8192, KD, 512, dt=F32), rounded("wv_lo", "RW", 8192, KD, 512)
        wv_hi = rounded("wv_hi", "RB", 0, KD, 512)
        hm_hi = rounded("hm_hi", "RT", 0, 2, KD, P)
        hm_lo = rounded("hm_lo", "RD", 0, 2, KD, P)
        wo_raw = [rounded(f"wo_raw{h}", "RW", 4096 * (1 + h), KD, 512, dt=F32) for h in range(2)]
        wo_lo = [rounded(f"wo_lo{h}", "RW", 4096 * (1 + h), KD, 512) for h in range(2)]
        wo_hi = [rounded("wo_hi0", "RA", 5120, KD, 512), rounded("wo_hi1", "RW", 0, KD, 512)]
        m_hi = rounded("m_hi", "RD", 0, 2, KD, P)
        u_lo = rounded("u_lo", "RB", 0, KG, TOK)
        b_lo = rounded("b_lo", "RC", 0, KG, TOK)
        WO_PIECES = [(0, 0), (0, 2), (0, 4), (0, 6), (1, 4), (1, 6), (1, 0), (1, 2)]
        SLICE_ORDER = [("gate", 0), ("up", 0), ("gate", 1), ("up", 1), ("gate", 2), ("up", 2), ("gate", 3), ("up", 3)] \
            + [("down", f) for f in range(KE)]

        YA = area("RW", 0, 4, 2, D)
        fin = area("RW", 8192, 4, D)
        gfin = area("RG", 0, D)
        rt = area("RC", 0, 16, NT * NE)

        ident = sb("ident", [P, P])
        tri = sb("tri", [P, P], BF16)
        ones = sb("ones", [P, P], BF16)
        modT = sb("modT", [P, 48, NC])
        Am = sb("Am", [P, KD, NC])
        Af = sb("Af", [P, KD, NC])
        vecT = sb("vecT", [P, 68])
        cT = sb("cT", [P, NC, KD])
        wT = sb("wT", [P, GH, P])
        LP = sb("LP", [P, 2, PR, L + 1])
        LR = sb("LR", [P, 2, PR, L])
        aT = sb("aT", [P, 2, PR])
        h0 = sb("h0", [P, 2, DB, PR])
        q = sb("q", [P, 24, PR])
        qi = sb("qi", [P, PR], I32)
        bb = sb("bb", [P, 2, PR, SQ])
        dq = sb("dq", [SQ, SG])
        fs = sb("fs", [P, 2, NC, PR])
        st = sb("st", [P, 6, NT])
        bn6 = sb("bn6", [P, 2, 6])
        wr = sb("wr", [P, KD, NE])
        brt = sb("brt", [P, NE])
        mv = sb("mv", [P, NT, 2])
        small = area("RC", 2304, 20, NT)
        ohb = sb("ohb", [P, NT, NE], BF16)
        ebase = sb("ebase", [P, NE])
        iot = sb("iot", [1, EXTRA])
        etab = sb("etab", [1, NE])
        lst = sb("lst", [P, 2, NT], I32)
        blocks = sb("blocks", [P, MAXB])
        firsts = sb("firsts", [P, MAXB])
        places = sb("places", [P, BN])
        tok_low = sb("tok_low", [P, 1])
        tok_high = sb("tok_high", [P, 2, NT])
        gates = sb("gates", [P, 2, NT])
        tab = sb("tab", [1, 32], I32)
        nblk = sb("nblk", [1, 2], I32)
        idx = sb("idx", [HB, 2], I32)
        eps = sb("eps", [P, 1])
        b64 = area("RC", 2560, 32, parts=1)
        at_place = area("RT", 0, NT * BN).bitcast(BF16).rearrange("p (j n) -> p j n", n=BN)
        in_block = area("RG", D, 2 * NT, MAXB)
        num = area("RG", 2 * D, 2 * NT * MAXB).bitcast(BF16).rearrange("p (r j n) -> p r j n", r=2, n=MAXB)
        blk = area("RG", 3 * D, 2 * NT)
        list_i = area("RG", 3 * D + 64, BN, parts=MAXB).bitcast(I32)

        B = [ctx.enter_context(nc.psum_tensor(f"bank{i}", [P, 512], F32)) for i in range(8)]

        names = ("ys_zero idx_seen wide_in ws_zero ld_gain ld_vec ld_s5 ld_c ld_mlp ld_x0 ld_x1 ld_x2 ld_x3 ld_w0 "
                 "ld_w1 ld_w2 ld_xres consts zeroed cols_t cond_t s5_t ws_t vec_t cond_done w_table kt_ps kt_sb "
                 "kt_done mt_placed ada_rows ada_ps ada_sb am_done sq_done x_norm xt_ps ht_sb_v ht_sb_s ring_used "
                 "ub_ps ub_sb ub_out0 ub_out1 u_in v_ps v_gelu v_done v_out uu_ps u_sb e_done g_nat g_ps g_sb "
                 "v5_ps v5_used h_done ws_done mix_ps mix_sb y_ps y_sb y_out y_in glu_ps sig_sb b_done bc_ps "
                 "bc_sb wo_ps wo_used x1_done ss_done h2_rows h2_out0 h2_out1 h2t_ps h2t_sb lg_ps exp_done e_in "
                 "wv_hi_done wv_lo_done hmh_done hml_done wo_hi_done wo_lo_done mh_done ml_done oh_done pre_ps "
                 "num_done place_done list_ps list_sb list_out tab_done idx_in rows_in xt2_ps xt2_sb gate_done "
                 "up_done he_full silu_done he_done w_used hi_done lo_done xh_done down_ps out_sb out_d rows_free "
                 "comb_in0 comb_in1 comb_in2 comb_in3 comb_used comb_scaled fin_ss fin_rs rs_done fin_scaled "
                 "fin_done y_done0 y_done1 y_done2 y_done3 fs_t fs_sb fs_out chain_v chain_s chain_g wdiag e_out "
                 "dt_in mg_in stats_v std_v mod_all").split()
        S = {n: sem(n) for n in names}
        LDS = [sem(f"ld_slice{n}") for n in range(SLOTS)]

        block = ctx.enter_context(nc.Block())

        def chained(eng, s):
            count = [0]

            def link(ins):
                count[0] += 1
                ins.then_inc(s, 1)
                eng.wait_ge(s, count[0])
            return link

        def cols(w, c):
            return w.rearrange("(k p) n -> p k n", p=P)[:, :, c * 512:(c + 1) * 512]
        ORDER = [("ada", c) for c in range(4)] + [("in", 2), ("in", 1), ("in", 0)] \
            + [("ada", c) for c in range(4, 12)] + [("glu", 0), ("out", 0), ("out", 1)]
        WSRC = {"ada": w_ada[0], "in": w_in[0], "glu": w_glu[0], "out": w_out[0]}
        place = {item: n for n, item in enumerate(ORDER)}
        LDW = [S["ld_w0"], S["ld_w1"], S["ld_w2"]]
        assert [place[item] % 3 for item in (("glu", 0), ("out", 0), ("out", 1), ("in", 1))] == [0, 1, 2, 2]

        def arrived(eng, item):
            n = place[item]
            eng.wait_ge(LDW[n % 3], 16 * (n // 3 + 1))
            return ring[:, n % 3]

        def ada_bank(c):
            return B[(4 if c < 4 else 0) + c % 2]

        x_rows = x_prompt[0].rearrange("(t p) d -> t p d", p=P)
        xs_rows = x_sample.rearrange("b s d -> (b s) d")

        def x_tile(t):
            return x_rows[t] if t < TP else xs_rows

        def c_rows(eng, r, c_in):
            for h in range(2):
                for gg in range(8):
                    src = c_in[0, 16 * h + 2 * gg:16 * h + 2 * gg + 2].rearrange("a q p -> q a p")
                    eng.dma_start(crow[16 * gg:16 * gg + 16, 2 * r + h].rearrange("q (a p) -> q a p", a=2), src).then_inc(S["ld_c"], 16)

        def y_store(eng, pos):
            eng.dma_start(y_d[:, pos].rearrange("(g q) c -> q g c", q=SQ), Y[SQ * pos:SQ * pos + SQ]).then_inc(S["y_out"], 16)

        @block.sync
        def _(sp):
            sp.dma_start(rows[0:8, 0], c_prompt.rearrange("a (k p) -> (a k) p", p=P)).then_inc(S["ld_vec"], 16)
            sp.dma_start(rows[8:72, 0], c_sample.rearrange("a (k p) -> (a k) p", p=P)).then_inc(S["ld_vec"], 16)
            for n in range(3):
                kind, c = ORDER[n]
                sp.dma_start(ring[:, n], cols(WSRC[kind], c)).then_inc(LDW[n], 16)
                if n == 0:
                    sp.dma_start(rows[0:48, 1], b_ada.rearrange("a (k p) -> (a k) p", p=P)).then_inc(S["ld_mlp"], 16)
                    sp.dma_start(rows[48:56, 1], g_mix.rearrange("a (k p) -> (a k) p", p=P)).then_inc(S["ld_mlp"], 16)
                    sp.dma_start(rows[56:64, 1], g_ffn.rearrange("a (k p) -> (a k) p", p=P)).then_inc(S["ld_mlp"], 16)
                    sp.dma_start(rows[64:68, 1], b_glu.rearrange("a (k p) -> (a k) p", p=P)).then_inc(S["ld_mlp"], 16)
            for n in range(3, len(ORDER)):
                if n == place["ada", 5]:
                    sp.wait_ge(S["kt_done"], 1)
                    sp.wait_ge(S["zeroed"], 1)
                    for s in range(L):
                        sp.dma_start(MT[SQ * s:SQ * s + SQ, :, SQ * s:P], KT[:, :, 0:P - SQ * s]).then_inc(S["mt_placed"], 16)
                    sp.wait_ge(S["mt_placed"], 16 * L)
                    sp.wait_ge(S["ub_out0"], 16 * KG // 2)
                    sp.wait_ge(S["ub_out1"], 16 * KG // 2)
                    for s in range(L):
                        sp.dma_start(U[SQ * s:SQ * s + SQ], ub_d[:, s].rearrange("(g q) c -> q g c", q=SQ)).then_inc(S["u_in"], 16)
                kind, c = ORDER[n]
                sp.wait_ge(S["ring_used"], n - 2)
                dst = {"glu": ring[:, n % 3, 0:4], "out": wo_raw[c % 2][:, :, :]}.get(kind, ring[:, n % 3])
                if (kind, c) == ("in", 1):
                    dst = wv_raw[:, :, :]
                sp.dma_start(dst, cols(WSRC[kind], c)).then_inc(LDW[n % 3], 16)
            sp.wait_ge(S["y_sb"], 6)
            for pos in range(L // 2):
                y_store(sp, pos)
            sp.wait_ge(S["y_out"], 16 * L)
            sp.dma_start(yT, y_d.rearrange("(j p) s c -> p j (s c)", p=P)).then_inc(S["y_in"], 16)
            def slices(e, used):
                for n, (kind, f) in enumerate(SLICE_ORDER):
                    if used is not None:
                        sp.wait_ge(S["w_used"], used + n + 1)
                    if kind == "down":
                        sp.dma_start(w_raw[n], w_down[0, e].rearrange("a (f p) n -> p (a f) n", p=P)[:, f]).then_inc(LDS[n], 16)
                    else:
                        w = w_gate if kind == "gate" else w_up
                        src = w[0, e].rearrange("a (k p) n -> p (a k) n", p=P)[:, :, P * f:P * f + P]
                        sp.dma_start(w_raw[n].rearrange("p (k n) -> p k n", k=KD), src).then_inc(LDS[n], 16)
            sp.wait_ge(S["ring_used"], len(ORDER))
            slices(slice(0, 1), None)
            sp.wait_ge(S["list_sb"], 1)
            sp.dma_start(list_d.rearrange("(b n) a -> b (n a)", n=BN), list_i).then_inc(S["list_out"], 16)
            sp.wait_ge(S["tab_done"], 1)
            n_blocks = sp.value_load(nblk[0:1, 0:1], min_val=NE, max_val=NE + EXTRA)
            with sp.Fori(1, n_blocks) as i:
                e = sp.value_load(tab[0:1, bass.ds(i, 1)], min_val=0, max_val=NE - 1)
                slices(bass.ds(e, 1), SLOTS * (i - 1))
            for t in range(NT):
                sp.wait_ge(S["fin_done"], t + 1)
                dst = y_prompt[0].rearrange("(t p) d -> t p d", p=P)[t] if t < TP else y_sample.rearrange("b s d -> (b s) d")
                sp.dma_start(dst, fin[:, t % 4]).then_inc(S[f"y_done{t % 4}"], 16)
            for r in range(4):
                sp.wait_ge(S[f"y_done{r}"], 16 * len(range(r, NT, 4)))
            sp.wait_ge(S["fs_out"], 64)
            sp.wait_ge(S["v_out"], 16)

        @block.gpsimd
        def _(gp):
            g = nc.gpsimd
            lk = chained(gp, S["chain_g"])
            lk(g.memset(ident[:, :], 0.0))
            lk(g.affine_select(out=ident[:, :], in_=ident[:, :], compare_op=ALU.not_equal, fill=1.0, base=0,
                               pattern=[[-1, P]], channel_multiplier=1))
            g.memset(eps[:, :], EPS).then_inc(S["consts"], 1)
            g.memset(ones[:, :], 1.0).then_inc(S["consts"], 1)
            lk(g.memset(tri[:, :], 1.0))
            g.affine_select(out=tri[:, :], in_=tri[:, :], compare_op=ALU.is_gt, fill=0.0, base=0,
                            pattern=[[1, P]], channel_multiplier=-1).then_inc(S["consts"], 1)
            gp.dma_start(arow[0:PR, 0], a_re[0].rearrange("(g a) p -> g (a p)", a=2)).then_inc(S["ld_s5"], 16)
            gp.dma_start(arow[0:PR, 1], a_im[0].rearrange("(g a) p -> g (a p)", a=2)).then_inc(S["ld_s5"], 16)
            for r, (s_in, b_in) in enumerate(((state_re, b_re), (state_im, b_im))):
                gp.dma_start(srow[:, r], s_in[0].rearrange("b (g a) p -> (b g) (a p)", a=2)).then_inc(S["ld_s5"], 16)
                gp.dma_start(bnat[:, r], b_in[0].rearrange("(g a) p q -> (a p) g q", a=2)).then_inc(S["ld_s5"], 16)
            for a in range(2):
                gp.dma_start(q[SS * a:SS * a + SS, 0], log_dt[0].rearrange("(g a) -> a g", a=2)[a].partition_broadcast(SS)).then_inc(S["ld_s5"], 16)
            gp.dma_start(dq[:, :], d_skip[0].rearrange("g q -> q g")).then_inc(S["ld_s5"], 16)
            c_rows(gp, 0, c_re)
            c_rows(gp, 1, c_im)
            g.memset(MT, 0.0).then_inc(S["zeroed"], 1)
            g.iota(ebase[:, :], pattern=[[BN, NE]], base=0, channel_multiplier=0, allow_small_or_imprecise_dtypes=True).then_inc(S["zeroed"], 1)
            g.iota(iot[:, :], pattern=[[1, EXTRA]], base=0, channel_multiplier=0, allow_small_or_imprecise_dtypes=True).then_inc(S["zeroed"], 1)
            g.iota(etab[:, :], pattern=[[1, NE]], base=0, channel_multiplier=0, allow_small_or_imprecise_dtypes=True).then_inc(S["zeroed"], 1)
            for dst, pattern, base, each in ((blocks[:, :], [[1, MAXB]], 0, 0), (firsts[:, :], [[BN, MAXB]], BN, 0), (places[:, :], [[1, BN]], 0, 0),
                                             (tok_low[:, :], [[0, 1]], 0, 1), (tok_high[:, :, :], [[0, 2], [P, NT]], 0, 0)):
                g.iota(dst, pattern=pattern, base=base, channel_multiplier=each, allow_small_or_imprecise_dtypes=True).then_inc(S["zeroed"], 1)
            gp.wait_ge(S["w_table"], 1)
            for s in range(PR // SB):
                sl = slice(SB * s, SB * s + SB)
                if s == 0:
                    gp.wait_ge(S["xt_ps"], NT)
                    gp.wait_ge(S["e_done"], 1)
                    gp.wait_ge(S["ub_out0"], 16 * KG // 2)
                    gp.wait_ge(S["ub_out1"], 16 * KG // 2)
                else:
                    gp.wait_ge(S["g_ps"], s)
                for r in range(2):
                    lam0 = LR[:, 0, sl].unsqueeze(3).to_broadcast([P, SB, L, SQ])
                    lam1 = LR[:, 1, sl].unsqueeze(3).to_broadcast([P, SB, L, SQ])
                    b0 = bb[:, r, sl].unsqueeze(2).to_broadcast([P, SB, L, SQ])
                    b1 = bb[:, 1 - r, sl].unsqueeze(2).to_broadcast([P, SB, L, SQ])
                    t0, t1 = gtm[:, 0], gtm[:, 1]
                    lk(g.tensor_tensor(t0, lam0, b0, ALU.mult))
                    lk(g.tensor_tensor(t1, lam1, b1, ALU.mult))
                    last = g.tensor_tensor(gnat[:, r], t0, t1, ALU.subtract if r == 0 else ALU.add)
                    if r == 0:
                        lk(last)
                    else:
                        last.then_inc(S["g_nat"], 1)
                        gp.wait_ge(S["g_nat"], s + 1)
            gp.wait_ge(S["g_ps"], PR // SB)
            g.memset(wS, 0.0).then_inc(S["ws_zero"], 1)
            gp.wait_ge(S["mix_ps"], NT)
            gp.wait_ge(S["h_done"], 1)
            gp.wait_ge(S["ld_xres"], 32)
            lk(g.memset(zf, 0.0))
            gp.dma_start(ys_d[NE * BN:MAXB * BN].rearrange("(p a) (b n) -> p (a b) n", p=64, n=256),
                         zf[0:64].unsqueeze(1).to_broadcast([64, EXTRA * BN // 64 * 4, 256])).then_inc(S["ys_zero"], 16)
            gp.wait_ge(S["list_out"], 16)
            gp.wait_ge(S["h2_out0"], 16 * 5)
            gp.wait_ge(S["h2_out1"], 16 * 4)

            def rows_of_block(first):
                gp.dma_start(idx[:, :], list_d[first].rearrange("(h p) a -> p (h a)", p=HB)).then_inc(S["idx_in"], 16)

            def gather_rows():
                for h in range(2):
                    gp.indirect_dma_start(out=XR[:, h], out_offset=None, in_=h2_d,
                                          in_offset=bass.IndirectOffsetOnAxis(ap=idx[:, h:h + 1], axis=0)).then_inc(S["rows_in"], 16)
            rows_of_block(slice(0, BN))
            gp.wait_ge(S["idx_in"], 16)
            gather_rows()
            gp.wait_ge(S["rows_in"], 32)
            gp.wait_ge(S["tab_done"], 1)
            n_blocks = gp.value_load(nblk[0:1, 0:1], min_val=NE, max_val=NE + EXTRA)
            with gp.Fori(1, n_blocks) as i:
                gp.wait_ge(S["rows_free"], i)
                rows_of_block(bass.ds(i * BN, BN))
                gp.wait_ge(S["idx_in"], 16 * i + 16)
                gp.sem_inc(S["idx_seen"], 1)
                gather_rows()
                gp.wait_ge(S["rows_in"], 32 * i + 32)
            gp.wait_ge(S["ys_zero"], 16)
            gp.wait_ge(S["out_d"], 32 * n_blocks + 16)
            gp.sem_inc(S["idx_seen"], 1)
            gp.wait_ge(S["w_used"], SLOTS * n_blocks)
            gp.sem_inc(S["idx_seen"], 1)

            def gather_choices(t):
                if t >= 4:
                    gp.wait_ge(S["comb_used"], t - 3)
                for k in range(2):
                    gp.indirect_dma_start(out=YA[:, t % 4, k], out_offset=None, in_=ys_d,
                                          in_offset=bass.IndirectOffsetOnAxis(ap=lst[:, k, t:t + 1], axis=0)).then_inc(S[f"comb_in{t % 4}"], 16)
            for t in range(4):
                gather_choices(t)
            gp.wait_ge(S["ld_gain"], 48)
            for t in range(NT):
                if t + 4 < NT:
                    gather_choices(t + 4)
                gp.wait_ge(S["fin_scaled"], t + 1)
                g.tensor_tensor(fin[:, t % 4], fin[:, t % 4], gfin, ALU.mult).then_inc(S["fin_done"], 1)

        @block.scalar
        def _(act):
            a = nc.scalar
            lk = chained(act, S["chain_s"])
            act.dma_start(wsrow, w_sp[0].rearrange("h i j -> i h j")).then_inc(S["ld_mlp"], 16)
            act.dma_start(wr[:, :, :], w_router.rearrange("(k p) n -> p k n", p=P)).then_inc(S["ld_mlp"], 16)
            act.dma_start(brt[:, :], b_router.partition_broadcast(P)).then_inc(S["ld_mlp"], 16)

            def x_sumsq(t):
                act.wait_ge(S[f"ld_x{t % 4}"], 16 * (t // 4 + 1))
                lk(a.activation(junk_x, xin[t % 8], ACT.Square, accum_out=st[:, 0, t:t + 1]))
                a.activation(st[:, 1, t:t + 1], st[:, 0, t:t + 1], ACT.Sqrt, scale=1.0 / D, bias=eps[:, 0:1]).then_inc(S["sq_done"], 1)

            def x_load(t):
                if t >= 8:
                    act.wait_ge(S["xt_ps"], t - 7)
                act.dma_start(xin[t % 8], x_tile(t)).then_inc(S[f"ld_x{t % 4}"], 16)

            def modulation_rows(c):
                act.wait_ge(S["ring_used"], place["ada", c] + 1)
                if c:
                    act.wait_ge(S["ada_ps"], c)
                a.copy(arows, ada_bank(c)[0:NC, :]).then_inc(S["ada_rows"], 1)
            act.wait_ge(S["cols_t"], 1)
            a.activation(cT[:, :, :], B[0][:, 128:200].rearrange("p (j k) -> p j k", k=KD), ACT.Silu).then_inc(S["cond_done"], 1)
            for t in range(4):
                act.dma_start(xin[t], x_tile(t)).then_inc(S[f"ld_x{t}"], 16)
            act.wait_ge(S["ws_t"], 1)
            a.copy(wT[:, :, :], B[3][:, :].rearrange("p (h i) -> p h i", h=GH)).then_inc(S["ws_done"], 1)
            act.wait_ge(S["consts"], 3)
            x_sumsq(0)
            x_load(4)
            x_sumsq(1)
            x_load(5)
            modulation_rows(0)
            act.wait_ge(S["vec_t"], 1)
            a.copy(vecT[:, :], B[6][:, 0:68]).then_inc(S["cond_done"], 1)
            x_sumsq(2)
            x_load(6)
            modulation_rows(1)
            x_sumsq(3)
            x_load(7)
            x_sumsq(4)
            modulation_rows(2)
            x_sumsq(5)
            x_load(8)
            modulation_rows(3)
            act.wait_ge(S["am_done"], 1)
            for t in range(NT):
                act.wait_ge(S["xt_ps"], t + 1)
                if t < TP:
                    for k in range(4, KD):
                        last = a.activation(hT[:, k, P * t:P * t + P], B[2 * (t % 2) + k // 4][:, P * (k % 4):P * (k % 4) + P],
                                            ACT.Identity, scale=Am[:, k, 0:1], bias=modT[:, k, 0:1])
                    last.then_inc(S["ht_sb_s"], 1)
                if t + 6 < NT:
                    x_sumsq(t + 6)
            act.wait_ge(S["s5_t"], 1)
            a.copy(aT[:, :, :], B[6][:, 0:32].rearrange("p (r g) -> p r g", r=2)).then_inc(S["cond_t"], 1)
            a.copy(h0[:, :, :, :], B[6][:, 128:384].rearrange("p (r b g) -> p r b g", r=2, b=DB)).then_inc(S["cond_t"], 1)
            a.copy(cc, B[7][:, :].rearrange("p (r g q) -> p r g q", r=2, g=PR)).then_inc(S["cond_t"], 1)
            act.wait_ge(S["ld_s5"], 16 * 9)
            a.activation(q[:, 1], q[:, 0], ACT.Exp).then_inc(S["dt_in"], 1)
            act.wait_ge(S["mg_in"], 1)
            a.activation(q[:, 4], q[:, 2], ACT.Exp).then_inc(S["dt_in"], 1)
            a.activation(q[:, 5], q[:, 2], ACT.Exp, scale=float(L)).then_inc(S["dt_in"], 1)
            act.wait_ge(S["mg_in"], 2)
            a.activation(q[:, 8], q[:, 6], ACT.Sin).then_inc(S["dt_in"], 1)
            a.activation(q[:, 9], q[:, 7], ACT.Sin).then_inc(S["dt_in"], 1)

            def v_weights_high(k):
                a.copy(wv_hi[:, k], wv_raw[:, k]).then_inc(S["wv_hi_done"], 1)

            def v_columns_high(t):
                if t >= 2:
                    act.wait_ge(S["v_ps"], t - 1)
                a.copy(hm_hi[:, t % 2], hT[:, :, P * t:P * t + P]).then_inc(S["hmh_done"], 1)
            for n in range(12):
                j, tb = divmod(n, 3)
                act.wait_ge(S["ub_ps"], n + 1)
                if tb == 0 and j >= 2:
                    act.wait_ge(S[f"ub_out{j % 2}"], 16 * (j // 2))
                a.copy(ubT[:, j % 2, :, 48 * tb:48 * tb + 48],
                       B[4 + n % 4][:, 0:384].rearrange("p (c s) -> p s c", s=L)).then_inc(S["ub_sb"], 1)
                if tb == 2:
                    act.wait_ge(S["ub_sb"], n + 1)
                    act.dma_start(ub_d[P * j:P * j + P], ubT[:, j % 2]).then_inc(S[f"ub_out{j % 2}"], 16)
                if n == 6:
                    act.wait_ge(S["w_table"], 1)
                    arrived(act, ("in", 1))
                if n >= 6:
                    v_weights_high(n - 6)
            v_weights_high(6)
            v_weights_high(7)
            act.wait_ge(S["ht_sb_v"], NT)
            v_columns_high(0)
            v_columns_high(1)
            for n in range(SG // 8):
                act.wait_ge(S["kt_ps"], n + 1)
                for o in range(2):
                    last = a.copy(KT[:, 8 * n + o:8 * n + 8:2], B[4 + 2 * (n % 2) + o][0:SQ, :].rearrange("p (g m) -> p g m", g=4))
                last.then_inc(S["kt_sb"], 1)
            act.wait_ge(S["kt_done"], 1)
            for t in range(NT):
                act.wait_ge(S["v_ps"], t + 1)
                if t + 2 < NT:
                    v_columns_high(t + 2)
                a.activation(vn[:, t], B[4 + (12 + t) % 4][:, :], ACT.Gelu_apprx_tanh).then_inc(S["v_gelu"], 1)
            act.dma_start(vgain, v_gain[0].partition_broadcast(P)).then_inc(S["ld_gain"], 16)
            act.dma_start(bsp, b_sp[0].partition_broadcast(P)).then_inc(S["ld_gain"], 16)
            act.wait_ge(S["stats_v"], NT)
            a.activation(st[:, 2], st[:, 3], ACT.Sqrt, bias=eps[:, 0:1]).then_inc(S["std_v"], 1)
            for n in range(12):
                j, tb = divmod(n, 3)
                act.wait_ge(S["uu_ps"], n + 1)
                a.activation(uT[:, j, 384 * tb:384 * tb + 384], B[4 + (21 + n) % 4][:, 0:384], ACT.Gelu_apprx_tanh).then_inc(S["u_sb"], 1)
            act.wait_ge(S["uu_ps"], 12)
            act.wait_ge(S["e_done"], 1)
            for r in range(2):
                a.copy(H[:, r, :, 0:SS], EH[:, r]).then_inc(S["e_out"], 1)
            for s in range(PR // SB):
                act.wait_ge(S["g_ps"], s + 1)
                if s:
                    act.wait_ge(S["v5_ps"], s)
                else:
                    act.wait_ge(S["v_done"], 1)
                a.copy(gt, B[2 + s % 2][:, :].rearrange("p (r g m) -> p r g m", r=2, g=SB)).then_inc(S["g_sb"], 1)
                if s:
                    modulation_rows(3 + s)
            modulation_rows(11)
            act.wait_ge(S["ws_zero"], 1)
            act.wait_ge(S["ws_done"], 2)
            for b in range(DB):
                act.dma_start(wS[DS * b:DS * b + DS, :, DS * b:DS * b + DS], wT[0:DS, :, 0:DS]).then_inc(S["wdiag"], 16)
            for n in range(6):
                act.wait_ge(S["y_ps"], n + 1)
                m = min(3, PR - 3 * n)
                for o in range(2):
                    last = a.activation(Y[:, 6 * n + o:6 * n + 2 * m:2], B[4 + 2 * (n % 2) + o][:, 0:m * CH].rearrange("p (g c) -> p g c", g=m),
                                        ACT.Gelu_apprx_tanh)
                last.then_inc(S["y_sb"], 1)
            act.wait_ge(S["y_sb"], 6)
            for pos in range(L // 2, L):
                y_store(act, pos)
            act.wait_ge(S["fs_t"], 1)
            a.copy(fsr, B[2][:, :].rearrange("p (r m) -> p r m", r=4)).then_inc(S["fs_sb"], 1)
            act.wait_ge(S["fs_sb"], 1)
            for r, (o_p, o_s) in enumerate(((sp_re, ss_re), (sp_im, ss_im))):
                act.dma_start(o_s[0].rearrange("b (g a) p -> (b g) (a p)", a=2), fsr[:, r]).then_inc(S["fs_out"], 16)
                act.dma_start(o_p[0, 0].rearrange("(g a) p -> g (a p)", a=2), fsr[0:PR, 2 + r]).then_inc(S["fs_out"], 16)
            act.wait_ge(S["v_done"], 1)
            act.dma_start(v_new[0].rearrange("b s d -> (b s) d"), vn[:, NT - 1]).then_inc(S["v_out"], 16)
            act.wait_ge(S["mix_ps"], NT)
            act.wait_ge(S["mod_all"], 1)

            def widen(dst, src, first):
                a.copy(dst.rearrange("p (k b s) -> p k b s", k=KD, b=DB),
                       src[:, first:first + KD, 1:NC].unsqueeze(3).to_broadcast([P, KD, DB, DS])).then_inc(S["wide_in"], 1)
            for n, (src, first) in ((1, (Af, 0)), (3, (modT, 24)), (5, (modT, 16))):
                widen(bc[:, n], src, first)
            for n in range(6):
                act.wait_ge(S["bc_ps"], n + 1)
                for h in range(2):
                    last = a.copy(bc[:, n, 512 * h:512 * h + 512], B[2 * (n % 2) + h][:, :])
                last.then_inc(S["bc_sb"], 1)
            def wo_high(piece):
                h, k = WO_PIECES[piece]
                a.copy(wo_hi[h][:, k:k + 2], wo_raw[h][:, k:k + 2]).then_inc(S["wo_hi_done"], 1)

            def m_high(t):
                if t >= 2:
                    act.wait_ge(S["wo_ps"], 2 * t - 2)
                a.copy(m_hi[:, t % 2, 0:KG], uT[:, :, P * t:P * t + P])
                a.copy(m_hi[:, t % 2, KG:KD], bT[:, :, P * t:P * t + P]).then_inc(S["mh_done"], 1)
            for n in range(16):
                j = n // 4
                act.wait_ge(S["glu_ps"], n + 1)
                if n >= 2:
                    act.wait_ge(S["b_done"], n - 1)
                a.activation(ytm[:, n % 2], B[4 + n % 4][:, 0:288], ACT.Sigmoid, bias=vecT[:, 64 + j:65 + j]).then_inc(S["sig_sb"], 1)
                if n == 4:
                    act.wait_ge(S["y_out"], 16 * L)
                    for h in range(2):
                        arrived(act, ("out", h))
                if 4 <= n < 10:
                    wo_high(n - 4)
            act.wait_ge(S["fs_out"], 64)
            act.wait_ge(S["b_done"], 16)
            m_high(0)
            wo_high(6)
            wo_high(7)
            m_high(1)
            act.dma_start(X1[:, 0:TP], x_prompt[0].rearrange("(t p) d -> p t d", p=P)).then_inc(S["ld_xres"], 16)
            act.dma_start(X1[:, TP], xs_rows).then_inc(S["ld_xres"], 16)
            def h2_columns(t):
                act.wait_ge(S["h2t_ps"], t + 1)
                if t >= 2:
                    act.wait_ge(S["lg_ps"], t - 1)
                for h in range(2):
                    last = a.copy(h2T[:, t % 2, 4 * h:4 * h + 4], B[h][:, :].rearrange("p (k m) -> p k m", k=4))
                last.then_inc(S["h2t_sb"], 1)
                act.dma_start(h2_d[P * t:P * t + P], h2r[:, t % 2]).then_inc(S[f"h2_out{t % 2}"], 16)

            for t in range(NT):
                act.wait_ge(S["x1_done"], t + 1)
                lk(a.activation(junk_h, X1[:, t], ACT.Square, accum_out=st[:, 0, t:t + 1]))
                a.activation(st[:, 1, t:t + 1], st[:, 0, t:t + 1], ACT.Sqrt, scale=1.0 / D, bias=eps[:, 0:1]).then_inc(S["ss_done"], 1)
                if t:
                    h2_columns(t - 1)
                if t + 2 < NT:
                    m_high(t + 2)
            h2_columns(NT - 1)
            act.wait_ge(S["wo_ps"], 2 * NT)
            widen(gfb[:, 1], modT, 40)
            act.dma_start(gfin, g_final.partition_broadcast(P)).then_inc(S["ld_gain"], 16)
            act.wait_ge(S["e_in"], 1)
            a.activation(rt[:, 1], rt[:, 0], ACT.Exp).then_inc(S["exp_done"], 1)
            for n in range(6, 8):
                act.wait_ge(S["bc_ps"], n + 1)
                for h in range(2):
                    last = a.copy(gfb[:, n - 6, 512 * h:512 * h + 512], B[4 + 2 * (n % 2) + h][:, :])
                last.then_inc(S["bc_sb"], 1)
            def high_parts(i, *slots):
                for n in slots:
                    act.wait_ge(LDS[n], 16 * i + 16)
                    a.copy(w_hi[n], w_raw[n]).then_inc(S["hi_done"], 1)
            act.wait_ge(S["h2_out0"], 16 * 5)
            act.wait_ge(S["h2_out1"], 16 * 4)
            high_parts(0, *range(8))
            act.wait_ge(S["tab_done"], 1)
            n_blocks = act.value_load(nblk[0:1, 0:1], min_val=NE, max_val=NE + EXTRA)
            last_block = act.value_load(nblk[0:1, 1:2], min_val=NE - 1, max_val=NE + EXTRA - 1)

            def rows_to_columns(i, h):
                act.wait_ge(S["xt2_ps"], 2 * i + h + 1)
                for m in range(2):
                    last = a.copy(x_hl[:, 4 * m:4 * m + 4, 0, HB * h:HB * h + HB],
                                  B[2 * h + m][:, 0:4 * HB].rearrange("p (k n) -> p k n", k=4))
                last.then_inc(S["xh_done"], 1)

            def block_on_act(i, more):
                for f in range(KE):
                    here = (i, 8 + 2 * f) if f < 2 else (i + 1, 2 * f - 4)
                    split = f < 2 or more
                    if split:
                        high_parts(here[0], here[1])
                    act.wait_ge(S["gate_done"], KE * i + f + 1)
                    a.activation(sil[:, f % 2], gate[:, f % 2], ACT.Silu).then_inc(S["silu_done"], 1)
                    if split:
                        high_parts(here[0], here[1] + 1)
                if more:
                    high_parts(i + 1, 4)
                    rows_to_columns(i + 1, 0)
                    rows_to_columns(i + 1, 1)
                    high_parts(i + 1, 5, 6, 7)
                for h in range(2):
                    act.wait_ge(S["out_sb"], 2 * i + h + 2)
                    act.dma_start(ys_d[bass.ds(i * BN + HB * h, HB)], OUT[:, h]).then_inc(S["out_d"], 16)
            for h in range(2):
                rows_to_columns(0, h)
            with act.Fori(0, last_block) as i:
                block_on_act(i, True)
            block_on_act(last_block, False)
            def first_choice(t):
                act.wait_ge(S[f"comb_in{t % 4}"], 32 * (t // 4) + 32)
                a.activation(YA[:, t % 4, 0], YA[:, t % 4, 0], ACT.Copy, scale=gates[:, 0, t:t + 1]).then_inc(S["comb_scaled"], 1)
            first_choice(0)
            first_choice(1)
            for t in range(NT):
                act.wait_ge(S["fin_ss"], t + 1)
                lk(a.activation(junk_h, X1[:, t], ACT.Square, accum_out=st[:, 0, t:t + 1]))
                a.activation(st[:, 1, t:t + 1], st[:, 0, t:t + 1], ACT.Sqrt, scale=1.0 / D, bias=eps[:, 0:1]).then_inc(S["fin_rs"], 1)
                if t + 2 < NT:
                    first_choice(t + 2)
                act.wait_ge(S["rs_done"], t + 1)
                if t >= 4:
                    act.wait_ge(S[f"y_done{t % 4}"], 16 * (t // 4))
                a.activation(fin[:, t % 4], X1[:, t], ACT.Copy, scale=st[:, 4, t:t + 1]).then_inc(S["fin_scaled"], 1)

        @block.tensor
        def _(pe):
            T = nc.tensor
            pe.wait_ge(S["consts"], 1)
            pe.wait_ge(S["ld_vec"], 16 * 2)
            T.transpose(B[0][:, 128:200], rows[0:72, 0], ident[0:72, 0:72]).then_inc(S["cols_t"], 1)
            def modulation(c):
                w = arrived(pe, ("ada", c))
                if c >= 2:
                    pe.wait_ge(S["ada_sb"], c - 1)
                for k in range(KD):
                    last = T.matmul(ada_bank(c)[0:NC, :], cT[:, :, k], w[:, k], start=(k == 0), stop=(k == KD - 1))
                last.then_inc(S["ring_used"], 1)

            def modulation_turned(c):
                pe.wait_ge(S["ada_rows"], c + 1)
                for j in range(4):
                    last = T.transpose(ada_bank(c)[:, NC * j:NC * j + NC], arows[:, P * j:P * j + P], ident[0:NC, 0:NC])
                last.then_inc(S["ada_ps"], 1)

            def turned(x, t, banks):
                for k in range(KD):
                    last = T.transpose(B[banks + k // 4][:, P * (k % 4):P * (k % 4) + P], x[:, P * k:P * k + P], ident[:, :])
                return last

            def x_turned(t):
                pe.wait_ge(S["x_norm"], t + 1)
                if t >= 2:
                    pe.wait_ge(S["ht_sb_v"], t - 1)
                    pe.wait_ge(S["ht_sb_s"], t - 1)
                turned(xin[t % 8], t, 2 * (t % 2)).then_inc(S["xt_ps"], 1)

            pe.wait_ge(S["cond_done"], 1)
            modulation(0)
            pe.wait_ge(S["ld_mlp"], 16 * 7)
            for h in range(GH):
                last = T.transpose(B[3][:, P * h:P * h + P], wsrow[:, h], ident[:, :])
            last.then_inc(S["ws_t"], 1)
            T.transpose(B[6][:, 0:68], rows[0:68, 1], ident[0:68, 0:68]).then_inc(S["vec_t"], 1)
            modulation(1)
            pe.wait_ge(S["ws_done"], 1)
            modulation_turned(0)
            x_turned(0)
            modulation(2)
            modulation_turned(1)
            x_turned(1)
            modulation(3)
            modulation_turned(2)
            modulation_turned(3)
            for t in range(2, NT):
                x_turned(t)
            pe.wait_ge(S["ld_s5"], 16 * 9)
            pe.wait_ge(S["ld_c"], 16 * 32)
            pe.wait_ge(S["cond_done"], 2)
            for r in range(2):
                T.transpose(B[6][:, PR * r:PR * r + PR], arow[0:PR, r], ident[0:PR, 0:PR])
                T.transpose(B[6][:, P + P * r:2 * P + P * r], srow[:, r], ident[:, :])
            for n in range(4):
                last = T.transpose(B[7][:, P * n:P * n + P], crow[:, n], ident[:, :])
            last.then_inc(S["s5_t"], 1)
            pe.wait_ge(S["ada_sb"], 4)
            pe.wait_ge(S["cond_t"], 3)
            w = arrived(pe, ("in", 2))
            for n in range(12):
                j, tb = divmod(n, 3)
                if n < 3:
                    pe.wait_ge(S["ht_sb_v"], 3 * (n + 1))
                    pe.wait_ge(S["ht_sb_s"], min(TP, 3 * (n + 1)))
                if n >= 4:
                    pe.wait_ge(S["ub_sb"], n - 3)
                for k in range(KD):
                    last = T.matmul(B[4 + n % 4][:, 0:384], w[:, k, P * j:P * j + P], hT[:, k, 384 * tb:384 * tb + 384],
                                    start=(k == 0), stop=(k == KD - 1))
                last.then_inc(S["ub_ps"], 1)
            pe.wait_ge(S["ub_ps"], 12)
            pe.sem_inc(S["ring_used"], 1)
            pe.wait_ge(S["ub_sb"], 12)
            pe.wait_ge(S["w_table"], 1)
            for g in range(SG):
                n, gp, lo = g // 8, g // 2, SS * (g % 2)
                if g % 8 == 0 and n >= 2:
                    pe.wait_ge(S["kt_sb"], n - 1)
                for r in range(2):
                    last = T.matmul(B[4 + 2 * (n % 2) + g % 2][0:SQ, P * (gp % 4):P * (gp % 4) + P], bb[lo:lo + SS, r, gp, :],
                                    W[lo:lo + SS, r, gp, 0:L, :], start=(r == 0), stop=(r == 1))
                if g % 8 == 7:
                    last.then_inc(S["kt_ps"], 1)
            pe.wait_ge(S["wv_lo_done"], KD)
            pe.wait_ge(S["kt_sb"], SG // 8)
            for t in range(NT):
                if t >= 4:
                    pe.wait_ge(S["v_gelu"], t - 3)
                pe.wait_ge(S["hml_done"], t + 1)
                for k in range(KD):
                    o = B[4 + (12 + t) % 4][:, :]
                    T.matmul(o, hm_hi[:, t % 2, k], wv_hi[:, k], start=(k == 0), stop=False)
                    T.matmul(o, hm_hi[:, t % 2, k], wv_lo[:, k], start=False, stop=False)
                    last = T.matmul(o, hm_lo[:, t % 2, k], wv_hi[:, k], start=False, stop=(k == KD - 1))
                last.then_inc(S["v_ps"], 1)
            pe.wait_ge(S["v_ps"], NT)
            pe.sem_inc(S["ring_used"], 1)
            w = arrived(pe, ("in", 0))
            for n in range(12):
                j, tb = divmod(n, 3)
                pe.wait_ge(S["v_gelu"], min(NT, 6 + n))
                if n >= 4:
                    pe.wait_ge(S["u_sb"], n - 3)
                for k in range(KD):
                    last = T.matmul(B[4 + (21 + n) % 4][:, 0:384], w[:, k, P * j:P * j + P], hT[:, k, 384 * tb:384 * tb + 384],
                                    start=(k == 0), stop=(k == KD - 1))
                last.then_inc(S["uu_ps"], 1)
            pe.wait_ge(S["uu_ps"], 12)
            pe.sem_inc(S["ring_used"], 1)
            pe.wait_ge(S["u_in"], 16 * L)
            pe.wait_ge(S["u_sb"], 12)

            def g_turned(s):
                pe.wait_ge(S["g_nat"], s + 1)
                if s >= 2:
                    pe.wait_ge(S["g_sb"], s - 1)
                for r in range(2):
                    for i in range(SB):
                        last = T.transpose(B[2 + s % 2][:, P * (SB * r + i):P * (SB * r + i) + P],
                                           gnat[:, r, i].rearrange("p l q -> p (l q)"), ident[:, :])
                last.then_inc(S["g_ps"], 1)
            g_turned(0)
            for s in range(PR // SB):
                pe.wait_ge(S["g_sb"], s + 1)
                if s >= 2:
                    pe.wait_ge(S["v5_used"], s - 1)
                for r in range(2):
                    for i in range(SB):
                        for lo in (0, SS):
                            last = T.matmul(B[4 + 2 * (s % 2) + r][lo:lo + SS, CH * i:CH * i + CH], gt[:, r, i, lo:lo + SS],
                                            U[:, 2 * (SB * s + i) + lo // SS], start=True, stop=True)
                last.then_inc(S["v5_ps"], 1)
                if s + 1 < PR // SB:
                    g_turned(s + 1)
                modulation(4 + s)
                if s:
                    modulation_turned(3 + s)
            modulation_turned(11)
            def mix(t):
                if t >= 2:
                    pe.wait_ge(S["mix_sb"], t - 1)
                for h in range(GH):
                    last = T.matmul(B[t % 2][:, P * h:P * h + P], vn[:, t, P * h:P * h + P], (wT if t < TP else wS)[:, h],
                                    start=True, stop=True)
                last.then_inc(S["mix_ps"], 1)
            pe.wait_ge(S["v5_used"], PR // SB)
            pe.wait_ge(S["mt_placed"], 16 * L)
            pe.wait_ge(S["v_done"], 1)
            pe.wait_ge(S["ws_done"], 2)
            pe.wait_ge(S["ada_sb"], 12)
            mix(0)
            mix(1)
            pe.wait_ge(S["h_done"], 1)
            for g in range(SG):
                n, gp, lo = g // 6, g // 2, SS * (g % 2)
                if g % 6 == 0 and n >= 2:
                    pe.wait_ge(S["y_sb"], n - 1)
                o = B[4 + 2 * (n % 2) + g % 2][:, CH * (gp % 3):CH * (gp % 3) + CH]
                T.matmul(o, MT[:, g], U[:, g], start=True, stop=False)
                for r in range(2):
                    last = T.matmul(o, W[lo:lo + SS, r, gp, 1:L + 1, :], H[lo:lo + SS, r, gp], start=False, stop=(r == 1))
                if g % 6 == 5 or g == SG - 1:
                    last.then_inc(S["y_ps"], 1)
                    mix(n + 2)
            pe.wait_ge(S["wdiag"], 16 * DB)
            mix(TP)
            pe.wait_ge(S["g_sb"], PR // SB)
            for r in range(2):
                T.transpose(B[2][:, P * r:P * r + P], fs[:, r, 1:NC].rearrange("p b g -> p (b g)"), ident[:, :])
            for r in range(2):
                last = T.transpose(B[2][0:PR, P * (2 + r):P * (2 + r) + P], fs[:, r, 0], ident[:, :])
            last.then_inc(S["fs_t"], 1)
            pe.wait_ge(S["mix_sb"], NT)
            pe.wait_ge(S["mod_all"], 1)

            def spread(n, src, first, own, banks=0):
                if n >= 2:
                    pe.wait_ge(S["bc_sb"], min(n - 1, 6))
                if n % 2:
                    pe.wait_ge(S["wide_in"], n // 2 + 1)
                for k in range(KD):
                    col = src[:, first + k]
                    wide = col[:, 0:1].to_broadcast([P, P]) if n % 2 == 0 else own[:, P * k:P * k + P]
                    last = T.transpose(B[banks + 2 * (n % 2) + k // 4][:, P * (k % 4):P * (k % 4) + P], wide, ident[:, :])
                last.then_inc(S["bc_ps"], 1)
            pe.wait_ge(S["fs_sb"], 1)
            for n, (src, first) in enumerate(((Af, 0), (Af, 0), (modT, 24), (modT, 24), (modT, 16), (modT, 16))):
                spread(n, src, first, bc[:, n])
            w = arrived(pe, ("glu", 0))
            pe.wait_ge(S["y_sb"], 6)
            pe.wait_ge(S["y_in"], 16)
            for n in range(16):
                j, tb = divmod(n, 4)
                if n >= 4:
                    pe.wait_ge(S["sig_sb"], n - 3)
                for k in range(KG):
                    last = T.matmul(B[4 + n % 4][:, 0:288], w[:, k, P * j:P * j + P], yT[:, k, 288 * tb:288 * tb + 288],
                                    start=(k == 0), stop=(k == KG - 1))
                last.then_inc(S["glu_ps"], 1)
            pe.wait_ge(S["glu_ps"], 16)
            pe.sem_inc(S["ring_used"], 1)
            pe.wait_ge(S["bc_sb"], 6)
            pe.wait_ge(S["sig_sb"], 16)

            def h2_turn(t):
                pe.wait_ge(S["h2_rows"], t + 1)
                if t:
                    pe.wait_ge(S["h2t_sb"], t)
                turned(h2r[:, t % 2], t, 0).then_inc(S["h2t_ps"], 1)

            def router(t):
                pe.wait_ge(S["h2t_sb"], t + 1)
                for k in range(KD):
                    last = T.matmul(B[2][:, NE * t:NE * t + NE], h2T[:, t % 2, k], wr[:, k], start=(k == 0), stop=(k == KD - 1))
                last.then_inc(S["lg_ps"], 1)

            for t in range(NT):
                for h in range(2):
                    n = 2 * t + h
                    if n >= 4:
                        pe.wait_ge(S["wo_used"], n - 3)
                    pe.wait_ge(S["ml_done"], t + 1)
                    if t == 0:
                        pe.wait_ge(S["wo_lo_done"], 4 + 4 * h)
                    o = B[4 + n % 4][:, :]
                    for k in range(KD):
                        m_h, m_l = m_hi[:, t % 2, k], (u_lo if k < KG else b_lo)[:, k % KG, P * t:P * t + P]
                        T.matmul(o, m_h, wo_hi[h][:, k], start=(k == 0), stop=False)
                        T.matmul(o, m_h, wo_lo[h][:, k], start=False, stop=False)
                        last = T.matmul(o, m_l, wo_hi[h][:, k], start=False, stop=(k == KD - 1))
                    last.then_inc(S["wo_ps"], 1)
                if t >= 1:
                    h2_turn(t - 1)
                if t >= 2:
                    router(t - 2)
            pe.wait_ge(S["wo_ps"], 2 * NT)
            pe.sem_inc(S["ring_used"], 1)
            pe.sem_inc(S["ring_used"], 1)
            router(NT - 2)
            h2_turn(NT - 1)
            router(NT - 1)
            pe.wait_ge(S["wo_used"], 2 * NT)
            for n in (6, 7):
                spread(n, modT, 40, gfb[:, 1], banks=4)
            pe.wait_ge(S["consts"], 3)
            pe.wait_ge(S["oh_done"], 1)
            oh = ohb[:, :, :].rearrange("p t e -> p (t e)")
            T.matmul(B[3][:, 0:NT * NE], tri[:, :], oh, start=True, stop=False)
            for d in range(1, NT):
                T.matmul(B[3][:, NE * d:NT * NE], ones[:, :], oh[:, 0:(NT - d) * NE], start=False, stop=(d == NT - 1))
            for t in range(NT):
                last = T.matmul(B[2][:, 256:256 + NE], ones[:, :], oh[:, NE * t:NE * t + NE], start=(t == 0), stop=(t == NT - 1))
            last.then_inc(S["pre_ps"], 1)
            pe.wait_ge(S["num_done"], 1)
            for c in range(2 * NT):
                if c % 3 == 0:
                    pe.wait_ge(S["place_done"], c // 3 + 1)
                for r in range(2):
                    last = T.matmul(B[0][0:MAXB, 0:BN], num[:, r, c], at_place[:, c], start=(c == 0 and r == 0), stop=(c == 2 * NT - 1 and r == 1))
            last.then_inc(S["list_ps"], 1)
            pe.wait_ge(S["list_sb"], 1)
            pe.wait_ge(S["bc_sb"], 8)
            pe.wait_ge(S["tab_done"], 1)
            n_blocks = pe.value_load(nblk[0:1, 0:1], min_val=NE, max_val=NE + EXTRA)
            last_block = pe.value_load(nblk[0:1, 1:2], min_val=NE - 1, max_val=NE + EXTRA - 1)

            def turn_rows(i):
                pe.wait_ge(S["rows_in"], 32 * i + 32)
                for h in range(2):
                    for k in range(KD):
                        last = T.transpose(B[2 * h + k // 4][:, HB * (k % 4):HB * (k % 4) + HB], XR[:, h, P * k:P * k + P],
                                           ident[0:HB, 0:HB])
                    last.then_inc(S["xt2_ps"], 1)
            turn_rows(0)
            pe.wait_ge(S["xt2_ps"], 2)
            pe.sem_inc(S["rows_free"], 1)

            def products(o, w_h, w_l, k, first, last):
                T.matmul(o[:, 0:2 * BN], w_h, x_hl[:, k].rearrange("p r n -> p (r n)"), start=first, stop=False)
                return T.matmul(o[:, 0:BN], w_l, x_hl[:, k, 0], start=False, stop=last)

            def block_on_pe(i, more):
                pe.wait_ge(S["xt2_sb"], 2 * i + 2)
                for f in range(KE):
                    for m, (bank, name) in enumerate(((f % 2, "gate_ps"), (2 + f % 2, "up_ps"))):
                        n = 2 * f + m
                        pe.wait_ge(S["lo_done"], SLOTS * i + n + 1)
                        if m == 0:
                            pe.wait_ge(S["he_done"], KE * i + (f if f >= 2 else 1))
                        for k in range(KD):
                            last = products(B[bank], w_hi[n][:, P * k:P * k + P], w_lo[n][:, P * k:P * k + P], k, k == 0, k == KD - 1)
                        last.then_inc(S["w_used"], 1)
                pe.wait_ge(S["out_sb"], 2 * i + 1)
                for f in range(KE):
                    pe.wait_ge(S["lo_done"], SLOTS * i + 8 + f + 1)
                    pe.wait_ge(S["he_done"], KE * i + f + 2)
                    for h in range(2):
                        rows_h, rows_l = (he_hl[:, r, f, HB * h:HB * h + P] for r in range(2))
                        for n in range(2):
                            o = B[4 + 2 * h + n][:, :]
                            w_h, w_l = w_hi[8 + f][:, 512 * n:512 * n + 512], w_lo[8 + f][:, 512 * n:512 * n + 512]
                            T.matmul(o, rows_h, w_h, start=(f == 0), stop=False)
                            T.matmul(o, rows_h, w_l, start=False, stop=False)
                            last = T.matmul(o, rows_l, w_h, start=False, stop=(f == KE - 1))
                            if f == KE - 1 and not (h == 1 and n == 1):
                                last.then_inc(S["down_ps"], 1)
                    last.then_inc(S["w_used"], 1)
                    if f == 0 and more:
                        pe.wait_ge(S["he_done"], KE * i + KE + 1)
                        turn_rows(i + 1)
                    if f == 1 and more:
                        pe.wait_ge(S["xt2_ps"], 2 * i + 4)
                        pe.sem_inc(S["rows_free"], 1)
            with pe.Fori(0, last_block) as i:
                block_on_pe(i, True)
            block_on_pe(last_block, False)

        @block.vector
        def _(dve):
            v = nc.vector
            lk = chained(dve, S["chain_v"])

            def tt(o, a, b, op):
                return v.tensor_tensor(o, a, b, op)

            dve.wait_ge(S["ws_done"], 1)
            v.memset(wT[64:P, :, 0:64], 0.0).then_inc(S["ws_done"], 1)
            def cmul(o, x, y, t):
                lk(tt(t[0], x[0], y[0], ALU.mult))
                lk(tt(t[1], x[1], y[1], ALU.mult))
                lk(tt(o[0], t[0], t[1], ALU.subtract))
                lk(tt(t[0], x[0], y[1], ALU.mult))
                lk(tt(t[1], x[1], y[0], ALU.mult))
                lk(tt(o[1], t[0], t[1], ALU.add))

            def modulation(c):
                dve.wait_ge(S["ada_ps"], c + 1)
                tt(modT[:, 4 * c:4 * c + 4], ada_bank(c)[:, 0:4 * NC].rearrange("p (j c) -> p j c", j=4),
                   vecT[:, 4 * c:4 * c + 4].unsqueeze(2).to_broadcast([P, 4, NC]), ALU.add).then_inc(S["ada_sb"], 1)

            def x_normalised(t):
                dve.wait_ge(S["sq_done"], t + 1)
                lk(v.reciprocal(st[:, 4, t:t + 1], st[:, 1, t:t + 1]))
                v.tensor_scalar(xin[t % 8], xin[t % 8], st[:, 4, t:t + 1], None, ALU.mult).then_inc(S["x_norm"], 1)
            x_normalised(0)
            x_normalised(1)
            dve.wait_ge(S["cond_done"], 2)
            for c in range(4):
                modulation(c)
                x_normalised(c + 2)
            dve.wait_ge(S["ada_sb"], 4)
            v.scalar_tensor_tensor(out=Am[:, :, :], in0=modT[:, 8:16], scalar=1.0,
                                   in1=vecT[:, 48:56].unsqueeze(2).to_broadcast([P, KD, NC]),
                                   op0=ALU.add, op1=ALU.mult).then_inc(S["am_done"], 1)
            for t in range(NT):
                dve.wait_ge(S["xt_ps"], t + 1)
                dve.wait_ge(S["am_done"], 1)
                if t < TP:
                    for k in range(4):
                        last = v.tensor_scalar(hT[:, k, P * t:P * t + P], B[2 * (t % 2) + k // 4][:, P * (k % 4):P * (k % 4) + P],
                                               Am[:, k, 0:1], modT[:, k, 0:1], ALU.mult, ALU.add)
                else:
                    for k in range(KD):
                        src = B[2 * (t % 2) + k // 4][:, P * (k % 4):P * (k % 4) + P].rearrange("p (b s) -> p b s", b=DB)
                        o = hT[:, k, P * t:P * t + P].rearrange("p (b s) -> p b s", b=DB)
                        lk(tt(o, src, Am[:, k, 1:NC].unsqueeze(2).to_broadcast([P, DB, DS]), ALU.mult))
                        last = tt(o, o, modT[:, k, 1:NC].unsqueeze(2).to_broadcast([P, DB, DS]), ALU.add)
                last.then_inc(S["ht_sb_v"], 1)
                if t + 6 < NT:
                    x_normalised(t + 6)
            dve.wait_ge(S["cond_t"], 3)
            dve.wait_ge(S["dt_in"], 1)
            tt(q[:, 2], aT[:, 0], q[:, 1], ALU.mult).then_inc(S["mg_in"], 1)
            lk(tt(q[:, 3], aT[:, 1], q[:, 1], ALU.mult))
            lk(v.tensor_scalar(q[:, 10], q[:, 3], 1.0 / (2 * PI), None, ALU.mult))
            lk(v.tensor_copy(qi[:, :], q[:, 10]))
            lk(v.tensor_copy(q[:, 10], qi[:, :]))
            for part in (TWO_PI_HI, TWO_PI_MID, TWO_PI_LO):
                lk(v.scalar_tensor_tensor(out=q[:, 3], in0=q[:, 10], scalar=-part, in1=q[:, 3], op0=ALU.mult, op1=ALU.add))

            def wrap(x):
                for op, lim, add in ((ALU.is_gt, PI, -2 * PI), (ALU.is_lt, -PI, 2 * PI)):
                    lk(v.tensor_scalar(q[:, 10], x, lim, add, op, ALU.mult))
                    lk(tt(x, x, q[:, 10], ALU.add))
            wrap(q[:, 3])
            lk(v.tensor_scalar(q[:, 7], q[:, 3], PI / 2, None, ALU.add))
            wrap(q[:, 7])
            lk(v.tensor_scalar(q[:, 7], q[:, 7], 3.1415925, -3.1415925, ALU.min, ALU.max))
            v.tensor_scalar(q[:, 6], q[:, 3], 3.1415925, -3.1415925, ALU.min, ALU.max).then_inc(S["mg_in"], 1)

            dve.wait_ge(S["dt_in"], 5)
            lk(v.memset(LP[:, 0, :, 0], 1.0))
            lk(v.memset(LP[:, 1, :, 0], 0.0))
            lk(tt(LP[:, 0, :, 1], q[:, 4], q[:, 9], ALU.mult))
            lk(tt(LP[:, 1, :, 1], q[:, 4], q[:, 8], ALU.mult))
            n = 1
            while n < L:
                x = (LP[:, 0, :, 1:n + 1], LP[:, 1, :, 1:n + 1])
                y = tuple(LP[:, r, :, n:n + 1].to_broadcast([P, PR, n]) for r in range(2))
                o = (LP[:, 0, :, n + 1:2 * n + 1], LP[:, 1, :, n + 1:2 * n + 1])
                t = tuple(wtmp2[:, :, r, 0:n] for r in range(2))
                cmul(o, x, y, t)
                n *= 2
            for r in range(2):
                for s in range(L):
                    lk(v.tensor_copy(LR[:, r, :, s], LP[:, r, :, L - 1 - s]))
            lk(v.tensor_copy(q[:, 11], q[:, 9]))
            lk(v.tensor_copy(q[:, 12], q[:, 8]))

            def square(c, s, t0, t1):
                lk(tt(t0, c, c, ALU.mult))
                lk(tt(t1, s, s, ALU.mult))
                lk(v.scalar_tensor_tensor(out=s, in0=s, scalar=2.0, in1=c, op0=ALU.mult, op1=ALU.mult))
                lk(tt(c, t0, t1, ALU.subtract))
                lk(tt(t0, c, c, ALU.mult))
                lk(tt(t1, s, s, ALU.mult))
                lk(tt(t0, t0, t1, ALU.add))
                lk(v.tensor_scalar(t0, t0, -0.5, 1.5, ALU.mult, ALU.add))
                lk(tt(c, c, t0, ALU.mult))
                lk(tt(s, s, t0, ALU.mult))
            for _ in range(3):
                square(q[:, 11], q[:, 12], q[:, 13], q[:, 14])
            lk(v.tensor_scalar(q[:, 13], LP[:, 0, :, 1], -1.0, None, ALU.add))
            lk(tt(q[:, 14], aT[:, 0], aT[:, 0], ALU.mult))
            lk(tt(q[:, 15], aT[:, 1], aT[:, 1], ALU.mult))
            lk(tt(q[:, 14], q[:, 14], q[:, 15], ALU.add))
            lk(v.reciprocal(q[:, 14], q[:, 14]))
            lk(tt(q[:, 15], q[:, 13], aT[:, 0], ALU.mult))
            lk(tt(q[:, 16], LP[:, 1, :, 1], aT[:, 1], ALU.mult))
            lk(tt(q[:, 15], q[:, 15], q[:, 16], ALU.add))
            lk(tt(q[:, 15], q[:, 15], q[:, 14], ALU.mult))
            lk(tt(q[:, 16], LP[:, 1, :, 1], aT[:, 0], ALU.mult))
            lk(tt(q[:, 17], q[:, 13], aT[:, 1], ALU.mult))
            lk(tt(q[:, 16], q[:, 16], q[:, 17], ALU.subtract))
            lk(tt(q[:, 16], q[:, 16], q[:, 14], ALU.mult))
            coef = tuple(q[:, 15 + r].unsqueeze(2).to_broadcast([P, PR, SQ]) for r in range(2))
            cmul((bb[:, 0], bb[:, 1]), (bnat[:, 0], bnat[:, 1]), coef,
                 tuple(wtmp2[:, :, r, :] for r in range(2)))
            wide = [P, PR, L + 1, SQ]
            lam = tuple(LP[:, r].unsqueeze(3).to_broadcast(wide) for r in range(2))
            cx = tuple(cc[:, r].unsqueeze(2).to_broadcast(wide) for r in range(2))
            lk(tt(wtmp, lam[0], cx[0], ALU.mult))
            lk(tt(wtmp2, lam[1], cx[1], ALU.mult))
            lk(tt(W[:, 0], wtmp, wtmp2, ALU.subtract))
            lk(tt(wtmp, lam[1], cx[0], ALU.mult))
            lk(tt(wtmp2, lam[0], cx[1], ALU.mult))
            v.scalar_tensor_tensor(out=W[:, 1], in0=wtmp, scalar=-1.0, in1=wtmp2, op0=ALU.mult,
                                   op1=ALU.subtract).then_inc(S["w_table"], 1)

            for k in range(KD):
                dve.wait_ge(S["wv_hi_done"], k + 1)
                tt(wv_lo[:, k], wv_raw[:, k], wv_hi[:, k], ALU.subtract).then_inc(S["wv_lo_done"], 1)
            def v_columns_low(t):
                dve.wait_ge(S["hmh_done"], t + 1)
                tt(hm_lo[:, t % 2], hT[:, :, P * t:P * t + P], hm_hi[:, t % 2], ALU.subtract).then_inc(S["hml_done"], 1)
            for r in range(2):
                dve.wait_ge(S[f"ub_out{r}"], 16 * KG // 2)
            v_columns_low(0)
            v_columns_low(1)
            dve.wait_ge(S["kt_sb"], 4)
            dve.wait_ge(S["ld_s5"], 16 * 9)
            dd = dtmp[0:SQ]
            lk(tt(dd, ident[0:SQ, 0:SQ].unsqueeze(1).to_broadcast([SQ, SG, SQ]), dq[:, :].unsqueeze(2).to_broadcast([SQ, SG, SQ]), ALU.mult))
            tt(KT[:, :, 0:SQ], KT[:, :, 0:SQ], dd, ALU.add).then_inc(S["kt_done"], 1)
            for t in range(NT):
                if t + 2 < NT:
                    v_columns_low(t + 2)
                dve.wait_ge(S["v_gelu"], t + 1)
                lk(v.bn_stats(bn6[:, t % 2], vn[:, t]))
                lk(v.bn_aggr(mv[:, t], bn6[:, t % 2]))
                v.tensor_copy(st[:, 3, t:t + 1], mv[:, t, 1:2]).then_inc(S["stats_v"], 1)
            dve.wait_ge(S["std_v"], 1)
            dve.wait_ge(S["ld_gain"], 32)
            lk(v.reciprocal(st[:, 5], st[:, 2]))
            for t in range(NT):
                lk(v.tensor_scalar(vn[:, t], vn[:, t], mv[:, t, 0:1], st[:, 5, t:t + 1], ALU.subtract, ALU.mult))
                last = tt(vn[:, t], vn[:, t], vgain, ALU.mult)
            last.then_inc(S["v_done"], 1)
            E = tuple(H[:, r, :, 0:P] for r in range(2))
            lk(v.memset(EH[:, 0, :, 0], 1.0))
            lk(v.memset(EH[:, 1, :, 0], 0.0))
            n = 1
            while n < P:
                u = tuple(q[:, 11 + r].unsqueeze(2).to_broadcast([P, PR, n]) for r in range(2))
                if n == SS:
                    dve.sem_inc(S["e_done"], 1)
                    dve.wait_ge(S["uu_ps"], 12)
                    t0, t1 = (area("RA", 4608 + 1024 * r, PR, n) for r in range(2))
                    out = tuple(E[r][:, :, n:2 * n] for r in range(2))
                else:
                    t0, t1 = (area("RD", 1024 * r, PR, n) for r in range(2))
                    out = tuple(EH[:, r, :, n:2 * n] for r in range(2))
                cmul(out, tuple(EH[:, r, :, 0:n] for r in range(2)), u, (t0, t1))
                if n < SS:
                    square(q[:, 11], q[:, 12], q[:, 13], q[:, 14])
                n *= 2
            dve.sem_inc(S["e_out"], 1)
            dve.wait_ge(S["e_out"], 3)
            for s in range(PR // SB):
                sl = slice(SB * s, SB * s + SB)
                Er, Ei = E[0][:, sl], E[1][:, sl]
                dve.wait_ge(S["v5_ps"], s + 1)
                Vr, Vi = (B[4 + 2 * (s % 2) + r][:, 0:SB * CH].rearrange("p (i c) -> p i c", i=SB) for r in range(2))
                lk(v.tensor_copy(H[:, 0, sl, CP:CH], Vr[:, :, CP:CH]))
                lk(v.tensor_copy(H[:, 1, sl, CP:CH], Vi[:, :, CP:CH]))
                lk(tt(tm[:, 0], Er, Vr[:, :, 0:CP], ALU.mult))
                lk(tt(tm[:, 1], Ei, Vi[:, :, 0:CP], ALU.mult))
                lk(tt(tm[:, 2], Er, Vi[:, :, 0:CP], ALU.mult))
                tt(tm[:, 3], Ei, Vr[:, :, 0:CP], ALU.mult).then_inc(S["v5_used"], 1)
                lk(tt(tm[:, 0], tm[:, 0], tm[:, 1], ALU.add))
                dve.wait_ge(S["v5_used"], s + 1)
                lk(tt(tm[:, 2], tm[:, 2], tm[:, 3], ALU.subtract))
                for i in range(SB):
                    decay = q[:, 5, SB * s + i:SB * s + i + 1].to_broadcast([P, CP])
                    lk(v.tensor_tensor_scan(tm[:, 1, i], decay, tm[:, 0, i], 0.0, ALU.mult, ALU.add))
                    lk(v.tensor_tensor_scan(tm[:, 3, i], decay, tm[:, 2, i], 0.0, ALU.mult, ALU.add))
                lk(tt(tm[:, 0], Er, tm[:, 1], ALU.mult))
                lk(tt(tm[:, 2], Ei, tm[:, 3], ALU.mult))
                lk(tt(tm[:, 4], Er, tm[:, 3], ALU.mult))
                lk(tt(tm[:, 5], Ei, tm[:, 1], ALU.mult))
                lk(tt(H[:, 0, sl, 1:CP], tm[:, 0, :, 0:CP - 1], tm[:, 2, :, 0:CP - 1], ALU.subtract))
                lk(tt(H[:, 1, sl, 1:CP], tm[:, 4, :, 0:CP - 1], tm[:, 5, :, 0:CP - 1], ALU.add))
                lk(tt(fs[:, 0, 0, sl], tm[:, 0, :, CP - 1], tm[:, 2, :, CP - 1], ALU.subtract))
                lk(tt(fs[:, 1, 0, sl], tm[:, 4, :, CP - 1], tm[:, 5, :, CP - 1], ALU.add))
                if s:
                    modulation(3 + s)
            modulation(11)
            dve.wait_ge(S["ada_sb"], 12)
            v.scalar_tensor_tensor(out=Af[:, :, :], in0=modT[:, 32:40], scalar=1.0,
                                   in1=vecT[:, 56:64].unsqueeze(2).to_broadcast([P, KD, NC]),
                                   op0=ALU.add, op1=ALU.mult).then_inc(S["mod_all"], 1)
            lk(v.memset(H[:, :, :, 0], 0.0))
            lam8 = tuple(LP[:, r, :, L:L + 1].to_broadcast([P, PR, DB]) for r in range(2))
            hs = tuple(h0[:, r].rearrange("p b g -> p g b") for r in range(2))
            mid = tuple(smp[:, r] for r in range(2))
            ts = tuple(smp[:, 2 + r] for r in range(2))
            cmul(mid, hs, lam8, ts)
            for r in range(2):
                lk(tt(mid[r], mid[r], H[:, r, :, CP:CH:2], ALU.add))
            out = tuple(smp[:, 4 + r] for r in range(2))
            cmul(out, mid, lam8, ts)
            for r in range(2):
                lk(tt(fs[:, r, 1:NC].rearrange("p b g -> p g b"), out[r], H[:, r, :, CP + 1:CH:2], ALU.add))
            for r in range(2):
                lk(v.tensor_copy(H[:, r, :, CP:CH:2], hs[r]))
                last = v.tensor_copy(H[:, r, :, CP + 1:CH:2], mid[r])
            last.then_inc(S["h_done"], 1)
            for t in range(NT):
                dve.wait_ge(S["mix_ps"], t + 1)
                if t:
                    dve.wait_ge(S["mix_sb"], t)
                src = B[t % 2][:, :]
                if t < TP:
                    lk(tt(mtm, src.rearrange("p (h i) -> p h i", h=GH), bsp, ALU.add))
                else:
                    for h in range(GH):
                        lk(tt(mtm[:, h].rearrange("p (b s) -> p b s", b=DB), src[:, P * h:P * h + P].rearrange("p (b s) -> p b s", b=DB),
                              bsp[:, h, 0:DS].unsqueeze(1).to_broadcast([P, DB, DS]), ALU.add))
                tt(uT[:, :, P * t:P * t + P], uT[:, :, P * t:P * t + P], mtm, ALU.mult).then_inc(S["mix_sb"], 1)
            def wo_low(piece):
                h, k = WO_PIECES[piece]
                dve.wait_ge(S["wo_hi_done"], piece + 1)
                tt(wo_lo[h][:, k:k + 2], wo_raw[h][:, k:k + 2], wo_hi[h][:, k:k + 2], ALU.subtract).then_inc(S["wo_lo_done"], 1)

            def m_low(t):
                dve.wait_ge(S["mh_done"], t + 1)
                sl = slice(P * t, P * t + P)
                tt(u_lo[:, :, sl], uT[:, :, sl], m_hi[:, t % 2, 0:KG], ALU.subtract)
                tt(b_lo[:, :, sl], bT[:, :, sl], m_hi[:, t % 2, KG:KD], ALU.subtract).then_inc(S["ml_done"], 1)
            dve.wait_ge(S["v_out"], 16)
            for n in range(16):
                j, tb = divmod(n, 4)
                dve.wait_ge(S["sig_sb"], n + 1)
                o = bT[:, j].rearrange("p (c s) -> p s c", s=L)[:, 2 * tb:2 * tb + 2]
                tt(o, ytm[:, n % 2].rearrange("p (s c) -> p s c", s=2),
                   yT[:, j, 288 * tb:288 * tb + 288].rearrange("p (s c) -> p s c", s=2), ALU.mult).then_inc(S["b_done"], 1)
                if 4 <= n < 10:
                    wo_low(n - 4)
            m_low(0)
            wo_low(6)
            wo_low(7)
            m_low(1)
            dve.wait_ge(S["ld_xres"], 32)
            dve.wait_ge(S["bc_sb"], 6)
            dve.wait_ge(S["y_out"], 16 * L)
            for t in range(NT):
                c = 0 if t < TP else 1
                for h in range(2):
                    n = 2 * t + h
                    sl = slice(512 * h, 512 * h + 512)
                    dve.wait_ge(S["wo_ps"], n + 1)
                    tt(wtm[:, h], B[4 + n % 4][:, :], bc[:, 4 + c, sl], ALU.mult).then_inc(S["wo_used"], 1)
                    dve.wait_ge(S["wo_used"], n + 1)
                    last = tt(X1[:, t, sl], X1[:, t, sl], wtm[:, h], ALU.add)
                    if h == 0:
                        lk(last)
                last.then_inc(S["x1_done"], 1)
                dve.wait_ge(S["ss_done"], t + 1)
                lk(v.reciprocal(st[:, 4, t:t + 1], st[:, 1, t:t + 1]))
                if t >= 2:
                    dve.wait_ge(S[f"h2_out{t % 2}"], 16 * (t // 2))
                    dve.wait_ge(S["h2t_ps"], t - 1)
                lk(v.scalar_tensor_tensor(out=h2r[:, t % 2], in0=X1[:, t], scalar=st[:, 4, t:t + 1], in1=bc[:, c],
                                          op0=ALU.mult, op1=ALU.mult))
                tt(h2r[:, t % 2], h2r[:, t % 2], bc[:, 2 + c], ALU.add).then_inc(S["h2_rows"], 1)
                if t + 2 < NT:
                    m_low(t + 2)
            def low_parts(i, *slots):
                for n in slots:
                    dve.wait_ge(S["hi_done"], SLOTS * i + n + 1)
                    tt(w_lo[n], w_raw[n], w_hi[n], ALU.subtract).then_inc(S["lo_done"], 1)

            dve.wait_ge(S["lg_ps"], NT)
            dve.wait_ge(S["v_out"], 16)
            r3 = [rt[:, n].rearrange("p (t e) -> p t e", e=NE) for n in range(16)]
            r4 = [rt[:, n].rearrange("p (g e) -> p g e", e=EG) for n in range(16)]
            n9 = small[:, 0:8]
            col = lambda n: n9[:, n]
            spread = lambda x: x.unsqueeze(2).to_broadcast([P, NT, NE])
            lk(tt(r3[0], B[2][:, 0:NT * NE].rearrange("p (t e) -> p t e", e=NE),
                  brt[:, :].unsqueeze(1).to_broadcast([P, NT, NE]), ALU.add))
            lk(v.tensor_reduce(col(0), r3[0], AX.X, ALU.max))
            tt(r3[0], r3[0], spread(col(0)), ALU.subtract).then_inc(S["e_in"], 1)
            dve.wait_ge(S["exp_done"], 1)
            lk(v.tensor_reduce(col(1), r3[1], AX.X, ALU.add))
            lk(v.reciprocal(col(1), col(1)))
            lk(tt(r3[1], r3[1], spread(col(1)), ALU.mult))

            def rank(o, x, t, w):
                for i in range(4):
                    lk(v.memset(o[:, :, i], float(i)))
                for d in (1, 2, 3):
                    lk(tt(t[:, :, 0:4 - d], x[:, :, d:4], x[:, :, 0:4 - d], ALU.is_gt))
                    lk(tt(o[:, :, 0:4 - d], o[:, :, 0:4 - d], t[:, :, 0:4 - d], ALU.add))
                    lk(tt(o[:, :, d:4], o[:, :, d:4], t[:, :, 0:4 - d], ALU.subtract))
            rank(r4[2], r4[1], r4[3], NT * NG)
            lk(v.tensor_scalar(rt[:, 4], rt[:, 2], 1.5, None, ALU.is_lt))
            lk(tt(rt[:, 5], rt[:, 4], rt[:, 1], ALU.mult))
            gsum = small[:, 8:12].rearrange("p a b -> p (a b)")
            g3 = [small[:, 8 + 4 * n:12 + 4 * n].rearrange("p a b -> p (a b)").rearrange("p (t g) -> p t g", g=NG) for n in range(3)]
            lk(v.tensor_reduce(gsum, r4[5], AX.X, ALU.add))
            rank(g3[1], g3[0], g3[2], NT)
            g1f = small[:, 12:16].rearrange("p a b -> p (a b)")
            lk(v.tensor_scalar(g1f, g1f, 0.5, None, ALU.is_lt))
            gsel = g1f.unsqueeze(2).to_broadcast([P, NT * NG, EG])
            lk(v.tensor_scalar(rt[:, 6], rt[:, 2], 0.5, None, ALU.is_lt))
            lk(tt(rt[:, 7], rt[:, 4], rt[:, 6], ALU.subtract))
            for n in (6, 7):
                lk(tt(r4[n], r4[n], gsel, ALU.mult))
            tt(ohb[:, :, :], r3[6], r3[7], ALU.add).then_inc(S["oh_done"], 1)
            dve.wait_ge(S["zeroed"], 9)
            dve.wait_ge(S["pre_ps"], 1)
            cnt = B[2][:, 256:256 + NE]
            nb, cum, shift = rt[:, 10, 0:NE], rt[:, 11, 0:NE], rt[:, 12, 0:NE]
            lk(v.tensor_scalar(nb, cnt, BN + 0.5, None, ALU.is_gt))
            for r in range(2, ROUNDS):
                lk(v.tensor_scalar(cum, cnt, r * BN + 0.5, None, ALU.is_gt))
                lk(tt(nb, nb, cum, ALU.add))
            lk(v.memset(shift, 1.0))
            lk(v.tensor_tensor_scan(cum, shift, nb, 0.0, ALU.mult, ALU.add))
            lk(tt(shift, cum, nb, ALU.subtract))
            lk(v.tensor_scalar(shift, shift, NE - 1.0, float(BN), ALU.add, ALU.mult))
            lk(tt(shift, shift, ebase[:, :], ALU.subtract))
            wide = lambda x: x.unsqueeze(1).to_broadcast([P, NT, NE])
            before = B[3][:, 0:NT * NE].rearrange("p (t e) -> p t e", e=NE)
            lk(v.tensor_scalar(r3[9], before, BN - 0.5, None, ALU.is_gt))
            lk(tt(r3[9], r3[9], wide(shift), ALU.mult))
            lk(tt(r3[9], r3[9], before, ALU.add))
            lk(tt(r3[9], r3[9], wide(ebase[:, :]), ALU.add))
            for k in range(2):
                lk(tt(rt[:, 8], rt[:, 6 + k], rt[:, 9], ALU.mult))
                lk(v.tensor_reduce(col(5 + k), r3[8], AX.X, ALU.add))
            pos = small[:, 5:7].rearrange("p k t -> p (k t)")
            by = lambda x, n: x.unsqueeze(2).to_broadcast([P, 2 * NT, n])
            of = lambda x, n: x.unsqueeze(1).to_broadcast([P, 2 * NT, n])
            lk(tt(in_block, by(pos, MAXB), of(firsts[:, :], MAXB), ALU.is_ge))
            lk(v.tensor_reduce(blk, in_block, AX.X, ALU.add))
            lk(v.scalar_tensor_tensor(out=pos, in0=blk, scalar=-float(BN), in1=pos, op0=ALU.mult, op1=ALU.add))
            lk(tt(in_block, of(blocks[:, :], MAXB), by(blk, MAXB), ALU.is_equal))
            lk(v.tensor_scalar(num[:, 0], in_block, tok_low[:, 0:1], None, ALU.mult))
            tt(num[:, 1], in_block, by(tok_high[:, :, :].rearrange("p k t -> p (k t)"), MAXB), ALU.mult).then_inc(S["num_done"], 1)
            for c in range(0, 2 * NT, 3):
                tt(at_place[:, c:c + 3], places[:, :].unsqueeze(1).to_broadcast([P, 3, BN]),
                   pos[:, c:c + 3].unsqueeze(2).to_broadcast([P, 3, BN]), ALU.is_equal).then_inc(S["place_done"], 1)
            low_parts(0, 0, 1)
            dve.wait_ge(S["list_ps"], 1)
            v.tensor_copy(list_i, B[0][0:MAXB, 0:BN]).then_inc(S["list_sb"], 1)
            lk(v.scalar_tensor_tensor(out=pos, in0=blk, scalar=float(BN), in1=pos, op0=ALU.mult, op1=ALU.add))
            lk(v.tensor_copy(lst[:, :, :].rearrange("p k t -> p (k t)"), pos))
            for k in range(2):
                lk(tt(rt[:, 8], rt[:, 6 + k], rt[:, 1], ALU.mult))
                lk(v.tensor_reduce(col(2 + k), r3[8], AX.X, ALU.add))
            lk(tt(col(4), col(2), col(3), ALU.add))
            lk(v.reciprocal(col(4), col(4)))
            for k in range(2):
                lk(tt(gates[:, k], col(2 + k), col(4), ALU.mult))
            big = rt[0:1, 13:15].rearrange("p a b -> p (a b)")[:, 0:EXTRA * NE].rearrange("p (x e) -> p x e", e=NE)
            lk(tt(big, cum[0:1].unsqueeze(1).to_broadcast([1, EXTRA, NE]), iot[:, :].unsqueeze(2).to_broadcast([1, EXTRA, NE]), ALU.is_le))
            lk(v.tensor_copy(b64[:, 0:NE], etab[:, :]))
            lk(v.tensor_reduce(b64[:, NE:MAXB], big, AX.X, ALU.add))
            lk(v.tensor_scalar(b64[:, NE:MAXB], b64[:, NE:MAXB], NE - 1.0, None, ALU.min))
            lk(v.tensor_copy(tab[:, 0:MAXB], b64[:, 0:MAXB]))
            lk(v.tensor_scalar(shift[0:1, 0:1], cum[0:1, NE - 1:NE], float(NE), None, ALU.add))
            lk(v.tensor_scalar(shift[0:1, 1:2], cum[0:1, NE - 1:NE], float(NE - 1), None, ALU.add))
            v.tensor_copy(nblk[:, :], shift[0:1, 0:2]).then_inc(S["tab_done"], 1)
            dve.wait_ge(S["tab_done"], 1)
            n_blocks = dve.value_load(nblk[0:1, 0:1], min_val=NE, max_val=NE + EXTRA)
            last_block = dve.value_load(nblk[0:1, 1:2], min_val=NE - 1, max_val=NE + EXTRA - 1)
            dve.sem_inc(S["he_done"], 1)
            dve.sem_inc(S["out_sb"], 1)
            dve.sem_inc(S["out_d"], 16)

            def both_halves(o, bank):
                return v.tensor_reduce(o, bank[:, 0:2 * BN].rearrange("p (r n) -> p n r", r=2), AX.X, ALU.add)

            def columns_low(i, h):
                dve.wait_ge(S["xh_done"], 2 * i + h + 1)
                for m in range(2):
                    sl = slice(HB * h, HB * h + HB)
                    last = tt(x_hl[:, 4 * m:4 * m + 4, 1, sl], B[2 * h + m][:, 0:4 * HB].rearrange("p (k n) -> p k n", k=4),
                              x_hl[:, 4 * m:4 * m + 4, 0, sl], ALU.subtract)
                last.then_inc(S["xt2_sb"], 1)

            def block_on_dve(i, more):
                for f in range(KE):
                    here = (i, 8 + 2 * f) if f < 2 else (i + 1, 2 * f - 4)
                    split = f < 2 or more
                    dve.wait_ge(S["w_used"], SLOTS * i + 2 * f + 1)
                    both_halves(gate[:, f % 2], B[f % 2]).then_inc(S["gate_done"], 1)
                    if split:
                        low_parts(*here)
                    dve.wait_ge(S["w_used"], SLOTS * i + 2 * f + 2)
                    both_halves(up[:, f % 2], B[2 + f % 2]).then_inc(S["up_done"], 1)
                    dve.wait_ge(S["up_done"], KE * i + f + 1)
                    dve.wait_ge(S["silu_done"], KE * i + f + 1)
                    tt(he[:, f % 2], sil[:, f % 2], up[:, f % 2], ALU.mult).then_inc(S["he_full"], 1)
                    tt(he_hl[:, 0, f, 0:BN], sil[:, f % 2], up[:, f % 2], ALU.mult).then_inc(S["he_full"], 1)
                    dve.wait_ge(S["he_full"], 2 * (KE * i + f) + 2)
                    tt(he_hl[:, 1, f, 0:BN], he[:, f % 2], he_hl[:, 0, f, 0:BN], ALU.subtract).then_inc(S["he_done"], 1)
                    if split:
                        low_parts(here[0], here[1] + 1)
                if more:
                    low_parts(i + 1, 4)
                    columns_low(i + 1, 0)
                    columns_low(i + 1, 1)
                    low_parts(i + 1, 5, 6, 7)
                dve.wait_ge(S["out_d"], 32 * i + 16)
                for h in range(2):
                    for n in range(2):
                        if h == 1 and n == 1:
                            dve.wait_ge(S["w_used"], SLOTS * i + SLOTS)
                        else:
                            dve.wait_ge(S["down_ps"], 3 * i + 2 * h + n + 1)
                        last = v.tensor_copy(OUT[:, h, 512 * n:512 * n + 512], B[4 + 2 * h + n][0:HB, :])
                    last.then_inc(S["out_sb"], 1)
            for r in range(2):
                lk(v.tensor_scalar(he_hl[:, r, :, BN:], ident[:, 0:P - HB].unsqueeze(1).to_broadcast([P, KE, P - HB]), 0.0, None, ALU.mult))
            low_parts(0, *range(2, 6))
            for h in range(2):
                columns_low(0, h)
            low_parts(0, 6, 7)
            with dve.Fori(0, last_block) as i:
                block_on_dve(i, True)
            block_on_dve(last_block, False)
            dve.wait_ge(S["ld_gain"], 48)
            dve.wait_ge(S["bc_sb"], 8)

            def combined(t):
                dve.wait_ge(S["comb_scaled"], t + 1)
                y0, y1 = YA[:, t % 4, 0], YA[:, t % 4, 1]
                lk(v.scalar_tensor_tensor(out=y0, in0=y1, scalar=gates[:, 1, t:t + 1], in1=y0, op0=ALU.mult, op1=ALU.add))
                lk(tt(y0, y0, gfb[:, 0 if t < TP else 1], ALU.mult))
                tt(X1[:, t], X1[:, t], y0, ALU.add).then_inc(S["fin_ss"], 1)
            combined(0)
            for t in range(NT):
                if t + 1 < NT:
                    combined(t + 1)
                dve.wait_ge(S["fin_ss"], t + 1)
                dve.sem_inc(S["comb_used"], 1)
                dve.wait_ge(S["fin_rs"], t + 1)
                v.reciprocal(st[:, 4, t:t + 1], st[:, 1, t:t + 1]).then_inc(S["rs_done"], 1)


_INS = ['x_prompt', 'x_sample', 'c_prompt', 'c_sample', 'state_s5_re', 'state_s5_im', 'w_ada', 'b_ada', 'g_norm_mix',
        'g_norm_ffn', 'w_in', 'gmlp_v_gain', 'gmlp_w_spatial', 'gmlp_b_spatial', 's5_a_re', 's5_a_im', 's5_log_dt',
        's5_b_re', 's5_b_im', 's5_c_re', 's5_c_im', 's5_d', 's5_w_glu', 's5_b_glu', 'w_out', 'w_router', 'b_router',
        'w_gate', 'w_up', 'w_down', 'g_final']
_OUTS = [(1, SEQ, D), (DB, DS, D), (1, 1, SG, SS), (1, 1, SG, SS), (1, DB, SG, SS), (1, DB, SG, SS), (1, DB, DS, GW)]


def kernel(**inputs):
    import numpy as _np
    import concourse.bacc as _bacc
    from concourse import mybir as _mybir
    from concourse.bass_utils import run_bass_kernel_spmd as _run

    nc = _bacc.Bacc("TRN2", target_bir_lowering=False, num_devices=1)
    arrays, args = {}, []
    for name in _INS:
        a = _np.ascontiguousarray(inputs[name])
        arrays[f"in_{name}_dram"] = a
        args.append(nc.dram_tensor(f"in_{name}_dram", a.shape, _mybir.dt.from_np(a.dtype), kind="ExternalInput").ap())
    for i, shape in enumerate(_OUTS):
        args.append(nc.dram_tensor(f"out_{i}_dram", shape, _mybir.dt.float32, kind="ExternalOutput").ap())
    hybrid_step(nc, *args)
    r = _run(nc, [arrays], core_ids=[0])
    return tuple(r.results[0][f"out_{i}_dram"] for i in range(len(_OUTS)))
```
